# Optimizing a Trainium2 kernel written in Bass

```python
import math
import jax, jax.numpy as jnp
from jax import lax
import numpy as np

D_MODEL = 1024
BATCH = 1
SEQ = 256
DEPTH = 2
DEC_BATCH = 8
DEC_SEQ = 4
PAST_LEN = 2048
PAGE_SIZE = 128

A_HEADS = 8
A_KV_HEADS = 2
A_GROUP = A_HEADS // A_KV_HEADS
A_HEAD_DIM = 64
A_WIDTH = A_HEADS * A_HEAD_DIM
A_KV_WIDTH = A_KV_HEADS * A_HEAD_DIM
WINDOW = 128
ATT_SCALE = A_HEAD_DIM ** -0.5
N_BUCKETS = 32
MAX_DISTANCE = WINDOW
M_HEADS = 4
M_HEAD_DIM = 128
M_WIDTH = M_HEADS * M_HEAD_DIM
CONV_W = 4
M_CHUNK = 64
MIX_WIDTH = A_WIDTH + M_WIDTH
IN_COLS = A_WIDTH + 2 * A_KV_WIDTH + 4 * M_WIDTH + 2 * M_HEADS
N_KEYS = 128
N_EXPERTS = N_KEYS * N_KEYS
P_HEADS = 8
P_TOPK = 16
P_KEY_DIM = 256
P_HALF = P_KEY_DIM // 2
P_TOKEN_BLOCK = 128
EPS = 1e-6
NEG_INF = -1e30

kernel_name = "hymba_swa_mlstm_peer_adaln_step"

def rmsnorm(x, g):
    x32 = x.astype(jnp.float32)
    y = x32 * lax.rsqrt(jnp.mean(x32 * x32, axis=-1, keepdims=True) + EPS)
    return (y * g.astype(jnp.float32)).astype(x.dtype)

def t5_bucket(dist):
    n = jnp.maximum(dist, 0)
    max_exact = N_BUCKETS // 2
    nf = jnp.maximum(n, 1).astype(jnp.float32)
    large = max_exact + (jnp.log(nf / max_exact) / math.log(MAX_DISTANCE / max_exact)
                         * (N_BUCKETS - max_exact)).astype(jnp.int32)
    return jnp.where(n < max_exact, n, jnp.minimum(large, N_BUCKETS - 1))

def rel_bias_heads(rel_bias, dist):
    b = jnp.take(rel_bias, t5_bucket(dist), axis=0).astype(jnp.float32)
    nq, nk = dist.shape
    return b.reshape(nq, nk, A_KV_HEADS, A_GROUP).transpose(2, 3, 0, 1)

def sink_softmax(s, sinks):
    sk = sinks.astype(jnp.float32).reshape(A_KV_HEADS, A_GROUP, 1, 1)
    mx = jnp.maximum(jnp.max(s, axis=-1, keepdims=True), sk)
    e = jnp.exp(s - mx)
    return e / (jnp.sum(e, axis=-1, keepdims=True) + jnp.exp(sk - mx))

def swa_prompt(q, k, v, sinks, rel_bias):
    B, T = q.shape[:2]
    nb = T // WINDOW
    qb = q.reshape(B, nb, WINDOW, A_KV_HEADS, A_GROUP, A_HEAD_DIM)

    def band(t):
        t = t.reshape(B, nb, WINDOW, A_KV_HEADS, A_HEAD_DIM)
        prev = jnp.concatenate([jnp.zeros_like(t[:, :1]), t[:, :-1]], axis=1)
        return jnp.concatenate([prev, t], axis=2)

    kb, vb = band(k), band(v)
    s = jnp.einsum('bnqhgd,bnkhd->bnhgqk', qb, kb, preferred_element_type=jnp.float32) * ATT_SCALE
    qi = jnp.arange(WINDOW)[:, None]
    kj = jnp.arange(2 * WINDOW)[None, :]
    dist = qi + WINDOW - kj
    valid = (dist >= 0) & (dist < WINDOW)
    mask = valid[None] & ((jnp.arange(nb)[:, None, None] > 0) | (kj >= WINDOW)[None])
    s = s + rel_bias_heads(rel_bias, dist)
    s = jnp.where(mask[None, :, None, None], s, NEG_INF)
    p = sink_softmax(s, sinks)
    o = jnp.einsum('bnhgqk,bnkhd->bnqhgd', p.astype(vb.dtype), vb)
    return o.reshape(B, T, A_WIDTH)

def swa_sample(q, k, v, k_buf, v_buf, sinks, rel_bias):
    B, S = q.shape[:2]
    kk = jnp.concatenate([k_buf.astype(k.dtype), k], axis=1)
    vv = jnp.concatenate([v_buf.astype(v.dtype), v], axis=1)
    qg = q.reshape(B, S, A_KV_HEADS, A_GROUP, A_HEAD_DIM)
    s = jnp.einsum('bqhgd,bkhd->bhgqk', qg, kk, preferred_element_type=jnp.float32) * ATT_SCALE
    dist = jnp.arange(S)[:, None] + WINDOW - jnp.arange(WINDOW + S)[None, :]
    valid = (dist >= 0) & (dist < WINDOW)
    s = s + rel_bias_heads(rel_bias, dist)
    s = jnp.where(valid, s, NEG_INF)
    p = sink_softmax(s, sinks)
    o = jnp.einsum('bhgqk,bkhd->bqhgd', p.astype(vv.dtype), vv)
    return o.reshape(B, S, A_WIDTH), kk[:, -WINDOW:], vv[:, -WINDOW:]

def causal_conv(x, buf, w, b):
    T = x.shape[1]
    xp = jnp.concatenate([buf.astype(x.dtype), x], axis=1)
    y = b + sum(xp[:, i:i + T] * w[i] for i in range(CONV_W))
    return jax.nn.silu(y), xp[:, -(CONV_W - 1):]

def mlstm_chunk(carry, xs):
    C, n, m = carry
    q, k, v, ig, lf = xs
    L = q.shape[1]
    b = jnp.cumsum(lf, axis=1)
    causal = jnp.tril(jnp.ones((L, L), dtype=bool))
    logw = b[:, :, None, :] - b[:, None, :, :] + ig[:, None, :, :]
    logw = jnp.where(causal[None, :, :, None], logw, -jnp.inf)
    inter = b + m[:, None, :]
    m_t = jnp.maximum(inter, jnp.max(logw, axis=2))
    w = jnp.exp(logw - m_t[:, :, None, :])
    a = jnp.exp(inter - m_t)
    qk = jnp.einsum('bthd,bshd->btsh', q, k)
    wqk = w * qk
    num = jnp.einsum('btsh,bshd->bthd', wqk, v) + a[..., None] * jnp.einsum('bhvk,bthk->bthv', C, q)
    den = jnp.sum(wqk, axis=2) + a * jnp.einsum('bhk,bthk->bth', n, q)
    h = num / jnp.maximum(jnp.abs(den), jnp.exp(-m_t))[..., None]
    m_new = m_t[:, -1]
    wl = jnp.exp(b[:, -1:, :] - b + ig - m_new[:, None, :])
    al = jnp.exp(b[:, -1] + m - m_new)
    C_new = al[..., None, None] * C + jnp.einsum('bsh,bshv,bshk->bhvk', wl, v, k)
    n_new = al[..., None] * n + jnp.einsum('bsh,bshk->bhk', wl, k)
    return (C_new, n_new, m_new), h

def mlstm_run(q, k, v, ig, lf, state, chunk):
    B, T = q.shape[:2]
    nc = T // chunk

    def to_chunks(t):
        return t.reshape((B, nc, chunk) + t.shape[2:]).swapaxes(0, 1)

    state, h = lax.scan(mlstm_chunk, state, (to_chunks(q), to_chunks(k), to_chunks(v),
                                             to_chunks(ig), to_chunks(lf)))
    return state, h.swapaxes(0, 1).reshape(B, T, M_HEADS, M_HEAD_DIM)

def peer(h, w_query, sub_keys, u, v):
    B, T, D = h.shape
    xf = h.reshape(-1, D)
    N = xf.shape[0]
    pad = (-N) % P_TOKEN_BLOCK
    xb = jnp.pad(xf, ((0, pad), (0, 0))).reshape(-1, P_TOKEN_BLOCK, D)

    def block(xt):
        q = (xt @ w_query).reshape(P_TOKEN_BLOCK, P_HEADS, 2, P_HALF)
        s = jnp.einsum('thcd,hckd->thck', q, sub_keys, preferred_element_type=jnp.float32)
        s_top, i_top = lax.top_k(s, P_TOPK)
        cand = s_top[:, :, 0, :, None] + s_top[:, :, 1, None, :]
        cand_idx = i_top[:, :, 0, :, None] * N_KEYS + i_top[:, :, 1, None, :]
        best, pos = lax.top_k(cand.reshape(P_TOKEN_BLOCK, P_HEADS, P_TOPK * P_TOPK), P_TOPK)
        idx = jnp.take_along_axis(cand_idx.reshape(P_TOKEN_BLOCK, P_HEADS, P_TOPK * P_TOPK), pos, axis=-1)
        g = jax.nn.softmax(best, axis=-1)
        ue = jnp.take(u, idx, axis=0)
        ve = jnp.take(v, idx, axis=0)
        act = jax.nn.gelu(jnp.einsum('thkd,td->thk', ue, xt, preferred_element_type=jnp.float32))
        return jnp.einsum('thk,thkd->td', (g * act).astype(ve.dtype), ve)

    out = lax.map(block, xb)
    return out.reshape(-1, D)[:N].reshape(B, T, D).astype(h.dtype)

def decoder_layer(x, c, rel_bias, w_ada, b_ada, norm_mix, norm_ffn, w_in, conv_w, conv_b, gate_b,
                  sinks, m_norm, w_out, peer_query, peer_keys, peer_u, peer_v,
                  kv_buf, conv_buf, m_state):
    B, T, _ = x.shape
    mod = jax.nn.silu(c) @ w_ada + b_ada
    sh1, sc1, g1, sh2, sc2, g2 = jnp.split(mod[:, None, :], 6, axis=-1)

    h = rmsnorm(x, norm_mix) * (1 + sc1) + sh1
    proj = h @ w_in
    cuts = np.cumsum([A_WIDTH, A_KV_WIDTH, A_KV_WIDTH, M_WIDTH, M_WIDTH, M_WIDTH, M_WIDTH]).tolist()
    q_a, k_a, v_a, q_m, k_m, v_m, o_m, gates = jnp.split(proj, cuts, axis=-1)

    q_a = q_a.reshape(B, T, A_HEADS, A_HEAD_DIM)
    k_a = k_a.reshape(B, T, A_KV_HEADS, A_HEAD_DIM)
    v_a = v_a.reshape(B, T, A_KV_HEADS, A_HEAD_DIM)
    if kv_buf is None:
        att = swa_prompt(q_a, k_a, v_a, sinks, rel_bias)
        new_k, new_v = k_a[:, -WINDOW:], v_a[:, -WINDOW:]
    else:
        att, new_k, new_v = swa_sample(q_a, k_a, v_a, kv_buf[0], kv_buf[1], sinks, rel_bias)

    if conv_buf is None:
        conv_buf = jnp.zeros((B, CONV_W - 1, 2 * M_WIDTH), x.dtype)
    qk_conv, new_conv = causal_conv(jnp.concatenate([q_m, k_m], axis=-1), conv_buf, conv_w, conv_b)
    q_m, k_m = jnp.split(qk_conv, 2, axis=-1)
    gates = gates.astype(jnp.float32) + gate_b.astype(jnp.float32)
    ig = gates[..., :M_HEADS]
    lf = jax.nn.log_sigmoid(gates[..., M_HEADS:])
    if m_state is None:
        state = (jnp.zeros((B, M_HEADS, M_HEAD_DIM, M_HEAD_DIM), jnp.float32),
                 jnp.zeros((B, M_HEADS, M_HEAD_DIM), jnp.float32),
                 jnp.zeros((B, M_HEADS), jnp.float32))
        chunk = M_CHUNK
    else:
        state = tuple(s.astype(jnp.float32) for s in m_state)
        chunk = T
    qf = q_m.reshape(B, T, M_HEADS, M_HEAD_DIM).astype(jnp.float32)
    kf = k_m.reshape(B, T, M_HEADS, M_HEAD_DIM).astype(jnp.float32) * (M_HEAD_DIM ** -0.5)
    vf = v_m.reshape(B, T, M_HEADS, M_HEAD_DIM).astype(jnp.float32)
    (C_new, n_new, m_new), hm = mlstm_run(qf, kf, vf, ig, lf, state, chunk)
    hm = hm * lax.rsqrt(jnp.mean(hm * hm, axis=-1, keepdims=True) + EPS)
    hm = hm * m_norm.astype(jnp.float32).reshape(M_HEADS, M_HEAD_DIM)
    m_out = (jax.nn.sigmoid(o_m.astype(jnp.float32)) * hm.reshape(B, T, M_WIDTH)).astype(x.dtype)

    mix = jnp.concatenate([att, m_out], axis=-1) @ w_out
    x = x + g1 * mix

    h2 = rmsnorm(x, norm_ffn) * (1 + sc2) + sh2
    x = x + g2 * peer(h2, peer_query, peer_keys, peer_u, peer_v)
    return x, new_k, new_v, new_conv, C_new, n_new, m_new

def setup_inputs(seed: int = 0) -> dict:
    key = jax.random.key(seed)
    ks = jax.random.split(key, 32)
    D = D_MODEL

    def nrm(k, shape, s):
        return jax.random.normal(k, shape, jnp.float32) * s

    gate_b = jnp.concatenate([nrm(ks[20], (DEPTH, M_HEADS), 0.1),
                              3.0 + nrm(ks[21], (DEPTH, M_HEADS), 0.5)], axis=-1)
    return {
        "x_prompt": nrm(ks[0], (BATCH, SEQ, D), 1.0),
        "x_sample": nrm(ks[1], (DEC_BATCH, DEC_SEQ, D), 1.0),
        "c_prompt": nrm(ks[2], (BATCH, D), 1.0),
        "c_sample": nrm(ks[3], (DEC_BATCH, D), 1.0),
        "cache_k": nrm(ks[4], (DEPTH, DEC_BATCH, WINDOW, A_KV_HEADS, A_HEAD_DIM), 1.0),
        "cache_v": nrm(ks[5], (DEPTH, DEC_BATCH, WINDOW, A_KV_HEADS, A_HEAD_DIM), 1.0),
        "state_conv": nrm(ks[6], (DEPTH, DEC_BATCH, CONV_W - 1, 2 * M_WIDTH), 1.0),
        "state_C": nrm(ks[7], (DEPTH, DEC_BATCH, M_HEADS, M_HEAD_DIM, M_HEAD_DIM), 0.05),
        "state_n": nrm(ks[8], (DEPTH, DEC_BATCH, M_HEADS, M_HEAD_DIM), 0.5),
        "state_m": nrm(ks[9], (DEPTH, DEC_BATCH, M_HEADS), 0.5),
        "rel_bias": nrm(ks[10], (N_BUCKETS, A_HEADS), 0.5),
        "w_ada": nrm(ks[11], (DEPTH, D, 6 * D), 0.5 * D ** -0.5),
        "b_ada": nrm(ks[12], (DEPTH, 6 * D), 0.1),
        "norm_mix": 1.0 + nrm(ks[13], (DEPTH, D), 0.05),
        "norm_ffn": 1.0 + nrm(ks[14], (DEPTH, D), 0.05),
        "w_in": nrm(ks[15], (DEPTH, D, IN_COLS), D ** -0.5),
        "conv_w": nrm(ks[16], (DEPTH, CONV_W, 2 * M_WIDTH), CONV_W ** -0.5),
        "conv_b": nrm(ks[17], (DEPTH, 2 * M_WIDTH), 0.05),
        "gate_b": gate_b,
        "attn_sinks": nrm(ks[18], (DEPTH, A_HEADS), 1.0),
        "m_norm": 1.0 + nrm(ks[19], (DEPTH, M_WIDTH), 0.05),
        "w_out": nrm(ks[22], (DEPTH, MIX_WIDTH, D), MIX_WIDTH ** -0.5),
        "peer_query": nrm(ks[23], (DEPTH, D, P_HEADS * P_KEY_DIM), D ** -0.5),
        "peer_keys": nrm(ks[24], (DEPTH, P_HEADS, 2, N_KEYS, P_HALF), P_HALF ** -0.5),
        "peer_u": nrm(ks[25], (DEPTH, N_EXPERTS, D), D ** -0.5),
        "peer_v": nrm(ks[26], (DEPTH, N_EXPERTS, D), P_HEADS ** -0.5),
        "norm_final": 1.0 + nrm(ks[27], (D,), 0.05),
    }

def reference(x_prompt, x_sample, c_prompt, c_sample, cache_k, cache_v, state_conv, state_C, state_n,
              state_m, rel_bias, w_ada, b_ada, norm_mix, norm_ffn, w_in, conv_w, conv_b, gate_b,
              attn_sinks, m_norm, w_out, peer_query, peer_keys, peer_u, peer_v, norm_final):
    xp, xs = x_prompt, x_sample
    st_p, st_s = [], []
    for l in range(DEPTH):
        lw = (w_ada[l], b_ada[l], norm_mix[l], norm_ffn[l], w_in[l], conv_w[l], conv_b[l], gate_b[l],
              attn_sinks[l], m_norm[l], w_out[l], peer_query[l], peer_keys[l], peer_u[l], peer_v[l])
        xp, *sp = decoder_layer(xp, c_prompt, rel_bias, *lw, None, None, None)
        xs, *ss = decoder_layer(xs, c_sample, rel_bias, *lw, (cache_k[l], cache_v[l]), state_conv[l],
                                (state_C[l], state_n[l], state_m[l]))
        st_p.append(sp)
        st_s.append(ss)
    y_prompt = rmsnorm(xp, norm_final)
    y_sample = rmsnorm(xs, norm_final)
    k_p, v_p, conv_p, C_p, n_p, m_p = [jnp.stack([s[i] for s in st_p]) for i in range(6)]
    k_s, v_s, conv_s, C_s, n_s, m_s = [jnp.stack([s[i] for s in st_s]) for i in range(6)]
    return (y_prompt, y_sample, k_p, v_p, conv_p, C_p, n_p, m_p, k_s, v_s, conv_s, C_s, n_s, m_s)


_drawn_inputs = setup_inputs


def setup_inputs(seed=0):
    import zlib

    import numpy as np

    out = dict(_drawn_inputs(seed))
    spreads = {}
    factors = {'attn_sinks': 6.511, 'm_norm': 4.74}
    for name, (base, spread) in spreads.items():
        noise = np.random.default_rng([zlib.crc32(name.encode()), seed]).standard_normal(out[name].shape)
        drawn = base * np.exp(spread * noise) if base else spread * noise
        out[name] = __import__('jax').numpy.asarray(drawn.astype(out[name].dtype))
    for name, factor in factors.items():
        out[name] = (out[name] * factor).astype(out[name].dtype)
    return out
```

```python
from contextlib import ExitStack

import numpy as np

import concourse.bass as bass
from concourse import mybir

F32 = mybir.dt.float32
I32 = mybir.dt.int32
U32 = mybir.dt.uint32
ALU = mybir.AluOpType
ACT = mybir.ActivationFunctionType
AX = mybir.AxisListType.X

P = 128
DEPTH, D, SEQ, DEC_B, DEC_S = 2, 1024, 256, 8, 4
KD = D // P
NS = DEC_B * DEC_S
TOK = SEQ + NS
NC = 1 + DEC_B
A_HEADS, A_KV, DH, WINDOW = 8, 2, 64, 128
GROUP = A_HEADS // A_KV
MH, MD = 4, 128
CONV_W = 4
EPS = 1e-6
BIG = 1e30
N_KEYS, P_HEADS, TOPK = 128, 8, 16
N_EXPERTS = N_KEYS * N_KEYS
IN_COLS = 2824
GATE_COL = IN_COLS - 2 * MH
QA, KA, VA, VM, OM = 0, 4, 5, 6, 10
SKEW = 384
K = 16
RU, RV = 4, 8
DIAGS = 4
BANKS = 6
WSLOTS = 2
R_NMIX, R_NFFN, R_BADA, R_CONVW, R_CONVB, R_MNORM, R_NFIN, R_ROWS = 0, 8, 16, 64, 96, 104, 108, 116
C_ID, C_ONE, C_CAUSAL, C_CAUSALS, C_BLOCK, C_BLOCKADD, C_SUM, C_IOTA, C_COLS = 0, 128, 256, 384, 416, 424, 456, 488, 504
TILES = ["S", "T0", "T1"]
UNITS = {"S": 2, "T0": 8, "T1": 8}
COL = {"T0": 0, "T1": 128, "S": 256}
TI = {"T0": 0, "T1": 1, "S": 2}


def constants():
    c = np.zeros((P, C_COLS), np.float32)
    p = np.arange(P)
    c[:, C_ID:C_ID + P] = np.eye(P)
    c[:, C_ONE:C_ONE + P] = 1.0
    c[:, C_CAUSAL:C_CAUSAL + P] = np.where(p[:, None] > p[None, :], BIG, 0)
    s, t = np.arange(NS)[:, None], np.arange(NS)[None, :]
    c[:NS, C_CAUSALS:C_CAUSALS + NS] = np.where((s // DEC_S == t // DEC_S) & (s <= t), 0, BIG)
    c[:NS, C_BLOCK:C_BLOCK + DEC_B] = s // DEC_S == np.arange(DEC_B)[None, :]
    c[:, C_BLOCKADD:C_BLOCKADD + NS] = np.where((p[:, None] % NS) // DEC_S == t // DEC_S, 0, -BIG)
    c[:, C_SUM:C_SUM + NS] = p[:, None] % NS == t
    c[:, C_IOTA:C_IOTA + TOPK] = np.arange(TOPK)
    hot = np.zeros((33, SKEW), np.float32)
    for x in range(SKEW):
        n = 255 - x
        if 0 <= n < WINDOW:
            large = 16 + int(np.log(max(n, 1) / 16) / np.log(WINDOW / 16) * 16) if n >= 16 else n
            hot[min(large, 31), x] = 1
        else:
            hot[32, x] = 1
    return c, hot


def plan():
    out = []

    def add(eng, *key):
        out.append((key, eng))

    def ada(l, i):
        add("A", "ada", l, 2 * i)
        add("A", "ada", l, 2 * i + 1)
        add("V", "adaT", l, i)

    for l in range(DEPTH):
        add("V", "params", l)
    for k in range(KD):
        add("A", "x", k)
    add("V", "c")
    for h in range(A_HEADS):
        add("A", "rel", h)
    for l in range(DEPTH):
        if l == 0:
            for i in range(6):
                ada(0, i)
        add("V", "cvs", l)
        add("A", "ss1", l)
        for m in PROJ_ORDER[:-4]:
            add("V" if m in ("ig", "fg") else "A", "proj", l, m)
        for t in range(3):
            add("A", "kvtok", l, t)
        for j in range(2):
            add("A", "kct", l, j)
        for t in range(2):
            for j in range(4):
                add("V", "sc", l, t, j)
        for n in range(2):
            add("A", "ssT", l, n)
        for n in range(2):
            add("V", "ss", l, n)
        for m in PROJ_ORDER[-4:]:
            add("A", "proj", l, m)
        for t in range(3):
            add("A", "ktok", l, t)
        for t in range(3):
            add("A", "vtok", l, t)
        add("V", "cols", l)
        add("V", "nT", l)
        add("V", "bA", l)
        for h in range(MH):
            add("A", "bM", l, h)
            add("A", "bE", l, h)
            add("V", "qk", l, h)
        for t in range(2):
            for j in range(2 * (t + 1)):
                add("A", "pT", l, t, j)
            add("A", "o", l, t)
        for n in range(2):
            add("A", "spT", l, n)
        add("A", "o", l, 2)
        for h in range(MH):
            for j in range(2):
                add("A", "CT", l, h, j)
            add("V", "den", l, h)
            add("V", "num", l, h)
            for j in range(2):
                add("V", "Cs", l, h, j)
        for h in range(MH):
            add("A", "hss", l, h)
        add("A", "Cp", l)
        add("A", "np", l)
        add("V", "nn", l)
        add("A", "nnr", l)
        for j in range(2):
            add("A", "cvr", l, j)
        for j in range(4):
            add("A", "ky", l, j)
        for m in range(KD):
            add("V", "out", l, m)
        add("A", "ss2", l)
        for m in range(16):
            add("A", "qp", l, m)
        add("V", "rs", l, "S", 0)
        for t in (2, 0, 1):
            for j in range(2):
                add("A", "h2", l, t, j)
        for j in range(4):
            add("V", "rs", l, "T0", j)
        for g in TILES:
            if g == "T0":
                add("V", "rs", l, "T1", 0)
                for n in range(8):
                    if n < 3:
                        add("V", "rs", l, "T1", n + 1)
                    if n < 6 and l + 1 < DEPTH:
                        ada(l + 1, n)
            for j in range(2):
                add("V", "pt", l, g, j)
    add("A", "ssf")
    for t in range(3):
        for j in range(2):
            add("A", "y", t, j)
    return out


PROJ_TILES = [5, 1, 2, 3, 0, 4]
PROJ_ORDER = [20, 21, "ig", "fg"] + [4 * t + j for t in PROJ_TILES[1:] for j in range(4)]


def hybrid_trunk(nc, x_prompt, x_sample, c_prompt, c_sample, cache_k, cache_v, state_conv, state_C, state_n, state_m,
                 rel_bias, w_ada, b_ada, norm_mix, norm_ffn, w_in, conv_w, conv_b, gate_b, attn_sinks, m_norm, w_out,
                 peer_query, peer_keys, peer_u, peer_v, norm_final, consts, buckets,
                 y_p, y_s, k_p, v_p, conv_p, C_p, n_p, m_p, k_s, v_s, conv_s, C_s, n_s, m_s):
    PLAN = plan()
    nth = {key: n for n, (key, _) in enumerate(PLAN)}
    drains = {key: sum(e == eng for _, e in PLAN[:n + 1]) for n, (key, eng) in enumerate(PLAN)}

    ctx = ExitStack()
    with ctx:
        ctx.enter_context(nc.allow_non_contiguous_dma(reason="a few rows of gates, biases and running maxima"))

        def sb(name, shape, dt=F32):
            return ctx.enter_context(nc.sbuf_tensor(name, shape, dt))

        sems = {}

        def sem(name):
            if name not in sems:
                sems[name] = ctx.enter_context(nc.semaphore(name))
            return sems[name]

        rel_dram = nc.dram_tensor("rel_skewed", (A_HEADS, P, SKEW), F32, kind="Internal").ap()

        cst = sb("cst", [P, C_COLS])
        ident, ones = cst[:, C_ID:C_ID + P], cst[:, C_ONE:C_ONE + P]
        wring = sb("wring", [P, WSLOTS, KD, 512])
        xT = sb("xT", [P, KD, TOK])
        hT = sb("hT", [P, KD, TOK])
        region1 = sb("region1", [P, 16, TOK])
        cin = sb("cin", [P, KD * (SEQ + 3) + KD * DEC_B * (DEC_S + 3)])
        cin_p = cin[:, 0:KD * (SEQ + 3)].rearrange("p (k t) -> p k t", k=KD)
        cin_s = cin[:, KD * (SEQ + 3):].rearrange("p (k b t) -> p k b t", k=KD, b=DEC_B)
        keyT = cin[:, 0:16 * P].rearrange("p (m k) -> p m k", m=16)
        qks = sb("qks", [P, KD, TOK])
        qks_flat = qks[:, :, :].rearrange("p k t -> p (k t)")
        mixT = sb("mixT", [P, KD, TOK])
        ada_rows = mixT[:, :, :].rearrange("p k t -> p (k t)")[0:NC, 0:1024].rearrange("p (r c) -> p r c", r=2)
        bias = sb("bias", [P, A_HEADS, 2 * WINDOW])
        bias_s = sb("bias_s", [P, A_KV, WINDOW + NS])
        prm = sb("prm", [P, DEPTH, R_ROWS])
        gate_bias = sb("gate_bias", [MH, DEPTH, 2])
        sink_p = sb("sink_p", [P, DEPTH, A_HEADS])
        sink_s = sb("sink_s", [P, DEPTH, A_KV])
        eps_t = sb("eps_t", [P, 1])
        cT = sb("cT", [P, KD, NC])
        modT_all = sb("modT", [P, 2, 48, NC])
        modA = sb("modA", [P, 2, KD, NC])
        rstd = sb("rstd", [P, TOK])
        diag = sb("diag", [P, DIAGS, P])
        dots = sb("dots", [P, 2, K])
        gelus = sb("gelus", [P, 2, K])
        wts = sb("wts", [P, 2, K])
        idx_staged = sb("idx_staged", [P, 2, K], I32)
        idx_all = sb("idx_all", [P, 3, P_HEADS * TOPK], I32)
        g_all = sb("g_all", [P, 3, P_HEADS * TOPK])

        rings = sb("rings", [P, (RU + RV) * D])
        u_ring = rings[:, 0:RU * D].rearrange("p (r d) -> p r d", r=RU)
        v_ring = rings[:, RU * D:].rearrange("p (r d) -> p r d", r=RV)

        class Cut:
            def __init__(self, region, size):
                self.region, self.size, self.at = region, size, 0

            def __call__(self, n, parts=P):
                self.at += n
                assert self.at <= self.size, self.at
                return self.region[0:parts, self.at - n:self.at]

        cut = Cut(rings, (RU + RV) * D)
        C_flat = cut(2048)
        keys_raw = C_flat.rearrange("p (m k) -> p m k", m=16)
        C_sb = C_flat.rearrange("p (r b k) -> p r b k", r=2, b=DEC_B)
        CT_flat = cut(2048)
        CT = CT_flat.rearrange("p (r b k) -> p r b k", r=2, b=DEC_B)
        kc = cut(1024).rearrange("p (b c) -> p b c", b=DEC_B)
        vc = cut(1024).rearrange("p (b c) -> p b c", b=DEC_B)
        kcT_flat = cut(1024)
        kcT = kcT_flat.rearrange("p (b c) -> p b c", b=DEC_B)
        PT = cut(2048).rearrange("p (h b q) -> p h b q", h=A_HEADS, b=2)
        sT = cut(256).rearrange("p (n r) -> p n r", n=2)
        SS = cut(2 * 160).rearrange("p (n r) -> p n r", n=2)
        PTs_flat = cut(512)
        PTs = PTs_flat.rearrange("p (n j r) -> p n j r", n=2, j=2)
        row = {n: cut(TOK, MH) for n in ("ig", "b", "a", "M", "e", "wl")}
        row["aw"] = cut(NS, MH)
        x_tok = rings[:, 0:3 * D].rearrange("p (t d) -> p t d", t=3)
        c_tok = rings[0:NC, 3 * D:4 * D]
        prm_rows = rings[0:R_ROWS, 4 * D:4 * D + 2 * P].rearrange("p (l c) -> p l c", l=2)
        hot = rings[0:33, 5 * D:5 * D + SKEW]
        relb = rings[0:33, 6 * D:7 * D].rearrange("p (h c) -> p h c", h=A_HEADS)
        relraw = rings[0:33, 7 * D:7 * D + 8]
        rel_rows = rings[:, 8 * D:8 * D + 8 * SKEW].rearrange("p (h c) -> p h c", h=A_HEADS)
        hT_flat = hT[:, :, :].rearrange("p k t -> p (k t)")
        S1 = CT_flat.rearrange("p (h k) -> p h k", h=A_HEADS)
        S0 = mixT[:, 4:8, :].rearrange("p k t -> p (k t)")[:, 0:A_HEADS * P].rearrange("p (h k) -> p h k", h=A_HEADS)
        wv = hT_flat[:, 0:1024].rearrange("p (t h c) -> p t h c", t=2, h=MH)

        MSIZE = 6912
        mreg = sb("mreg", [P, MSIZE])
        cut = Cut(mreg, MSIZE)
        vt = cut(3 * 512).rearrange("p (t c) -> p t c", t=3)
        kt = cut(3 * 512).rearrange("p (t c) -> p t c", t=3)
        WT = cut(4 * 416).rearrange("p (h c) -> p h c", h=MH)
        eh_flat = cut(MH * TOK)
        eh = eh_flat.rearrange("p (h c) -> p h c", h=MH)
        kdup = eh_flat[:, 0:A_KV * TOK].rearrange("p (n t) -> p n t", n=A_KV)
        qd = eh_flat[:, A_KV * TOK:A_KV * TOK + GROUP * NS].rearrange("p (g t) -> p g t", g=GROUP)
        wk = cut(1024, NS).rearrange("p (b k) -> p b k", b=DEC_B)
        cut = Cut(mreg, MSIZE)
        h2tok = cut(3 * D).rearrange("p (t d) -> p t d", t=3)
        cand_flat = cut(2048)
        cand = cand_flat.rearrange("p (h c) -> p h c", h=P_HEADS)
        onehot = cand_flat.rearrange("p (h i j) -> p h i j", h=P_HEADS, i=TOPK)
        hS4 = cand_flat[:, 0:1024].rearrange("p (k q t) -> p k q t", k=KD, q=4)
        rep = cut(256)
        s_top = cut(256).rearrange("p (h c k) -> p h c k", h=P_HEADS, c=2)
        i_top = cut(256).bitcast(U32).rearrange("p (h c k) -> p h c k", h=P_HEADS, c=2)
        i_topf = cut(256).rearrange("p (h c k) -> p h c k", h=P_HEADS, c=2)
        best = cut(128).rearrange("p (h k) -> p h k", h=P_HEADS)
        pos = cut(128).bitcast(U32).rearrange("p (h k) -> p h k", h=P_HEADS)
        pij_flat = cut(256)
        pij = pij_flat.rearrange("p (c h k) -> p c h k", c=2, h=P_HEADS)
        small = sb("small", [P, 1000])
        cut = Cut(small, 1000)
        stat = [cut(40).rearrange("p (w h) -> p w h", w=5) for _ in range(3)]
        cols = cut(24).rearrange("p (t c) -> p t c", t=3)
        WB = cut(32, NS).rearrange("p (h b) -> p h b", h=MH)
        nrow = cut(P, NS)
        nT = cut(32)
        nnT = cut(32)
        abc = cut(P).rearrange("p (h t) -> p h t", h=MH)
        qa = cut(P).rearrange("p (h t) -> p h t", h=MH)
        nqa = cut(P).rearrange("p (h t) -> p h t", h=MH)
        m_in = cut(DEC_B, MH)
        m_out = cut(NC, MH)
        tmp = cut(P)
        zeros = sb("zeros", [P, 512])
        pe_tok = sb("pe_tok", [P, D])
        cvo = sb("cvo", [P, KD, 27])
        kvt = sb("kvt", [P, 3, 2 * P])

        banks = ctx.enter_context(nc.psum_tensor("banks", [P, BANKS, 512], F32))
        acc = ctx.enter_context(nc.psum_tensor("acc", [P, 2, 512], F32))

        product_ready = sem("product_ready")
        drained = {"A": sem("drained_by_act"), "V": sem("drained_by_dve")}

        def bank(key):
            return banks[:, nth[key] % BANKS, :]

        def drain_of(key):
            return drained[PLAN[nth[key]][1]], drains[key]

        def claim(pe, key):
            if nth[key] >= BANKS:
                pe.wait_ge(*drain_of(PLAN[nth[key] - BANKS][0]))
            return bank(key)

        class Steps:
            def __init__(self, eng, own):
                self.eng, self.own, self.count = eng, own, {}

            def __call__(self, ins, signal=None):
                s = signal or self.own
                ins.then_inc(sem(s) if isinstance(s, str) else s, 1)
                n = self.count[str(s)] = self.count.get(str(s), 0) + 1
                self.eng.wait_ge(sem(s) if isinstance(s, str) else s, n)

        def product(eng, key):
            eng.wait_ge(product_ready, nth[key] + 1)
            return bank(key)

        def bc(ap, axis, shape):
            return ap.unsqueeze(axis).broadcast_to(shape)

        def by_sample(ap):
            return ap.rearrange("p (b s) -> p b s", b=DEC_B) if len(ap.shape) == 2 else \
                ap.rearrange("p k (b s) -> p k b s", b=DEC_B)

        SB, ST = slice(SEQ, TOK), slice(0, SEQ)
        setup_loads = 7 + DEPTH * (9 + A_HEADS)
        first_slot, slots = {}, 0
        for l in range(DEPTH):
            for g in TILES:
                first_slot[l, g] = slots
                slots += UNITS[g] * K
        u_loaded = [sem(f"u_row_loaded_{r}") for r in range(RU)]
        v_loaded = [sem(f"v_row_loaded_{r}") for r in range(RV)]

        block = ctx.enter_context(nc.Block())

        @block.sync
        def _(sp):
            load = lambda dst, src: sp.dma_start(dst, src).then_inc(sem("setup_loaded"), 16)
            load(cst[:, :], consts)
            load(hot, buckets)
            load(relraw[0:32, :], rel_bias)
            load(x_tok[:, 0:2, :], x_prompt[0].rearrange("(t p) d -> p t d", p=P))
            load(x_tok[0:NS, 2, :], x_sample.rearrange("b s d -> (b s) d"))
            load(c_tok[0:1, :], c_prompt)
            load(c_tok[1:NC, :], c_sample)
            for l in range(DEPTH):
                for r, src, n in ((R_NMIX, norm_mix[l], 8), (R_NFFN, norm_ffn[l], 8), (R_BADA, b_ada[l], 48),
                                  (R_CONVB, conv_b[l], 8), (R_MNORM, m_norm[l], 4), (R_NFIN, norm_final, 8)):
                    load(prm_rows[r:r + n, l, :], src.rearrange("(k c) -> k c", c=P))
                load(prm_rows[R_CONVW:R_CONVW + 32, l, :], conv_w[l].rearrange("i (k c) -> (i k) c", c=P))
                load(gate_bias[:, l, :], gate_b[l].rearrange("(g h) -> h g", g=2))
                load(sink_p[:, l, :], attn_sinks[l:l + 1, :].broadcast_to([P, A_HEADS]))
                for h in range(A_HEADS):
                    n, g = h // GROUP, h % GROUP
                    load(sink_s[g * NS:(g + 1) * NS, l, n:n + 1],
                         attn_sinks[l:l + 1, h:h + 1].broadcast_to([NS, 1]))
            tile = 0
            for l in range(DEPTH):
                def weights(src, c0, n, layer=l):
                    nonlocal tile
                    if tile >= WSLOTS:
                        sp.wait_ge(sem("weights_used"), tile - WSLOTS + 1)
                    sp.dma_start(wring[:, tile % WSLOTS, :, 0:n],
                                 src[layer, :, c0:c0 + n].rearrange("(k p) n -> p k n", p=P))\
                        .then_inc(sem(f"weights_loaded_{tile % WSLOTS}"), 16)
                    tile += 1

                if l == 0:
                    for m in range(12):
                        weights(w_ada, 512 * m, 512)
                for m in PROJ_TILES:
                    weights(w_in, 512 * m, min(512, IN_COLS - 512 * m))
                    if m == 5:
                        if l:
                            sp.wait_ge(*drain_of(("pt", l - 1, TILES[-1], 1)))
                        else:
                            sp.wait_ge(sem("rel_stored"), 16)
                        sp.dma_start(kc, cache_k[l].rearrange("b w h d -> w b (h d)")).then_inc(sem("kc_loaded"), 16)
                        sp.dma_start(vc, cache_v[l].rearrange("b w h d -> w b (h d)")).then_inc(sem("vc_loaded"), 16)
                for m in range(2):
                    weights(w_out, 512 * m, 512)
                for m in range(4):
                    weights(peer_query, 512 * m, 512)
                if l + 1 < DEPTH:
                    for m in range(12):
                        weights(w_ada, 512 * m, 512, l + 1)
            sp.wait_ge(*drain_of(("y", 2, 1)))
            sp.dma_start(y_p[0].rearrange("(t p) d -> p t d", p=P), x_tok[:, 0:2, :]).then_inc(sem("y_stored"), 16)
            sp.dma_start(y_s.rearrange("b s d -> (b s) d"), x_tok[0:NS, 2, :]).then_inc(sem("y_stored"), 16)
            sp.wait_ge(sem("y_stored"), 32)

        @block.gpsimd
        def _(pool):
            u_rows = peer_u.rearrange("l e d -> (l e) d")
            v_rows = peer_v.rearrange("l e d -> (l e) d")
            u_free = pool.alloc_register("u_free")
            v_free = pool.alloc_register("v_free")
            stage_free = pool.alloc_register("stage_free")
            pool.reg_mov(u_free, 1)
            pool.reg_mov(v_free, 1)
            pool.reg_mov(stage_free, K)
            stored = 0

            def store(dst, src):
                nonlocal stored
                pool.dma_start(dst, src).then_inc(sem("outputs_stored"), 16)
                stored += 16

            def unit(g, i, half, n, first):
                if not first:
                    pool.wait_ge(sem("v_row_used"), stage_free)
                    pool.reg_add(stage_free, stage_free, K)
                pool.tensor_copy(idx_staged[:, half, :], idx_all[:, TI[g], bass.ds(i * 2 * K + half * K, K)])\
                    .then_inc(sem("idx_staged"), 1)
                pool.wait_ge(sem("idx_staged"), n + 1)
                for k in range(K):
                    if not (first and half == 0 and k < RU):
                        pool.wait_ge(sem("u_row_used"), u_free)
                        pool.reg_add(u_free, u_free, 1)
                    pool.indirect_dma_start(
                        out=u_ring[:, k % RU, :], out_offset=None, in_=u_rows,
                        in_offset=bass.IndirectOffsetOnAxis(ap=idx_staged[:, half, k:k + 1], axis=0))\
                        .then_inc(u_loaded[k % RU], 16)
                for k in range(K):
                    if not (first and half == 0 and k < RV):
                        pool.wait_ge(sem("v_row_used"), v_free)
                        pool.reg_add(v_free, v_free, 1)
                    pool.indirect_dma_start(
                        out=v_ring[:, k % RV, :], out_offset=None, in_=v_rows,
                        in_offset=bass.IndirectOffsetOnAxis(ap=idx_staged[:, half, k:k + 1], axis=0))\
                        .then_inc(v_loaded[k % RV], 16)

            for l in range(DEPTH):
                if l:
                    pool.wait_ge(*drain_of(("pt", l - 1, TILES[-1], 1)))
                else:
                    pool.wait_ge(sem("setup_loaded"), 16 * setup_loads)
                    pool.wait_ge(*drain_of(("x", KD - 1)))
                pool.dma_start(pe_tok[0:24, :], state_conv[l].rearrange("b r c -> (b r) c")).then_inc(sem("conv_state_loaded"), 16)
                pool.dma_start(nrow, state_n[l].rearrange("b h k -> (b h) k")).then_inc(sem("n_loaded"), 16)
                pool.dma_start(m_in, state_m[l].rearrange("b h -> h b")).then_inc(sem("m_loaded"), 16)
                if l == 0:
                    pool.wait_ge(*drain_of(("rel", A_HEADS - 1)))
                    pool.dma_start(rel_dram.rearrange("h p c -> p h c"), rel_rows).then_inc(sem("rel_stored"), 16)
                    pool.wait_ge(sem("rel_stored"), 16)
                    skew = lambda off, ap: bass.AP(rel_dram.tensor, off, ap)
                    pool.dma_start(bias[:, :, :], skew(127, [[SKEW - 1, P], [P * SKEW, A_HEADS], [1, 2 * WINDOW]]))\
                        .then_inc(sem("bias_loaded"), 16)
                    for h in range(A_HEADS):
                        n, g = h // GROUP, h % GROUP
                        src = slice(g * NS, (g + 1) * NS)
                        pool.dma_start(bias_s[src, n, 0:WINDOW], skew(h * P * SKEW + 127, [[0, DEC_B], [SKEW - 1, DEC_S], [1, WINDOW]]))\
                            .then_inc(sem("bias_loaded"), 16)
                        for b in range(DEC_B):
                            pool.dma_start(bias_s[src, n, WINDOW + b * DEC_S:WINDOW + (b + 1) * DEC_S],
                                           skew(h * P * SKEW + 127 + WINDOW, [[0, DEC_B], [SKEW - 1, DEC_S], [1, DEC_S]]))\
                                .then_inc(sem("bias_loaded"), 16)
                def load_C(h):
                    pool.dma_start(C_sb[:, h % 2, :, :], state_C[l, :, h].rearrange("b v k -> v b k"))\
                        .then_inc(sem(f"C_loaded_{h % 2}"), 16)
                load_C(0)
                load_C(1)
                pool.wait_ge(*drain_of(("proj", l, KA)))
                for n in range(A_KV):
                    for half in range(2):
                        pool.dma_start(kdup[half * DH:(half + 1) * DH, n, :], region1[n * DH:(n + 1) * DH, KA, :])\
                            .then_inc(sem("k_doubled"), 16)
                pool.wait_ge(*drain_of(("proj", l, QA + 3)))
                for n in range(A_KV):
                    for g in range(GROUP):
                        h = n * GROUP + g
                        pool.dma_start(qd[n * DH:(n + 1) * DH, g, :], region1[h % 2 * DH:(h % 2 + 1) * DH, h // 2, SB])\
                            .then_inc(sem("q_moved"), 16)
                pool.wait_ge(*drain_of(("kvtok", l, 2)))
                for dst_p, dst_s, cache, c0, loaded in ((k_p, k_s, kc, 0, "kc_loaded"), (v_p, v_s, vc, P, "vc_loaded")):
                    store(dst_p[l, 0].rearrange("w h d -> w (h d)"), kvt[:, 1, c0:c0 + P])
                    pool.wait_ge(sem(loaded), 16 * (l + 1))
                    store(dst_s[l, :, 0:WINDOW - DEC_S].rearrange("b w h d -> w b (h d)"), cache[DEC_S:WINDOW, :, :])
                    for b in range(DEC_B):
                        store(dst_s[l, b, WINDOW - DEC_S:].rearrange("w h d -> w (h d)"), kvt[b * DEC_S:(b + 1) * DEC_S, 2, c0:c0 + P])
                pool.wait_ge(sem("m_out_ready"), l + 1)
                store(m_p[l, 0].unsqueeze(1), m_out[:, 0:1])
                store(m_s[l].rearrange("b h -> h b"), m_out[:, 1:NC])
                for h in range(MH):
                    pool.wait_ge(*drain_of(("Cs", l, h, 1)))
                    store(C_s[l, :, h].rearrange("b v k -> v b k"), C_sb[:, h % 2, :, :])
                    if h + 2 < MH:
                        pool.wait_ge(sem("outputs_stored"), stored)
                        load_C(h + 2)
                pool.wait_ge(sem("outputs_stored"), stored)
                pool.dma_start(keys_raw, peer_keys[l].rearrange("h c k d -> k (h c) d")).then_inc(sem("keys_loaded"), 16)
                pool.wait_ge(*drain_of(("np", l)))
                store(C_p[l, 0].rearrange("h v k -> v h k"), PTs_flat.rearrange("p (h k) -> p h k", h=MH))
                store(n_p[l, 0].rearrange("h k -> (h k)").unsqueeze(0), kcT_flat[0:1, 0:512])
                pool.wait_ge(*drain_of(("nnr", l)))
                store(n_s[l].rearrange("b h k -> (b h) k"), nrow)
                pool.wait_ge(*drain_of(("cvr", l, 1)))
                store(conv_p[l, 0], pe_tok[0:3, :])
                store(conv_s[l].rearrange("b r c -> (b r) c"), pe_tok[3:27, :])
                pool.wait_ge(sem("outputs_stored"), stored)
                for g in TILES:
                    base = first_slot[l, g] // K
                    pool.wait_ge(sem("idx_ready"), l * 3 + TILES.index(g) + 1)
                    if UNITS[g] == 2:
                        for half in range(2):
                            unit(g, 0, half, base + half, l == 0)
                    else:
                        with pool.Fori(0, UNITS[g] // 2) as i:
                            for half in range(2):
                                unit(g, i, half, base + 2 * i + half, False)

        @block.scalar
        def _(act):
            step = Steps(act, "act_step")
            A = drained["A"]

            def evacuate(key, dst, cols=None, parts=None, src=None):
                b = product(act, key)
                src = b[:, 0:cols] if src is None else src
                if parts is not None:
                    src = src[0:parts]
                step(nc.scalar.activation(dst, src, ACT.Copy), A)

            def root(key, dst, n):
                b = product(act, key)
                step(nc.scalar.activation(dst, b[:, 0:TOK], ACT.Sqrt, bias=eps_t[:, 0:1], scale=1.0 / n), A)

            def squares():
                step(nc.scalar.activation(hT[:, :, :], xT[:, :, :], ACT.Square), "squares_ready")

            def modulate(l, w):
                modT = modT_all[:, l % 2]
                act.wait_ge(sem("xn_ready"), 2 * l + w + 1)
                shift = 24 * w
                for k in range(KD):
                    step(nc.scalar.activation(hT[:, k, ST], qks[:, k, ST], ACT.Identity,
                                              bias=modT[:, shift + k, 0:1], scale=modA[:, w, k, 0:1]), "h_ready")

            def softmax_exp(l, i, S, sink, width):
                act.wait_ge(sem("exp_wanted"), 3 * l + i + 1)
                nh = S.shape[1]
                for h in range(nh):
                    step(nc.scalar.activation(S[:, h, :], S[:, h, :], ACT.Exp, bias=stat[i][:, 1, h:h + 1],
                                              accum_out=stat[i][:, 3, h:h + 1]))
                step(nc.scalar.activation(stat[i][:, 2, 0:nh], stat[i][:, 2, 0:nh], ACT.Exp), "exp_done")

            def gate_exp(l, i, nh):
                act.wait_ge(sem("gate_exp_wanted"), 3 * l + i + 1)
                step(nc.scalar.activation(best[:, 0:nh, :], best[:, 0:nh, :], ACT.Exp), "gate_exp_done")

            def expert_unit(n, half, first):
                act.wait_ge(sem("u_row_used"), n * K + K)
                nc.scalar.activation(gelus[:, half, :], dots[:, half, :], ACT.Gelu_apprx_tanh).then_inc(sem("gelu_ready"), 1)
                act.wait_ge(sem("expert_weights_ready"), n + 1)
                for k in range(K):
                    if not (first and half == 0 and k < DIAGS):
                        act.wait_ge(sem("v_row_used"), n * K + (k - DIAGS + 1))
                    nc.scalar.activation(diag[:, k % DIAGS, :], ident, ACT.Copy, scale=wts[:, half, k:k + 1])\
                        .then_inc(sem("diag_ready"), 1)

            act.wait_ge(sem("setup_loaded"), 16 * setup_loads)
            step(nc.scalar.activation(c_tok, c_tok, ACT.Silu), "c_silu")
            for k in range(KD):
                evacuate(("x", k), xT[:, k, :], TOK)
            for h in range(A_HEADS):
                evacuate(("rel", h), rel_rows[:, h, :], SKEW)
            def ada(l, i):
                for m in (2 * i, 2 * i + 1):
                    if i:
                        act.wait_ge(product_ready, nth["adaT", l, i - 1] + 1)
                    evacuate(("ada", l, m), ada_rows[:, m % 2, :], 512, NC)

            for l in range(DEPTH):
                if l:
                    act.wait_ge(*drain_of(("pt", l - 1, TILES[-1], 1)))
                squares()
                if l == 0:
                    for i in range(6):
                        ada(0, i)
                root(("ss1", l), rstd[:, :], D)
                modulate(l, 0)
                for m in PROJ_ORDER[:-4]:
                    key = ("proj", l, m)
                    if m == "ig":
                        continue
                    if m == "fg":
                        act.wait_ge(sem("gate_abs_ready"), l + 1)
                        step(nc.scalar.activation(row["M"], row["M"], ACT.Exp, scale=-1.0))
                        step(nc.scalar.activation(row["M"], row["M"], ACT.Ln, bias=1.0), "gate_log_ready")
                        continue
                    if 6 <= m < 14:
                        k = m - 6
                        b = product(act, key)
                        act.wait_ge(sem("cin_padded"), l + 1)
                        step(nc.scalar.activation(cin_p[:, k, 3:], b[:, ST], ACT.Copy))
                        step(nc.scalar.activation(cin_s[:, k, :, 3:], by_sample(b[:, SB]), ACT.Copy), A)
                    else:
                        m = m if m < 6 else m - 8
                        evacuate(key, region1[:, m, :], TOK)
                for t in range(3):
                    n = P if t < 2 else NS
                    evacuate(("kvtok", l, t), kvt[0:n, t, :], 2 * P, n)
                for j in range(2):
                    evacuate(("kct", l, j), kcT[:, 4 * j:4 * j + 4, :].rearrange("p b c -> p (b c)"), 512)
                act.wait_ge(sem("conv_done"), (l + 1) * KD)
                for j in range(2):
                    step(nc.scalar.activation(qks[:, 4 * j:4 * j + 4, :], qks[:, 4 * j:4 * j + 4, :], ACT.Silu), "silu_done")
                act.wait_ge(sem("rows_wanted"), l + 1)
                for r, s in (("e", -1.0), ("wl", 1.0), ("aw", 1.0)):
                    step(nc.scalar.activation(row[r], row[r], ACT.Exp, scale=s), "rows_done")
                softmax_exp(l, 0, S0, None, P)
                softmax_exp(l, 1, S1, None, 2 * P)
                for n in range(A_KV):
                    evacuate(("ssT", l, n), sT[:, n, :], P)
                softmax_exp(l, 2, SS, None, 160)
                for m in PROJ_ORDER[-4:]:
                    evacuate(("proj", l, m), region1[:, m - 8, :], TOK)
                for t in range(3):
                    n = P if t < 2 else NS
                    evacuate(("ktok", l, t), kt[0:n, t, :], 512, n)
                for t in range(3):
                    n = P if t < 2 else NS
                    evacuate(("vtok", l, t), vt[0:n, t, :], 512, n)
                for h in range(MH):
                    b = product(act, ("bM", l, h))
                    act.wait_ge(sem("cols_ready"), l + 1)
                    step(nc.scalar.activation(WT[:, h, 0:256], b[:, 0:256], ACT.Exp, bias=cols[:, 0, h:h + 1], scale=-1.0))
                    step(nc.scalar.activation(WT[:, h, 256:384], b[:, 256:384], ACT.Exp, bias=cols[:, 1, h:h + 1], scale=-1.0))
                    step(nc.scalar.activation(WT[0:NS, h, 384:416], b[0:NS, 384:416], ACT.Exp,
                                              bias=cols[0:NS, 2, h:h + 1], scale=-1.0), A)
                    evacuate(("bE", l, h), eh[:, h, :], TOK)
                for t in range(2):
                    for j in range(2 * (t + 1)):
                        if t == 0:
                            b = product(act, ("pT", l, t, j))
                            step(nc.scalar.activation(PT[:, 4 * j:4 * j + 4, 0, :], b.rearrange("p (h q) -> p h q", h=4), ACT.Copy), A)
                        else:
                            b = product(act, ("pT", l, t, j))
                            step(nc.scalar.activation(PT[:, 2 * j:2 * j + 2, :, :].rearrange("p h b q -> p (h b q)"), b, ACT.Copy), A)
                    b = product(act, ("o", l, t))
                    step(nc.scalar.activation(mixT[:, 0:4, t * P:(t + 1) * P], b.rearrange("p (j q) -> p j q", j=4), ACT.Copy), A)
                for n in range(A_KV):
                    b = product(act, ("spT", l, n))
                    step(nc.scalar.activation(PTs[:, n, 0, :], b[:, 0:P], ACT.Copy))
                    step(nc.scalar.activation(PTs[0:NS, n, 1, :], b[0:NS, P:2 * P], ACT.Copy), A)
                b = product(act, ("o", l, 2))
                step(nc.scalar.activation(mixT[:, 0:4, SB], b[:, 0:P].rearrange("p (j q) -> p j q", j=4), ACT.Copy), A)
                for h in range(MH):
                    for j in range(2):
                        b = product(act, ("CT", l, h, j))
                        step(nc.scalar.activation(CT[:, h % 2, 4 * j:4 * j + 4, :].rearrange("p b k -> p (b k)"), b, ACT.Copy), A)
                    act.wait_ge(*drain_of(("num", l, h)))
                    step(nc.scalar.activation(WT[:, h, 0:TOK], eh[:, h, :], ACT.Square), "hm_squares_ready")
                step(nc.scalar.activation(region1[:, OM:OM + 4, :], region1[:, OM:OM + 4, :], ACT.Sigmoid), "sigmoid_done")
                for h in range(MH):
                    root(("hss", l, h), WT[:, h, 0:TOK], MD)
                evacuate(("Cp", l), PTs_flat, 512)
                evacuate(("np", l), kcT_flat[0:1, 0:512], 512, 1)
                evacuate(("nnr", l), nrow, P, NS)
                for j in range(2):
                    evacuate(("cvr", l, j), pe_tok[0:27, 512 * j:512 * j + 512], 512, 27)
                for j in range(4):
                    evacuate(("ky", l, j), keyT[:, 4 * j:4 * j + 4, :].rearrange("p m k -> p (m k)"), 512)
                act.wait_ge(*drain_of(("out", l, KD - 1)))
                squares()
                root(("ss2", l), rstd[:, :], D)
                modulate(l, 1)
                for m in range(16):
                    evacuate(("qp", l, m), region1[:, m, :], TOK)
                for t in (2, 0, 1):
                    for j in range(2):
                        evacuate(("h2", l, t, j), h2tok[:, t, 512 * j:512 * j + 512], 512)
                gate_exp(l, 0, 2)
                for g in TILES:
                    base = first_slot[l, g] // K
                    if g == "S":
                        for half in range(2):
                            expert_unit(base + half, half, l == 0)
                        gate_exp(l, 1, 8)
                    elif g == "T0":
                        for n in range(8):
                            expert_unit(base + n, n % 2, False)
                            if n < 6 and l + 1 < DEPTH:
                                ada(l + 1, n)
                            if n == 4:
                                gate_exp(l, 2, 8)
                    else:
                        with act.Fori(0, UNITS[g] // 2) as i:
                            for half in range(2):
                                expert_unit(base + 2 * i + half, half, False)
                    act.wait_ge(sem("v_row_used"), first_slot[l, g] + UNITS[g] * K)
                    step(nc.scalar.activation(pe_tok[:, :], acc[:, :, :].rearrange("p c d -> p (c d)"), ACT.Copy), "experts_summed")
            act.wait_ge(*drain_of(("pt", DEPTH - 1, TILES[-1], 1)))
            squares()
            root(("ssf",), rstd[:, :], D)
            act.wait_ge(sem("xn_ready"), 2 * DEPTH + 1)
            for k in range(KD):
                step(nc.scalar.activation(hT[:, k, :], qks[:, k, :], ACT.Copy, scale=prm[:, 0, R_NFIN + k:R_NFIN + k + 1]), "y_ready")
            for t in range(3):
                n = P if t < 2 else NS
                for j in range(2):
                    evacuate(("y", t, j), x_tok[0:n, t, 512 * j:512 * j + 512], 512, n)

        @block.tensor
        def _(pe):
            mm, tr = nc.tensor.matmul, nc.tensor.transpose

            def done(ins):
                ins.then_inc(product_ready, 1)

            def transposes(key, parts):
                b = claim(pe, key)
                for c0, src in parts:
                    n, w = src.shape[0], src.shape[1]
                    ins = tr(b[0:w, c0:c0 + n], src, ident[0:n, 0:n])
                done(ins)

            def sum_squares(key, src, chunks):
                b = claim(pe, key)
                for k in range(chunks):
                    ins = mm(b[:, 0:TOK], ones, src[:, k, :] if chunks > 1 else src, start=k == 0, stop=k == chunks - 1)
                done(ins)

            used = 0

            def weight_tile():
                nonlocal used
                pe.wait_ge(sem(f"weights_loaded_{used % WSLOTS}"), 16 * (used // WSLOTS + 1))
                used += 1
                return wring[:, (used - 1) % WSLOTS, :, :]

            def project(key, w, c, src, n=P, last=False):
                b = claim(pe, key)
                for k in range(KD):
                    ins = mm(b[0:n, 0:TOK], w[:, k, c:c + n], src[:, k, :], start=k == 0, stop=k == KD - 1)
                done(ins)

            def release(key):
                pe.wait_ge(product_ready, nth[key] + 1)
                pe.sem_inc(sem("weights_used"), 1)

            def ada(l, i):
                for m in (2 * i, 2 * i + 1):
                    w = weight_tile()
                    b = claim(pe, ("ada", l, m))
                    for k in range(KD):
                        ins = mm(b[0:NC, :], cT[:, k, :], w[:, k, :], start=k == 0, stop=k == KD - 1)
                    done(ins)
                    release(("ada", l, m))
                pe.wait_ge(*drain_of(("ada", l, 2 * i + 1)))
                transposes(("adaT", l, i), [(NC * (4 * r + j), ada_rows[:, r, P * j:P * j + P]) for r in range(2) for j in range(4)])

            pe.wait_ge(sem("setup_loaded"), 16 * setup_loads)
            for l in range(DEPTH):
                transposes(("params", l), [(0, prm_rows[:, l, :])])
            for k in range(KD):
                transposes(("x", k), [(P * t, x_tok[0:P if t < 2 else NS, t, P * k:P * k + P]) for t in range(3)])
            pe.wait_ge(sem("c_silu"), 1)
            transposes(("c",), [(NC * k, c_tok[:, P * k:P * k + P]) for k in range(KD)])
            pe.wait_ge(sem("rel_spread"), A_HEADS)
            for h in range(A_HEADS):
                b = claim(pe, ("rel", h))
                done(mm(b[:, 0:SKEW], relb[:, h, :], hot, start=True, stop=True))

            pe.wait_ge(*drain_of(("c",)))
            for l in range(DEPTH):
                if l == 0:
                    for i in range(6):
                        ada(0, i)
                pe.wait_ge(sem("conv_state_loaded"), 16 * (l + 1))
                transposes(("cvs", l), [(24 * k, pe_tok[0:24, P * k:P * k + P]) for k in range(KD)])
                pe.wait_ge(sem("squares_ready"), 2 * l + 1)
                sum_squares(("ss1", l), hT, KD)
                pe.wait_ge(sem("h_ready"), KD * (2 * l + 1))
                pe.wait_ge(sem("h_sample_ready"), 2 * l + 1)
                def project_tile(tile):
                    w = weight_tile()
                    for j in range(4 if tile < 5 else 2):
                        project(("proj", l, 4 * tile + j), w, P * j, hT)
                    if tile == 5:
                        project(("proj", l, "ig"), w, 2 * P, hT, MH)
                        project(("proj", l, "fg"), w, 2 * P + MH, hT, MH)
                    release(("proj", l, "fg" if tile == 5 else 4 * tile + 3))

                for tile in PROJ_TILES[:-1]:
                    project_tile(tile)
                pe.wait_ge(*drain_of(("proj", l, KA + 1)))
                tiles = [(slice(P * t, min(P * t + P, TOK)), t) for t in range(3)]
                for tok, t in tiles:
                    transposes(("kvtok", l, t), [(P * j, region1[:, KA + j, tok]) for j in range(2)])
                pe.wait_ge(sem("kc_loaded"), 16 * (l + 1))
                for j in range(2):
                    transposes(("kct", l, j), [(P * b, kc[:, 4 * j + b, :]) for b in range(4)])
                pe.wait_ge(sem("k_doubled"), 64 * (l + 1))
                for t in range(2):
                    for j in range(4):
                        b = claim(pe, ("sc", l, t, j))
                        h0 = j // 2 * GROUP + j % 2
                        for i, h in enumerate((h0, h0 + 2)):
                            half = slice(h % 2 * DH, (h % 2 + 1) * DH)
                            c0 = P if t == 0 else 0
                            ins = mm(b[:, 256 * i + c0:256 * i + 256], region1[half, h // 2, P * t:P * t + P],
                                     kdup[half, h // GROUP, P * (t - 1) + c0:P * (t + 1)], start=True, stop=True)
                        done(ins)
                pe.wait_ge(sem("q_moved"), 128 * (l + 1))
                for n in range(A_KV):
                    half = slice(n * DH, (n + 1) * DH)
                    pe.wait_ge(*drain_of(("kct", l, 1)))
                    bk = claim(pe, ("ssT", l, n))
                    out = bk[:, 0:P].rearrange("p (g b s) -> p g b s", g=GROUP, b=DEC_B)
                    for b in range(DEC_B):
                        ins = mm(out[:, :, b, :], kcT[half, b, :], qd[half, :, DEC_S * b:DEC_S * b + DEC_S], start=True, stop=True)
                    done(ins)
                for n in range(A_KV):
                    half = slice(n * DH, (n + 1) * DH)
                    pe.wait_ge(*drain_of(("ssT", l, n)))
                    b = claim(pe, ("ss", l, n))
                    tr(b[:, 0:P], sT[:, n, :], ident)
                    done(mm(b[:, P:P + NS], qd[half, :, :].rearrange("p g t -> p (g t)"), kdup[half, n, SB], start=True, stop=True))
                project_tile(PROJ_TILES[-1])
                pe.wait_ge(sem("k_scaled"), l + 1)
                for tok, t in tiles:
                    transposes(("ktok", l, t), [(P * h, qks[:, 4 + h, tok]) for h in range(MH)])
                pe.wait_ge(*drain_of(("proj", l, 17)))
                for tok, t in tiles:
                    transposes(("vtok", l, t), [(P * h, region1[:, VM + h, tok]) for h in range(MH)])
                pe.wait_ge(sem("rows_done"), 3 * (l + 1))
                b = claim(pe, ("cols", l))
                for tok, t in tiles:
                    w = P if t < 2 else NS
                    for j, r in enumerate(("a", "wl")):
                        ins = tr(b[0:w, 8 * t + 4 * j:8 * t + 4 * j + 4], row[r][:, tok], ident[0:MH, 0:MH])
                done(ins)
                pe.wait_ge(sem("n_loaded"), 16 * (l + 1))
                transposes(("nT", l), [(0, nrow)])

                def select(h):
                    return ident[0:MH, h:h + 1].broadcast_to([MH, P])

                b = claim(pe, ("bA", l))
                for h in range(MH):
                    ins = mm(b[:, NS * h:NS * h + NS], select(h), row["aw"], start=True, stop=True)
                done(ins)
                for h in range(MH):
                    b = claim(pe, ("bM", l, h))
                    mm(b[:, 0:256], select(h), row["M"][:, 0:256], start=True, stop=False, skip_group_check=True)
                    mm(b[:, 256:384], select(h), row["M"][:, 128:256], start=False, stop=False, skip_group_check=True)
                    mm(b[:, 384:416], select(h), row["M"][:, 256:288], start=False, stop=False, skip_group_check=True)
                    mm(b[:, 0:128], ident, cst[:, C_CAUSAL:C_CAUSAL + P], start=False, stop=False, skip_group_check=True)
                    mm(b[:, 256:384], ident, cst[:, C_CAUSAL:C_CAUSAL + P], start=False, stop=False, skip_group_check=True)
                    done(mm(b[0:NS, 384:416], ident[0:NS, 0:NS], cst[0:NS, C_CAUSALS:C_CAUSALS + NS], start=False, stop=True, skip_group_check=True))
                    b = claim(pe, ("bE", l, h))
                    done(mm(b[:, 0:TOK], select(h), row["e"], start=True, stop=True))
                    b = claim(pe, ("qk", l, h))
                    mm(b[:, 0:256], qks[:, 4 + h, 0:128], qks[:, h, 0:256], start=True, stop=True)
                    mm(b[:, 256:384], qks[:, 4 + h, 128:256], qks[:, h, 128:256], start=True, stop=True)
                    done(mm(b[0:NS, 384:416], qks[:, 4 + h, SB], qks[:, h, SB], start=True, stop=True))
                for t in range(2):
                    pe.wait_ge(sem("probs_ready"), 3 * l + t + 1)
                    for j in range(2 * (t + 1)):
                        if t == 0:
                            transposes(("pT", l, t, j), [(P * i, S0[:, 4 * j + i, :]) for i in range(4)])
                        else:
                            transposes(("pT", l, t, j), [(P * (2 * i + kb), S1[:, 2 * j + i, P * kb:P * kb + P])
                                                         for i in range(2) for kb in range(2)])
                    pe.wait_ge(*drain_of(("pT", l, t, 2 * t + 1)))
                    b = claim(pe, ("o", l, t))
                    for h in range(A_HEADS):
                        half, v0 = slice(h % 2 * DH, (h % 2 + 1) * DH), P + h // GROUP * DH
                        for kb in range(t + 1):
                            ins = mm(b[half, P * (h // 2):P * (h // 2) + P], kvt[:, kb, v0:v0 + DH], PT[:, h, kb, :],
                                     start=kb == 0, stop=kb == t)
                    done(ins)
                pe.wait_ge(sem("probs_ready"), 3 * l + 3)
                for n in range(A_KV):
                    transposes(("spT", l, n), [(0, SS[:, n, 0:P]), (P, SS[:, n, P:P + NS])])
                pe.wait_ge(*drain_of(("spT", l, 1)))
                pe.wait_ge(sem("vc_loaded"), 16 * (l + 1))
                bk = claim(pe, ("o", l, 2))
                out = bk[:, 0:P].rearrange("p (j t) -> p j t", j=4)
                for n in range(A_KV):
                    v0 = n * DH
                    for odd in range(2):
                        half = slice(odd * DH, (odd + 1) * DH)
                        to = out[half, 2 * n:2 * n + 2, :]
                        new = PTs[0:NS, n, 1, :].rearrange("p (g t) -> p g t", g=GROUP)[:, odd::2, :]
                        old = PTs[:, n, 0, :].rearrange("p (g t) -> p g t", g=GROUP)[:, odd::2, :]
                        mm(to, kvt[0:NS, 2, P + v0:P + v0 + DH], new, start=True, stop=False, skip_group_check=True)
                        for b in range(DEC_B):
                            t = slice(DEC_S * b, DEC_S * b + DEC_S)
                            ins = mm(to[:, :, t], vc[:, b, v0:v0 + DH], old[:, :, t], start=False, stop=b == DEC_B - 1, skip_group_check=True)
                done(ins)
                pe.wait_ge(*drain_of(("vtok", l, 2)))
                pe.wait_ge(*drain_of(("ktok", l, 2)))
                pe.wait_ge(*drain_of(("qk", l, MH - 1)))
                pe.wait_ge(sem("q_weighted"), l + 1)
                for h in range(MH):
                    pe.wait_ge(sem(f"C_loaded_{h % 2}"), 16 * (2 * l + h // 2 + 1))
                    for j in range(2):
                        transposes(("CT", l, h, j), [(P * b, C_sb[:, h % 2, 4 * j + b, :]) for b in range(4)])
                    b = claim(pe, ("den", l, h))
                    mm(b[:, 0:256], ones, WT[:, h, 0:256], start=True, stop=False, skip_group_check=True)
                    mm(b[:, 128:256], ones, WT[:, h, 256:384], start=False, stop=False, skip_group_check=True)
                    mm(b[:, SB], ones[0:NS, :], WT[0:NS, h, 384:416], start=False, stop=False, skip_group_check=True)
                    done(mm(b[:, SB], ones, nqa[:, h, :], start=False, stop=True, skip_group_check=True))
                    v = slice(P * h, P * h + P)
                    pe.wait_ge(*drain_of(("CT", l, h, 1)))
                    b = claim(pe, ("num", l, h))
                    mm(b[:, 0:256], vt[:, 0, v], WT[:, h, 0:256], start=True, stop=False, skip_group_check=True)
                    mm(b[:, 128:256], vt[:, 1, v], WT[:, h, 256:384], start=False, stop=False, skip_group_check=True)
                    mm(b[:, SB], vt[0:NS, 2, v], WT[0:NS, h, 384:416], start=False, stop=False, skip_group_check=True)
                    for s in range(DEC_B):
                        t = slice(DEC_S * s, DEC_S * s + DEC_S)
                        ins = mm(b[:, 256 + DEC_S * s:256 + DEC_S * (s + 1)], CT[:, h % 2, s, :], qa[:, h, t],
                                 start=False, stop=s == DEC_B - 1, skip_group_check=True)
                    done(ins)
                    pe.wait_ge(sem("weighted_k_ready"), MH * l + h + 1)
                    for j in range(2):
                        b = claim(pe, ("Cs", l, h, j))
                        done(mm(b, vt[0:NS, 2, v], wk[:, 4 * j:4 * j + 4, :].rearrange("p b k -> p (b k)"), start=True, stop=True))
                for h in range(MH):
                    pe.wait_ge(sem("hm_squares_ready"), MH * l + h + 1)
                    sum_squares(("hss", l, h), WT[:, h, 0:TOK], 1)
                pe.wait_ge(sem("weighted_v_ready"), l + 1)
                b = claim(pe, ("Cp", l))
                for h in range(MH):
                    for t in range(2):
                        ins = mm(b[:, P * h:P * h + P], wv[:, t, h, :], kt[:, t, P * h:P * h + P], start=t == 0, stop=t == 1)
                done(ins)
                b = claim(pe, ("np", l))
                for h in range(MH):
                    for t in range(2):
                        ins = mm(b[0:1, P * h:P * h + P], cols[:, t, 4 + h:5 + h], kt[:, t, P * h:P * h + P], start=t == 0, stop=t == 1)
                done(ins)
                b = claim(pe, ("nn", l))
                for h in range(MH):
                    ins = mm(b[:, DEC_B * h:DEC_B * h + DEC_B], kt[0:NS, 2, P * h:P * h + P], WB[:, h, :], start=True, stop=True)
                done(ins)
                pe.wait_ge(*drain_of(("nn", l)))
                transposes(("nnr", l), [(0, nnT)])
                pe.wait_ge(sem("conv_rows_ready"), l + 1)
                for j in range(2):
                    transposes(("cvr", l, j), [(P * k, cvo[:, 4 * j + k, :]) for k in range(4)])
                pe.wait_ge(sem("keys_loaded"), 16 * (l + 1))
                for j in range(4):
                    transposes(("ky", l, j), [(P * i, keys_raw[:, 4 * j + i, :]) for i in range(4)])
                pe.wait_ge(sem("mlstm_out_ready"), MH * (l + 1))
                for tile in range(2):
                    w = weight_tile()
                    for j in range(4):
                        project(("out", l, 4 * tile + j), w, P * j, mixT)
                    release(("out", l, 4 * tile + 3))
                pe.wait_ge(sem("squares_ready"), 2 * l + 2)
                sum_squares(("ss2", l), hT, KD)
                pe.wait_ge(sem("h_ready"), KD * (2 * l + 2))
                pe.wait_ge(sem("h_sample_ready"), 2 * l + 2)
                for tile in range(4):
                    w = weight_tile()
                    for j in range(4):
                        project(("qp", l, 4 * tile + j), w, P * j, hT)
                    release(("qp", l, 4 * tile + 3))
                pe.wait_ge(*drain_of(("qp", l, 15)))
                b = claim(pe, ("rs", l, "S", 0))
                for q in range(4):
                    for i in range(4):
                        m = 4 * q + i
                        ins = mm(b[NS * q:NS * q + NS, P * i:P * i + P], region1[:, m, SB], keyT[:, m, :], start=True, stop=True)
                done(ins)

                pe.wait_ge(sem("h_repeated"), l + 1)
                for t in (2, 0, 1):
                    for j in range(2):
                        transposes(("h2", l, t, j), [(P * k, hT[:, 4 * j + k, P * t:P * t + P] if t < 2 else
                                                      hS4[:, 4 * j + k, :, :].rearrange("p q t -> p (q t)")) for k in range(4)])

                def key_scores(g, quads):
                    for j in quads:
                        b = claim(pe, ("rs", l, g, j))
                        for i in range(4):
                            m = 4 * j + i
                            ins = mm(b[:, P * i:P * i + P], region1[:, m, COL[g]:COL[g] + P], keyT[:, m, :], start=True, stop=True)
                        done(ins)

                def weighted_rows(n, half):
                    for k in range(K):
                        pe.wait_ge(sem("diag_ready"), n * K + (k + 1))
                        pe.wait_ge(v_loaded[k % RV], n * (16 * K // RV) + 16 * (k // RV + 1))
                        for c in range(2):
                            ins = mm(acc[:, c, :], diag[:, k % DIAGS, :], v_ring[:, k % RV, 512 * c:512 * c + 512],
                                     start=False, stop=False, skip_group_check=True)
                        ins.then_inc(sem("v_row_used"), 1)

                key_scores("T0", range(4))
                for g in TILES:
                    base = first_slot[l, g] // K
                    if (l, g) != (0, TILES[0]):
                        pe.wait_ge(sem("experts_summed"), 3 * l + TILES.index(g))
                    for c in range(2):
                        mm(acc[:, c, :], zeros[:, 0:P], zeros[:, :], start=True, stop=False, skip_group_check=True)
                    if g == "S":
                        for half in range(2):
                            weighted_rows(base + half, half)
                    elif g == "T0":
                        key_scores("T1", [0])
                        for n in range(8):
                            weighted_rows(base + n, n % 2)
                            if n < 3:
                                key_scores("T1", [n + 1])
                            if n < 6 and l + 1 < DEPTH:
                                ada(l + 1, n)
                    else:
                        with pe.Fori(0, UNITS[g] // 2) as i:
                            for half in range(2):
                                weighted_rows(base + 2 * i + half, half)
                    pe.wait_ge(sem("experts_summed"), 3 * l + TILES.index(g) + 1)
                    for j in range(2):
                        b = claim(pe, ("pt", l, g, j))
                        for k in range(4):
                            src = pe_tok[:, 512 * j + P * k:512 * j + P * k + P]
                            if g == "S":
                                ins = mm(b[:, NS * k:NS * k + NS], src, cst[:, C_SUM:C_SUM + NS], start=True, stop=True)
                            else:
                                ins = tr(b[:, P * k:P * k + P], src, ident)
                        done(ins)
            pe.wait_ge(sem("squares_ready"), 2 * DEPTH + 1)
            sum_squares(("ssf",), hT, KD)
            pe.wait_ge(sem("y_ready"), KD)
            for t in range(3):
                for j in range(2):
                    n = P if t < 2 else NS
                    transposes(("y", t, j), [(P * k, hT[:, 4 * j + k, P * t:P * t + n]) for k in range(4)])

        @block.vector
        def _(dve):
            step = Steps(dve, "dve_step")
            V = drained["V"]
            tt, ts, stt = nc.vector.tensor_tensor, nc.vector.tensor_scalar, nc.vector.scalar_tensor_tensor
            copy, reduce = nc.vector.tensor_copy, nc.vector.tensor_reduce

            def normalise(l, w):
                dve.wait_ge(*drain_of((("ss1", "ss2")[w], l) if l < DEPTH else ("ssf",)))
                step(nc.vector.reciprocal(rstd[:, :], rstd[:, :]))
                step(tt(qks[:, :, :], xT[:, :, :], bc(rstd[:, :], 1, [P, KD, TOK]), ALU.mult), "xn_ready")
                if l == DEPTH:
                    return
                modT = modT_all[:, l % 2]
                hs, xs = by_sample(hT[:, :, SB]), by_sample(qks[:, :, SB])
                full = [P, KD, DEC_B, DEC_S]
                step(tt(hs, xs, bc(modA[:, w, :, 1:NC], 3, full), ALU.mult))
                step(tt(hs, hs, bc(modT[:, 24 * w:24 * w + KD, 1:NC], 3, full), ALU.add), "h_sample_ready")

            def gated_add(modT, b, k0, n, gate0):
                full = [P, n, DEC_B, DEC_S]
                t = tmp[:, 0:n * NS].rearrange("p (k b s) -> p k b s", k=n, b=DEC_B)
                xs = by_sample(xT[:, k0:k0 + n, SB])
                step(tt(t, b.rearrange("p (k b s) -> p k b s", k=n, b=DEC_B), bc(modT[:, gate0 + k0:gate0 + k0 + n, 1:NC], 3, full), ALU.mult))
                step(tt(xs, xs, t, ALU.add), V)

            def softmax_max(i, S, sink):
                nh = S.shape[1]
                st = stat[i][:, :, 0:nh]
                step(reduce(st[:, 0, :], S, AX, ALU.max))
                step(tt(st[:, 0, :], st[:, 0, :], sink, ALU.max))
                step(ts(st[:, 1, :], st[:, 0, :], -1.0, None, ALU.mult))
                step(tt(st[:, 2, :], sink, st[:, 1, :], ALU.add), "exp_wanted")

            def softmax_norm(l, i, S):
                nh = S.shape[1]
                st = stat[i][:, :, 0:nh]
                dve.wait_ge(sem("exp_done"), 3 * l + i + 1)
                step(tt(st[:, 4, :], st[:, 3, :], st[:, 2, :], ALU.add))
                step(nc.vector.reciprocal(st[:, 4, :], st[:, 4, :]))
                step(tt(S, S, bc(st[:, 4, :], 2, list(S.shape)), ALU.mult), "probs_ready")

            def top16(vals, idx, src, width):
                r = rep[:, 0:width]
                step(nc.vector.max(vals[:, 0:8], src))
                step(nc.vector.max_index(idx[:, 0:8], vals[:, 0:8], src))
                step(nc.vector.match_replace(r, vals[:, 0:8], src, -3e38))
                step(nc.vector.max(vals[:, 8:16], r))
                return nc.vector.max_index(idx[:, 8:16], vals[:, 8:16], r)

            def route_heads(l, g, j):
                b = product(dve, ("rs", l, g, j))
                for m in range(4):
                    h, c = 2 * j + m // 2, m % 2
                    step(top16(s_top[:, h, c, :], i_top[:, h, c, :], b[:, P * m:P * m + P], P), V if m == 3 else None)
                if g == "S":
                    dve.wait_ge(*drain_of(("h2", l, 2, 1)))
                for h in (2 * j, 2 * j + 1):
                    full = [P, TOPK, TOPK]
                    step(tt(cand[:, h, :].rearrange("p (i j) -> p i j", i=TOPK), bc(s_top[:, h, 0, :], 2, full),
                            bc(s_top[:, h, 1, :], 1, full), ALU.add))
                    step(top16(best[:, h, :], pos[:, h, :], cand[:, h, :], TOPK * TOPK))

            def route_gates(l, g):
                i = TILES.index(g)
                nh = 2 if g == "S" else P_HEADS
                gates = g_all[:, TI[g], 0:nh * TOPK].rearrange("p (h k) -> p h k", h=nh)
                bst = best[:, 0:nh, :]
                mx = rep[:, 0:nh]
                step(copy(mx, bst[:, :, 0]))
                step(tt(bst, bst, bc(mx, 2, [P, nh, TOPK]), ALU.subtract), "gate_exp_wanted")
                pi = pij[:, :, 0:nh, :]
                pu = pi.bitcast(U32)
                step(ts(pu[:, 0], pos[:, 0:nh, :], 4, None, ALU.logical_shift_right))
                step(ts(pu[:, 1], pos[:, 0:nh, :], 15, None, ALU.bitwise_and))
                for c in range(2):
                    step(copy(pi[:, c], pu[:, c]))
                step(copy(i_topf[:, 0:nh], i_top[:, 0:nh]))
                full = [P, nh, TOPK, TOPK]
                hit = onehot[:, 0:nh]
                iota = cst[:, C_IOTA:C_IOTA + TOPK].unsqueeze(1).unsqueeze(1).broadcast_to(full)
                for c in range(2):
                    step(tt(hit, iota, bc(pi[:, c], 3, full), ALU.is_equal))
                    step(tt(hit, hit, bc(i_topf[:, 0:nh, c, :], 2, full), ALU.mult))
                    step(reduce(pi[:, c], hit, AX, ALU.add))
                step(stt(pi[:, 0], pi[:, 0], float(N_KEYS), pi[:, 1], ALU.mult, ALU.add))
                dve.wait_ge(sem("gate_exp_done"), 3 * l + i + 1)
                step(reduce(mx, bst, AX, ALU.add))
                step(nc.vector.reciprocal(mx, mx))
                step(tt(gates, bst, bc(mx, 2, [P, nh, TOPK]), ALU.mult))
                step(ts(idx_all[:, TI[g], 0:nh * TOPK].rearrange("p (h k) -> p h k", h=nh), pi[:, 0],
                        float(l * N_EXPERTS), None, ALU.add), "idx_ready")

            def expert_unit(g, i, half, n):
                for k in range(K):
                    dve.wait_ge(u_loaded[k % RU], n * (16 * K // RU) + 16 * (k // RU + 1))
                    row_ = u_ring[:, k % RU, :]
                    nc.vector.tensor_tensor_reduce(out=row_, in0=row_, in1=h2tok[:, TI[g], :], scale=1.0, scalar=0.0,
                                                   op0=ALU.mult, op1=ALU.add, accum_out=dots[:, half, k:k + 1])\
                        .then_inc(sem("u_row_used"), 1)
                dve.wait_ge(sem("gelu_ready"), n + 1)
                tt(wts[:, half, :], gelus[:, half, :], g_all[:, TI[g], bass.ds(i * 2 * K + half * K, K)], ALU.mult)\
                    .then_inc(sem("expert_weights_ready"), 1)

            step(nc.vector.memset(eps_t[:, :], EPS))
            step(nc.vector.memset(zeros[:, :], 0.0))
            dve.wait_ge(sem("setup_loaded"), 16 * setup_loads)
            step(nc.vector.memset(relraw[32:33, :], -BIG))
            for h in range(A_HEADS):
                step(ts(relb[:, h, :], ones[0:33, :], relraw[:, h:h + 1], None, ALU.mult), "rel_spread")
            for l in range(DEPTH):
                step(copy(prm[:, l, :], product(dve, ("params", l))[:, 0:R_ROWS]), V)
            step(copy(cT[:, :, :].rearrange("p k c -> p (k c)"), product(dve, ("c",))[:, 0:KD * NC]), V)
            def ada(l, i):
                b = product(dve, ("adaT", l, i))
                step(tt(modT_all[:, l % 2, 8 * i:8 * i + 8, :], b[:, 0:8 * NC].rearrange("p (j c) -> p j c", j=8),
                        bc(prm[:, l, R_BADA + 8 * i:R_BADA + 8 * i + 8], 2, [P, 8, NC]), ALU.add), V)

            for l in range(DEPTH):
                modT = modT_all[:, l % 2]
                if l == 0:
                    for i in range(6):
                        ada(0, i)
                for w, r in ((0, R_NMIX), (1, R_NFFN)):
                    step(stt(modA[:, w], modT[:, 24 * w + KD:24 * w + 2 * KD, :], 1.0,
                             bc(prm[:, l, r:r + KD], 2, [P, KD, NC]), ALU.add, ALU.mult))
                step(nc.vector.memset(cin_p[:, :, 0:3], 0.0))
                b = product(dve, ("cvs", l))
                step(copy(cin_s[:, :, :, 0:3], b[:, 0:192].rearrange("p (k b r) -> p k b r", k=KD, b=DEC_B)), V)
                step(nc.vector.memset(tmp[:, 0:1], 0.0), "cin_padded")
                normalise(l, 0)
                b = product(dve, ("proj", l, "ig"))
                if l == 0:
                    dve.wait_ge(sem("rel_stored"), 16)
                step(ts(row["ig"], b[0:MH, 0:TOK], gate_bias[:, l, 0:1], None, ALU.add), V)
                b = product(dve, ("proj", l, "fg"))
                step(ts(row["e"], b[0:MH, 0:TOK], gate_bias[:, l, 1:2], None, ALU.add), V)
                step(stt(row["M"], row["e"], -1.0, row["e"], ALU.mult, ALU.max), "gate_abs_ready")
                step(ts(row["b"], row["e"], 0.0, None, ALU.min))
                dve.wait_ge(sem("gate_log_ready"), l + 1)
                step(tt(row["wl"], row["b"], row["M"], ALU.subtract))
                s4 = {r: by_sample(row[r][:, SB]) for r in ("ig", "b", "a", "M", "e", "wl")}
                one = ones[0:MH, 0:1].broadcast_to([MH, SEQ])
                step(nc.vector.tensor_tensor_scan(row["b"][:, ST], one, row["wl"][:, ST], 0.0, ALU.mult, ALU.add))
                step(copy(s4["b"][:, :, 0], s4["wl"][:, :, 0]))
                for s in range(1, DEC_S):
                    step(tt(s4["b"][:, :, s], s4["b"][:, :, s - 1], s4["wl"][:, :, s], ALU.add))
                step(tt(row["a"], row["ig"], row["b"], ALU.subtract))
                step(nc.vector.tensor_tensor_scan(row["M"][:, ST], row["a"][:, ST], row["a"][:, ST], 0.0, ALU.max, ALU.max))
                dve.wait_ge(sem("m_loaded"), 16 * (l + 1))
                for s in range(DEC_S):
                    step(tt(s4["M"][:, :, s], s4["a"][:, :, s], m_in if s == 0 else s4["M"][:, :, s - 1], ALU.max))
                step(tt(row["e"], row["b"], row["M"], ALU.add))
                step(copy(m_out[:, 0:1], row["e"][:, SEQ - 1:SEQ]))
                step(copy(m_out[:, 1:NC], s4["e"][:, :, DEC_S - 1]), "m_out_ready")
                step(ts(row["wl"][:, ST], row["a"][:, ST], row["M"][:, SEQ - 1:SEQ], None, ALU.subtract))
                full = [MH, DEC_B, DEC_S]
                step(tt(s4["wl"], s4["a"], bc(s4["M"][:, :, DEC_S - 1], 2, full), ALU.subtract))
                step(tt(by_sample(row["aw"]), bc(m_in, 2, full), s4["M"], ALU.subtract), "rows_wanted")
                for k in range(KD):
                    dve.wait_ge(*drain_of(("proj", l, 6 + k)))
                    for i in range(CONV_W):
                        tap = prm[:, l, R_CONVW + KD * i + k:R_CONVW + KD * i + k + 1]
                        cb = prm[:, l, R_CONVB + k:R_CONVB + k + 1]
                        for dst, src in ((qks[:, k, ST], cin_p[:, k, i:i + SEQ]),
                                         (by_sample(qks[:, k, SB]), cin_s[:, k, :, i:i + DEC_S])):
                            last = i == CONV_W - 1 and dst.shape[-1] == DEC_S
                            step(ts(dst, src, tap, cb, ALU.mult, ALU.add) if i == 0 else
                                 stt(dst, src, tap, dst, ALU.mult, ALU.add), "conv_done" if last else None)
                step(copy(cvo[:, :, 0:3], cin_p[:, :, SEQ:SEQ + 3]))
                step(copy(cvo[:, :, 3:27].rearrange("p k (b r) -> p k b r", b=DEC_B), cin_s[:, :, :, DEC_S:DEC_S + 3]), "conv_rows_ready")
                if l == 0:
                    dve.wait_ge(sem("bias_loaded"), 16 * (1 + A_HEADS * (1 + DEC_B)))
                    step(tt(bias_s[:, :, WINDOW:], bias_s[:, :, WINDOW:],
                            bc(cst[:, C_BLOCKADD:C_BLOCKADD + NS], 1, [P, A_KV, NS]), ALU.add))
                for t, S in ((0, S0), (1, S1)):
                    lo = P if t == 0 else 0
                    for j in range(4):
                        b = product(dve, ("sc", l, t, j)).rearrange("p (h k) -> p h k", h=2)[:, :, lo:]
                        h0 = j // 2 * GROUP + j % 2
                        step(stt(S[:, h0:h0 + 3:2, :], b, DH ** -0.5, bias[:, h0:h0 + 3:2, lo:], ALU.mult, ALU.add), V)
                    softmax_max(t, S, sink_p[:, l, :])
                    if t == 0:
                        dve.wait_ge(sem("silu_done"), 2 * (l + 1))
                        step(ts(qks[:, 4:8, :], qks[:, 4:8, :], MD ** -0.5, None, ALU.mult), "k_scaled")
                softmax_norm(l, 0, S0)
                softmax_norm(l, 1, S1)
                for n in range(A_KV):
                    b = product(dve, ("ss", l, n))
                    step(stt(SS[:, n, :], b[:, 0:160], DH ** -0.5, bias_s[:, n, :], ALU.mult, ALU.add), V)
                softmax_max(2, SS, sink_s[:, l, :])
                b = product(dve, ("cols", l))
                step(copy(cols[:, 0:2, :].rearrange("p t c -> p (t c)"), b[:, 0:16]))
                step(copy(cols[0:NS, 2, :], b[0:NS, 16:24]), V)
                step(nc.vector.memset(tmp[:, 0:1], 0.0), "cols_ready")
                full = [NS, MH, DEC_B]
                step(tt(WB, bc(cst[0:NS, C_BLOCK:C_BLOCK + DEC_B], 1, full), bc(cols[0:NS, 2, 4:8], 2, full), ALU.mult))
                step(copy(nT, product(dve, ("nT", l))[:, 0:NS]), V)
                step(copy(abc.rearrange("p h t -> p (h t)"), product(dve, ("bA", l))[:, 0:P]), V)
                step(tt(qa, qks[:, 0:4, SB], abc, ALU.mult))
                full = [P, MH, DEC_B, DEC_S]
                n_hb = nT.rearrange("p (b h) -> p h b", b=DEC_B)
                step(tt(by_sample(nqa), by_sample(qa), bc(n_hb, 3, full), ALU.mult), "q_weighted")
                softmax_norm(l, 2, SS)
                for h in range(MH):
                    b = product(dve, ("qk", l, h))
                    dve.wait_ge(*drain_of(("bM", l, h)))
                    step(tt(WT[:, h, 0:384], WT[:, h, 0:384], b[:, 0:384], ALU.mult))
                    step(tt(WT[0:NS, h, 384:416], WT[0:NS, h, 384:416], b[0:NS, 384:416], ALU.mult), V)
                dve.wait_ge(*drain_of(("vtok", l, 2)))
                dve.wait_ge(product_ready, nth["pT", l, 1, 3] + 1)
                for t in range(2):
                    step(tt(wv[:, t], vt[:, t, :].rearrange("p (h v) -> p h v", h=MH), bc(cols[:, t, 4:8], 2, [P, MH, MD]), ALU.mult),
                         "weighted_v_ready" if t else None)
                al = [by_sample(abc[:, h, :])[:, :, DEC_S - 1] for h in range(MH)]
                for h in range(MH):
                    dve.wait_ge(*drain_of(("ktok", l, 2)))
                    if h:
                        dve.wait_ge(product_ready, nth["Cs", l, h - 1, 1] + 1)
                    full = [NS, DEC_B, MD]
                    step(tt(wk, bc(kt[0:NS, 2, P * h:P * h + P], 1, full), bc(WB[:, h, :], 2, full), ALU.mult), "weighted_k_ready")
                    b = product(dve, ("den", l, h))
                    dve.wait_ge(*drain_of(("bE", l, h)))
                    step(tt(eh[:, h, :], eh[:, h, :], b[:, 0:TOK], ALU.max))
                    step(stt(eh[:, h, :], b[:, 0:TOK], -1.0, eh[:, h, :], ALU.mult, ALU.max), V)
                    step(nc.vector.reciprocal(eh[:, h, :], eh[:, h, :]))
                    b = product(dve, ("num", l, h))
                    step(tt(eh[:, h, :], eh[:, h, :], b[:, 0:TOK], ALU.mult), V)
                    full = [P, DEC_B, MD]
                    step(tt(C_sb[:, h % 2], C_sb[:, h % 2], bc(al[h], 2, full), ALU.mult))
                    for j in range(2):
                        b = product(dve, ("Cs", l, h, j))
                        c = C_sb[:, h % 2, 4 * j:4 * j + 4, :].rearrange("p b k -> p (b k)")
                        step(tt(c, c, b, ALU.add), V)
                for h in range(MH):
                    dve.wait_ge(*drain_of(("hss", l, h)))
                    r = WT[:, h, 0:TOK]
                    step(nc.vector.reciprocal(r, r))
                    step(tt(eh[:, h, :], eh[:, h, :], r, ALU.mult))
                    if h == 0:
                        dve.wait_ge(sem("sigmoid_done"), l + 1)
                    step(stt(mixT[:, 4 + h, :], eh[:, h, :], prm[:, l, R_MNORM + h:R_MNORM + h + 1], region1[:, OM + h, :],
                             ALU.mult, ALU.mult), "mlstm_out_ready")
                n_new = nnT.rearrange("p (b h) -> p h b", b=DEC_B)
                a_hb = abc.rearrange("p h (b s) -> p h b s", b=DEC_B)[:, :, :, DEC_S - 1]
                step(tt(n_new, n_hb, a_hb, ALU.mult))
                b = product(dve, ("nn", l))
                step(tt(n_new, n_new, b[:, 0:NS].rearrange("p (h b) -> p h b", h=MH), ALU.add), V)
                for m in range(KD):
                    b = product(dve, ("out", l, m))
                    step(stt(xT[:, m, ST], b[:, ST], modT[:, 16 + m, 0:1], xT[:, m, ST], ALU.mult, ALU.add))
                    gated_add(modT, b[:, SB], m, 1, 16)
                normalise(l, 1)
                step(copy(hS4, bc(hT[:, :, SB], 2, [P, KD, 4, NS])), "h_repeated")
                route_heads(l, "S", 0)
                route_gates(l, "S")
                for g in TILES:
                    base = first_slot[l, g] // K
                    if g == "S":
                        expert_unit(g, 0, 0, base)
                        for j in range(3):
                            route_heads(l, "T0", j)
                        expert_unit(g, 0, 1, base + 1)
                        route_heads(l, "T0", 3)
                        route_gates(l, "T0")
                    elif g == "T0":
                        for n in range(8):
                            expert_unit(g, n // 2, n % 2, base + n)
                            if n < 4:
                                route_heads(l, "T1", n)
                            if n == 4:
                                route_gates(l, "T1")
                            if 1 <= n < 7 and l + 1 < DEPTH:
                                ada(l + 1, n - 1)
                    else:
                        with dve.Fori(0, UNITS[g] // 2) as i:
                            for half in range(2):
                                expert_unit(g, i, half, base + 2 * i + half)
                    for j in range(2):
                        b = product(dve, ("pt", l, g, j))
                        if g == "S":
                            gated_add(modT, b[:, 0:4 * NS], 4 * j, 4, 40)
                        else:
                            for k in range(4):
                                m, c = 4 * j + k, slice(COL[g], COL[g] + P)
                                step(stt(xT[:, m, c], b[:, P * k:P * k + P], modT[:, 40 + m, 0:1], xT[:, m, c], ALU.mult, ALU.add),
                                     V if k == 3 else None)
            normalise(DEPTH, 0)


_INS = ["x_prompt", "x_sample", "c_prompt", "c_sample", "cache_k", "cache_v", "state_conv", "state_C", "state_n", "state_m",
        "rel_bias", "w_ada", "b_ada", "norm_mix", "norm_ffn", "w_in", "conv_w", "conv_b", "gate_b", "attn_sinks", "m_norm",
        "w_out", "peer_query", "peer_keys", "peer_u", "peer_v", "norm_final"]
_OUTS = [(1, SEQ, D), (DEC_B, DEC_S, D)] + [
    s for B in (1, DEC_B) for s in ((DEPTH, B, WINDOW, A_KV, DH), (DEPTH, B, WINDOW, A_KV, DH), (DEPTH, B, CONV_W - 1, 2 * MH * MD),
                                    (DEPTH, B, MH, MD, MD), (DEPTH, B, MH, MD), (DEPTH, B, MH))]


def kernel(**inputs):
    import numpy as _np
    import concourse.bacc as _bacc
    from concourse import mybir as _mybir
    from concourse.bass_utils import run_bass_kernel_spmd as _run

    nc = _bacc.Bacc("TRN2", target_bir_lowering=False, num_devices=1)
    arrays = {f"in_{name}": _np.ascontiguousarray(inputs[name]) for name in _INS}
    arrays["in_consts"], arrays["in_buckets"] = constants()
    args = [nc.dram_tensor(name, a.shape, _mybir.dt.from_np(a.dtype), kind="ExternalInput").ap() for name, a in arrays.items()]
    args += [nc.dram_tensor(f"out_{i}", shape, _mybir.dt.float32, kind="ExternalOutput").ap() for i, shape in enumerate(_OUTS)]
    hybrid_trunk(nc, *args)
    r = _run(nc, [arrays], core_ids=[0])
    return tuple(r.results[0][f"out_{i}"] for i in range(len(_OUTS)))
```

```python
from contextlib import ExitStack

import numpy as np

import concourse.bass as bass
from concourse import mybir

F32 = mybir.dt.float32
I32 = mybir.dt.int32
U32 = mybir.dt.uint32
ALU = mybir.AluOpType
ACT = mybir.ActivationFunctionType
AX = mybir.AxisListType.X

P = 128
DEPTH, D, SEQ, DEC_B, DEC_S = 2, 1024, 256, 8, 4
KD = D // P
NS = DEC_B * DEC_S
TOK = SEQ + NS
NC = 1 + DEC_B
A_HEADS, A_KV, DH, WINDOW = 8, 2, 64, 128
GROUP = A_HEADS // A_KV
MH, MD = 4, 128
CONV_W = 4
EPS = 1e-6
BIG = 1e30
N_KEYS, P_HEADS, TOPK = 128, 8, 16
N_EXPERTS = N_KEYS * N_KEYS
IN_COLS = 2824
GATE_COL = IN_COLS - 2 * MH
QA, KA, VA, VM, OM = 0, 4, 5, 6, 10
SKEW = 384
K = 16
RU, RV = 4, 8
DIAGS = 4
BANKS = 6
WSLOTS = 2
R_NMIX, R_NFFN, R_BADA, R_CONVW, R_CONVB, R_MNORM, R_NFIN, R_ROWS = 0, 8, 16, 64, 96, 104, 108, 116
C_ID, C_ONE, C_CAUSAL, C_CAUSALS, C_BLOCK, C_BLOCKADD, C_SUM, C_IOTA, C_COLS = 0, 128, 256, 384, 416, 424, 456, 488, 504
TILES = ["S", "T0", "T1"]
UNITS = {"S": 2, "T0": 8, "T1": 8}
COL = {"T0": 0, "T1": 128, "S": 256}
TI = {"T0": 0, "T1": 1, "S": 2}


def constants():
    c = np.zeros((P, C_COLS), np.float32)
    p = np.arange(P)
    c[:, C_ID:C_ID + P] = np.eye(P)
    c[:, C_ONE:C_ONE + P] = 1.0
    c[:, C_CAUSAL:C_CAUSAL + P] = np.where(p[:, None] > p[None, :], BIG, 0)
    s, t = np.arange(NS)[:, None], np.arange(NS)[None, :]
    c[:NS, C_CAUSALS:C_CAUSALS + NS] = np.where((s // DEC_S == t // DEC_S) & (s <= t), 0, BIG)
    c[:NS, C_BLOCK:C_BLOCK + DEC_B] = s // DEC_S == np.arange(DEC_B)[None, :]
    c[:, C_BLOCKADD:C_BLOCKADD + NS] = np.where((p[:, None] % NS) // DEC_S == t // DEC_S, 0, -BIG)
    c[:, C_SUM:C_SUM + NS] = p[:, None] % NS == t
    c[:, C_IOTA:C_IOTA + TOPK] = np.arange(TOPK)
    hot = np.zeros((33, SKEW), np.float32)
    for x in range(SKEW):
        n = 255 - x
        if 0 <= n < WINDOW:
            large = 16 + int(np.log(max(n, 1) / 16) / np.log(WINDOW / 16) * 16) if n >= 16 else n
            hot[min(large, 31), x] = 1
        else:
            hot[32, x] = 1
    return c, hot


def plan():
    out = []

    def add(eng, *key):
        out.append((key, eng))

    def ada(l, i):
        add("A", "ada", l, 2 * i)
        add("A", "ada", l, 2 * i + 1)
        add("V", "adaT", l, i)

    for l in range(DEPTH):
        add("V", "params", l)
    for k in range(KD):
        add("A", "x", k)
    add("V", "c")
    for h in range(A_HEADS):
        add("A", "rel", h)
    for l in range(DEPTH):
        if l == 0:
            for i in range(2):
                ada(0, i)
        add("V", "cvs", l)
        add("A", "ss1", l)
        for m in PROJ_ORDER[:-4]:
            add("V" if m in ("ig", "fg") else "A", "proj", l, m)
        for t in range(3):
            add("A", "kvtok", l, t)
        for j in range(2):
            add("A", "kct", l, j)
        for t in range(2):
            for j in range(4):
                add("V", "sc", l, t, j)
        for n in range(2):
            add("A", "ssT", l, n)
        for n in range(2):
            add("V", "ss", l, n)
        for m in PROJ_ORDER[-4:]:
            add("A", "proj", l, m)
        if l == 0:
            ada(0, 2)
        for t in range(3):
            add("A", "ktok", l, t)
        for t in range(3):
            add("A", "vtok", l, t)
        add("V", "cols", l)
        add("V", "nT", l)
        add("V", "bA", l)
        for h in range(MH):
            add("A", "bM", l, h)
            add("A", "bE", l, h)
            add("V", "qk", l, h)
        if l == 0:
            ada(0, 3)
        for t in range(2):
            for j in range(2 * (t + 1)):
                add("A", "pT", l, t, j)
            add("A", "o", l, t)
        for n in range(2):
            add("A", "spT", l, n)
        add("A", "o", l, 2)
        for h in range(MH):
            if l == 0 and h in ADA_AT_HEAD:
                ada(0, ADA_AT_HEAD[h])
            for j in range(2):
                add("A", "CT", l, h, j)
            add("V", "den", l, h)
            add("V", "num", l, h)
            for j in range(2):
                add("V", "Cs", l, h, j)
        for h in range(MH):
            add("A", "hss", l, h)
        add("A", "Cp", l)
        add("A", "np", l)
        add("V", "nn", l)
        add("A", "nnr", l)
        for j in range(2):
            add("A", "cvr", l, j)
        for j in range(4):
            add("A", "ky", l, j)
        for m in range(KD):
            add("V", "out", l, m)
        add("A", "ss2", l, "S")
        add("A", "ss2", l, "T")
        for m in QUERY_TILES:
            add("A", "qpS", l, m)
        add("A", "qST", l)
        add("V", "rs", l, "S", 0)
        for j in range(2):
            add("A", "h2", l, 2, j)
        for m in range(3):
            for j in range(4):
                add("A", "qp", l, 4 * m + j)
        for m in range(2):
            add("V", "rs", l, "T0", m)
        for t in (0, 1):
            for j in range(2):
                add("A", "h2", l, t, j)
        add("V", "rs", l, "T0", 2)
        for j in range(4):
            add("A", "qp", l, 12 + j)
        for g in TILES:
            if g == "T0":
                add("V", "rs", l, "T0", 3)
                for n in range(8):
                    if n < 4:
                        add("V", "rs", l, "T1", n)
                    if 1 <= n < 7 and l + 1 < DEPTH:
                        ada(l + 1, n - 1)
            for j in range(2):
                add("V", "pt", l, g, j)
    add("A", "ssf")
    for t in range(3):
        for j in range(2):
            add("A", "y", t, j)
    return out


PROJ_TILES = [5, 1, 2, 3, 0, 4]
QUERY_TILES = [0, 1, 2, 3]
ROUTED = {"S": 1, "T0": 2, "T1": 4}
ADA_AT_HEAD = {1: 4, 3: 5}
PROJ_ORDER = [20, 21, "ig", "fg"] + [4 * t + j for t in PROJ_TILES[1:] for j in range(4)]


def hybrid_trunk(nc, x_prompt, x_sample, c_prompt, c_sample, cache_k, cache_v, state_conv, state_C, state_n, state_m,
                 rel_bias, w_ada, b_ada, norm_mix, norm_ffn, w_in, conv_w, conv_b, gate_b, attn_sinks, m_norm, w_out,
                 peer_query, peer_keys, peer_u, peer_v, norm_final, consts, buckets,
                 y_p, y_s, k_p, v_p, conv_p, C_p, n_p, m_p, k_s, v_s, conv_s, C_s, n_s, m_s):
    PLAN = plan()
    nth = {key: n for n, (key, _) in enumerate(PLAN)}
    drains = {key: sum(e == eng for _, e in PLAN[:n + 1]) for n, (key, eng) in enumerate(PLAN)}

    ctx = ExitStack()
    with ctx:
        ctx.enter_context(nc.allow_non_contiguous_dma(reason="a few rows of gates, biases and running maxima"))

        def sb(name, shape, dt=F32):
            return ctx.enter_context(nc.sbuf_tensor(name, shape, dt))

        sems = {}

        def sem(name):
            if name not in sems:
                sems[name] = ctx.enter_context(nc.semaphore(name))
            return sems[name]

        rel_dram = nc.dram_tensor("rel_skewed", (A_HEADS, P, SKEW), F32, kind="Internal").ap()

        cst = sb("cst", [P, C_COLS])
        ident, ones = cst[:, C_ID:C_ID + P], cst[:, C_ONE:C_ONE + P]
        wring = sb("wring", [P, WSLOTS, KD, 512])
        xT = sb("xT", [P, KD, TOK])
        hT = sb("hT", [P, KD, TOK])
        region1 = sb("region1", [P, 16, TOK])
        cin = sb("cin", [P, KD * (SEQ + 3) + KD * DEC_B * (DEC_S + 3)])
        cin_p = cin[:, 0:KD * (SEQ + 3)].rearrange("p (k t) -> p k t", k=KD)
        cin_s = cin[:, KD * (SEQ + 3):].rearrange("p (k b t) -> p k b t", k=KD, b=DEC_B)
        keyT = cin[:, 0:16 * P].rearrange("p (m k) -> p m k", m=16)
        qks = sb("qks", [P, KD, TOK])
        qks_flat = qks[:, :, :].rearrange("p k t -> p (k t)")
        mixT = sb("mixT", [P, KD, TOK])
        mixT_flat = mixT[:, :, :].rearrange("p k t -> p (k t)")
        ada_rows = mixT_flat[:, 0:2 * P].rearrange("p (r c) -> p r c", r=2)
        query_rows = mixT_flat[:, 0:4 * P].rearrange("p (m c) -> p m c", m=4)
        bias = sb("bias", [P, A_HEADS, 2 * WINDOW])
        bias_s = sb("bias_s", [P, A_KV, WINDOW + NS])
        prm = sb("prm", [P, DEPTH, R_ROWS])
        gate_bias = sb("gate_bias", [MH, DEPTH, 2])
        sink_p = sb("sink_p", [P, DEPTH, A_HEADS])
        sink_s = sb("sink_s", [P, DEPTH, A_KV])
        eps_t = sb("eps_t", [P, 1])
        cT = sb("cT", [P, KD, NS])
        modT_all = sb("modT", [P, 2, 48, NC])
        modA = sb("modA", [P, 2, KD, NC])
        rstd = sb("rstd", [P, TOK])
        diag = sb("diag", [P, DIAGS, P])
        dots = sb("dots", [P, 2, K])
        gelus = sb("gelus", [P, 2, K])
        wts = sb("wts", [P, 2, K])
        idx_staged = sb("idx_staged", [P, 2, K], I32)
        idx_all = sb("idx_all", [P, 3, P_HEADS * TOPK], I32)
        g_all = sb("g_all", [P, 3, P_HEADS * TOPK])

        rings = sb("rings", [P, (RU + RV) * D])
        u_ring = rings[:, 0:RU * D].rearrange("p (r d) -> p r d", r=RU)
        v_ring = rings[:, RU * D:].rearrange("p (r d) -> p r d", r=RV)

        query_w = v_ring.rearrange("p (i h) d -> p i (h d)", i=2).rearrange("p i (k n) -> p i k n", k=KD)

        class Cut:
            def __init__(self, region, size):
                self.region, self.size, self.at = region, size, 0

            def __call__(self, n, parts=P):
                self.at += n
                assert self.at <= self.size, self.at
                return self.region[0:parts, self.at - n:self.at]

        cut = Cut(rings, (RU + RV) * D)
        C_flat = cut(2048)
        keys_raw = C_flat.rearrange("p (m k) -> p m k", m=16)
        C_sb = C_flat.rearrange("p (r b k) -> p r b k", r=2, b=DEC_B)
        CT_flat = cut(2048)
        CT = CT_flat.rearrange("p (r b k) -> p r b k", r=2, b=DEC_B)
        kc = cut(1024).rearrange("p (b c) -> p b c", b=DEC_B)
        vc = cut(1024).rearrange("p (b c) -> p b c", b=DEC_B)
        kcT_flat = cut(1024)
        kcT = kcT_flat.rearrange("p (b c) -> p b c", b=DEC_B)
        PT = cut(2048).rearrange("p (h b q) -> p h b q", h=A_HEADS, b=2)
        sT = cut(256).rearrange("p (n r) -> p n r", n=2)
        SS = cut(2 * 160).rearrange("p (n r) -> p n r", n=2)
        PTs_flat = cut(512)
        PTs = PTs_flat.rearrange("p (n j r) -> p n j r", n=2, j=2)
        row = {n: cut(TOK, MH) for n in ("ig", "b", "a", "M", "e", "wl")}
        row["aw"] = cut(NS, MH)
        x_tok = rings[:, 0:3 * D].rearrange("p (t d) -> p t d", t=3)
        c_tok = rings[0:NC, 3 * D:4 * D]
        prm_rows = rings[0:R_ROWS, 4 * D:4 * D + 2 * P].rearrange("p (l c) -> p l c", l=2)
        hot = rings[0:33, 5 * D:5 * D + SKEW]
        relb = rings[0:33, 6 * D:7 * D].rearrange("p (h c) -> p h c", h=A_HEADS)
        relraw = rings[0:33, 7 * D:7 * D + 8]
        rel_rows = rings[:, 8 * D:8 * D + 8 * SKEW].rearrange("p (h c) -> p h c", h=A_HEADS)
        hT_flat = hT[:, :, :].rearrange("p k t -> p (k t)")
        S1 = CT_flat.rearrange("p (h k) -> p h k", h=A_HEADS)
        S0 = mixT[:, 4:8, :].rearrange("p k t -> p (k t)")[:, 0:A_HEADS * P].rearrange("p (h k) -> p h k", h=A_HEADS)
        wv = hT_flat[:, 0:1024].rearrange("p (t h c) -> p t h c", t=2, h=MH)

        MSIZE = 6912
        mreg = sb("mreg", [P, MSIZE])
        cut = Cut(mreg, MSIZE)
        vt = cut(3 * 512).rearrange("p (t c) -> p t c", t=3)
        kt = cut(3 * 512).rearrange("p (t c) -> p t c", t=3)
        WT = cut(4 * 416).rearrange("p (h c) -> p h c", h=MH)
        eh_flat = cut(MH * TOK)
        eh = eh_flat.rearrange("p (h c) -> p h c", h=MH)
        kdup = eh_flat[:, 0:A_KV * TOK].rearrange("p (n t) -> p n t", n=A_KV)
        qd = eh_flat[:, A_KV * TOK:A_KV * TOK + GROUP * NS].rearrange("p (g t) -> p g t", g=GROUP)
        wk = cut(1024, NS).rearrange("p (b k) -> p b k", b=DEC_B)
        cut = Cut(mreg, MSIZE)
        h2tok = cut(3 * D).rearrange("p (t d) -> p t d", t=3)
        cand_flat = cut(2048)
        cand = cand_flat.rearrange("p (h c) -> p h c", h=P_HEADS)
        onehot = cand_flat.rearrange("p (h i j) -> p h i j", h=P_HEADS, i=TOPK)
        hS4 = cand_flat[:, 0:1024].rearrange("p (k q t) -> p k q t", k=KD, q=4)
        rep = cut(256)
        s_top = cut(256).rearrange("p (h c k) -> p h c k", h=P_HEADS, c=2)
        i_top = cut(256).bitcast(U32).rearrange("p (h c k) -> p h c k", h=P_HEADS, c=2)
        i_topf = cut(256).rearrange("p (h c k) -> p h c k", h=P_HEADS, c=2)
        best = cut(128).rearrange("p (h k) -> p h k", h=P_HEADS)
        pos = cut(128).bitcast(U32).rearrange("p (h k) -> p h k", h=P_HEADS)
        pij_flat = cut(256)
        pij = pij_flat.rearrange("p (c h k) -> p c h k", c=2, h=P_HEADS)
        small = sb("small", [P, 1000])
        cut = Cut(small, 1000)
        stat = [cut(40).rearrange("p (w h) -> p w h", w=5) for _ in range(3)]
        cols = cut(24).rearrange("p (t c) -> p t c", t=3)
        WB = cut(32, NS).rearrange("p (h b) -> p h b", h=MH)
        nrow = cut(P, NS)
        nT = cut(32)
        nnT = cut(32)
        abc = cut(P).rearrange("p (h t) -> p h t", h=MH)
        qa = cut(P).rearrange("p (h t) -> p h t", h=MH)
        nqa = cut(P).rearrange("p (h t) -> p h t", h=MH)
        m_in = cut(DEC_B, MH)
        m_out = cut(NC, MH)
        tmp = cut(P)
        zeros = sb("zeros", [P, P])
        pe_tok = sb("pe_tok", [P, D])
        ada_rows_mid = pe_tok[:, 0:2 * P].rearrange("p (r c) -> p r c", r=2)
        cvo = sb("cvo", [P, KD, 27])
        kvt = sb("kvt", [P, 3, 2 * P])

        banks = ctx.enter_context(nc.psum_tensor("banks", [P, BANKS, 512], F32))
        acc = ctx.enter_context(nc.psum_tensor("acc", [P, 2, 512], F32))

        product_ready = sem("product_ready")
        drained = {"A": sem("drained_by_act"), "V": sem("drained_by_dve")}

        def bank(key):
            return banks[:, nth[key] % BANKS, :]

        def drain_of(key):
            return drained[PLAN[nth[key]][1]], drains[key]

        def claim(pe, key):
            if nth[key] >= BANKS:
                pe.wait_ge(*drain_of(PLAN[nth[key] - BANKS][0]))
            return bank(key)

        class Steps:
            def __init__(self, eng, own):
                self.eng, self.own, self.count = eng, own, {}

            def __call__(self, ins, signal=None):
                s = signal or self.own
                ins.then_inc(sem(s) if isinstance(s, str) else s, 1)
                n = self.count[str(s)] = self.count.get(str(s), 0) + 1
                self.eng.wait_ge(sem(s) if isinstance(s, str) else s, n)

        def product(eng, key):
            eng.wait_ge(product_ready, nth[key] + 1)
            return bank(key)

        def bc(ap, axis, shape):
            return ap.unsqueeze(axis).broadcast_to(shape)

        def by_sample(ap):
            return ap.rearrange("p (b s) -> p b s", b=DEC_B) if len(ap.shape) == 2 else \
                ap.rearrange("p k (b s) -> p k b s", b=DEC_B)

        SB, ST = slice(SEQ, TOK), slice(0, SEQ)
        setup_loads = 7 + DEPTH * (9 + A_HEADS)
        first_slot, slots = {}, 0
        for l in range(DEPTH):
            for g in TILES:
                first_slot[l, g] = slots
                slots += UNITS[g] * K
        u_loaded = [sem(f"u_row_loaded_{r}") for r in range(RU)]
        v_loaded = [sem(f"v_row_loaded_{r}") for r in range(RV)]

        block = ctx.enter_context(nc.Block())

        @block.sync
        def _(sp):
            load = lambda dst, src: sp.dma_start(dst, src).then_inc(sem("setup_loaded"), 16)
            load(cst[:, :], consts)
            load(hot, buckets)
            load(relraw[0:32, :], rel_bias)
            load(x_tok[:, 0:2, :], x_prompt[0].rearrange("(t p) d -> p t d", p=P))
            load(x_tok[0:NS, 2, :], x_sample.rearrange("b s d -> (b s) d"))
            load(c_tok[0:1, :], c_prompt)
            load(c_tok[1:NC, :], c_sample)
            for l in range(DEPTH):
                for r, src, n in ((R_NMIX, norm_mix[l], 8), (R_NFFN, norm_ffn[l], 8), (R_BADA, b_ada[l], 48),
                                  (R_CONVB, conv_b[l], 8), (R_MNORM, m_norm[l], 4), (R_NFIN, norm_final, 8)):
                    load(prm_rows[r:r + n, l, :], src.rearrange("(k c) -> k c", c=P))
                load(prm_rows[R_CONVW:R_CONVW + 32, l, :], conv_w[l].rearrange("i (k c) -> (i k) c", c=P))
                load(gate_bias[:, l, :], gate_b[l].rearrange("(g h) -> h g", g=2))
                load(sink_p[:, l, :], attn_sinks[l:l + 1, :].broadcast_to([P, A_HEADS]))
                for h in range(A_HEADS):
                    n, g = h // GROUP, h % GROUP
                    load(sink_s[g * NS:(g + 1) * NS, l, n:n + 1],
                         attn_sinks[l:l + 1, h:h + 1].broadcast_to([NS, 1]))
            tile = 0
            for l in range(DEPTH):
                def weights(src, c0, n, layer=l):
                    nonlocal tile
                    if tile >= WSLOTS:
                        sp.wait_ge(sem("weights_used"), tile - WSLOTS + 1)
                    sp.dma_start(wring[:, tile % WSLOTS, :, 0:n],
                                 src[layer, :, c0:c0 + n].rearrange("(k p) n -> p k n", p=P))\
                        .then_inc(sem(f"weights_loaded_{tile % WSLOTS}"), 16)
                    tile += 1

                if l == 0:
                    for m in range(4):
                        weights(w_ada, 512 * m, 512)
                for m in PROJ_TILES:
                    weights(w_in, 512 * m, min(512, IN_COLS - 512 * m))
                    if m == 5:
                        if l:
                            sp.wait_ge(*drain_of(("pt", l - 1, TILES[-1], 1)))
                        else:
                            sp.wait_ge(sem("rel_stored"), 16)
                        sp.dma_start(kc, cache_k[l].rearrange("b w h d -> w b (h d)")).then_inc(sem("kc_loaded"), 16)
                        sp.dma_start(vc, cache_v[l].rearrange("b w h d -> w b (h d)")).then_inc(sem("vc_loaded"), 16)
                if l == 0:
                    for m in range(4, 12):
                        weights(w_ada, 512 * m, 512)
                for m in range(2):
                    weights(w_out, 512 * m, 512)
                sp.wait_ge(sem("scratch_free"), l + 1)
                for i, m in enumerate(QUERY_TILES[:2]):
                    sp.dma_start(query_w[:, i], peer_query[l, :, 512 * m:512 * m + 512].rearrange("(k p) n -> p k n", p=P))\
                        .then_inc(sem("query_weights_loaded"), 16)
                for m in QUERY_TILES[2:]:
                    weights(peer_query, 512 * m, 512)
                if l + 1 < DEPTH:
                    for m in range(12):
                        weights(w_ada, 512 * m, 512, l + 1)
            sp.wait_ge(*drain_of(("y", 2, 1)))
            sp.dma_start(y_p[0].rearrange("(t p) d -> p t d", p=P), x_tok[:, 0:2, :]).then_inc(sem("y_stored"), 16)
            sp.dma_start(y_s.rearrange("b s d -> (b s) d"), x_tok[0:NS, 2, :]).then_inc(sem("y_stored"), 16)
            sp.wait_ge(sem("y_stored"), 32)

        @block.gpsimd
        def _(pool):
            u_rows = peer_u.rearrange("l e d -> (l e) d")
            v_rows = peer_v.rearrange("l e d -> (l e) d")
            u_free = pool.alloc_register("u_free")
            v_free = pool.alloc_register("v_free")
            stage_free = pool.alloc_register("stage_free")
            pool.reg_mov(u_free, 1)
            pool.reg_mov(v_free, 1)
            pool.reg_mov(stage_free, K)
            stored = 0

            def store(dst, src):
                nonlocal stored
                pool.dma_start(dst, src).then_inc(sem("outputs_stored"), 16)
                stored += 16

            def unit(g, i, half, n, first, made=None):
                if not first:
                    pool.wait_ge(sem("v_row_used"), stage_free)
                    pool.reg_add(stage_free, stage_free, K)
                pool.tensor_copy(idx_staged[:, half, :], idx_all[:, TI[g], bass.ds(i * 2 * K + half * K, K)])\
                    .then_inc(sem("idx_staged"), 1)
                pool.wait_ge(sem("idx_staged"), n + 1)
                for k in range(K):
                    if not (first and half == 0 and k < RU):
                        pool.wait_ge(sem("u_row_used"), u_free)
                        pool.reg_add(u_free, u_free, 1)
                    pool.indirect_dma_start(
                        out=u_ring[:, k % RU, :], out_offset=None, in_=u_rows,
                        in_offset=bass.IndirectOffsetOnAxis(ap=idx_staged[:, half, k:k + 1], axis=0))\
                        .then_inc(u_loaded[k % RU], 16)
                if made:
                    pool.wait_ge(product_ready, nth[made] + 1)
                for k in range(K):
                    if not (first and half == 0 and k < RV):
                        pool.wait_ge(sem("v_row_used"), v_free)
                        pool.reg_add(v_free, v_free, 1)
                    pool.indirect_dma_start(
                        out=v_ring[:, k % RV, :], out_offset=None, in_=v_rows,
                        in_offset=bass.IndirectOffsetOnAxis(ap=idx_staged[:, half, k:k + 1], axis=0))\
                        .then_inc(v_loaded[k % RV], 16)

            for l in range(DEPTH):
                if l:
                    pool.wait_ge(*drain_of(("pt", l - 1, TILES[-1], 1)))
                else:
                    pool.wait_ge(sem("setup_loaded"), 16 * setup_loads)
                    pool.wait_ge(*drain_of(("x", KD - 1)))
                pool.dma_start(pe_tok[0:24, :], state_conv[l].rearrange("b r c -> (b r) c")).then_inc(sem("conv_state_loaded"), 16)
                pool.dma_start(nrow, state_n[l].rearrange("b h k -> (b h) k")).then_inc(sem("n_loaded"), 16)
                pool.dma_start(m_in, state_m[l].rearrange("b h -> h b")).then_inc(sem("m_loaded"), 16)
                if l == 0:
                    pool.wait_ge(*drain_of(("rel", A_HEADS - 1)))
                    pool.dma_start(rel_dram.rearrange("h p c -> p h c"), rel_rows).then_inc(sem("rel_stored"), 16)
                    pool.wait_ge(sem("rel_stored"), 16)
                    skew = lambda off, ap: bass.AP(rel_dram.tensor, off, ap)
                    pool.dma_start(bias[:, :, :], skew(127, [[SKEW - 1, P], [P * SKEW, A_HEADS], [1, 2 * WINDOW]]))\
                        .then_inc(sem("bias_loaded"), 16)
                    for h in range(A_HEADS):
                        n, g = h // GROUP, h % GROUP
                        src = slice(g * NS, (g + 1) * NS)
                        pool.dma_start(bias_s[src, n, 0:WINDOW], skew(h * P * SKEW + 127, [[0, DEC_B], [SKEW - 1, DEC_S], [1, WINDOW]]))\
                            .then_inc(sem("bias_loaded"), 16)
                        for b in range(DEC_B):
                            pool.dma_start(bias_s[src, n, WINDOW + b * DEC_S:WINDOW + (b + 1) * DEC_S],
                                           skew(h * P * SKEW + 127 + WINDOW, [[0, DEC_B], [SKEW - 1, DEC_S], [1, DEC_S]]))\
                                .then_inc(sem("bias_loaded"), 16)
                def load_C(h):
                    pool.dma_start(C_sb[:, h % 2, :, :], state_C[l, :, h].rearrange("b v k -> v b k"))\
                        .then_inc(sem(f"C_loaded_{h % 2}"), 16)
                load_C(0)
                load_C(1)
                pool.wait_ge(*drain_of(("proj", l, KA)))
                for n in range(A_KV):
                    for half in range(2):
                        pool.dma_start(kdup[half * DH:(half + 1) * DH, n, :], region1[n * DH:(n + 1) * DH, KA, :])\
                            .then_inc(sem("k_doubled"), 16)
                pool.wait_ge(*drain_of(("proj", l, QA + 3)))
                for n in range(A_KV):
                    for g in range(GROUP):
                        h = n * GROUP + g
                        pool.dma_start(qd[n * DH:(n + 1) * DH, g, :], region1[h % 2 * DH:(h % 2 + 1) * DH, h // 2, SB])\
                            .then_inc(sem("q_moved"), 16)
                pool.wait_ge(*drain_of(("kvtok", l, 2)))
                for dst_p, dst_s, cache, c0, loaded in ((k_p, k_s, kc, 0, "kc_loaded"), (v_p, v_s, vc, P, "vc_loaded")):
                    store(dst_p[l, 0].rearrange("w h d -> w (h d)"), kvt[:, 1, c0:c0 + P])
                    pool.wait_ge(sem(loaded), 16 * (l + 1))
                    store(dst_s[l, :, 0:WINDOW - DEC_S].rearrange("b w h d -> w b (h d)"), cache[DEC_S:WINDOW, :, :])
                    for b in range(DEC_B):
                        store(dst_s[l, b, WINDOW - DEC_S:].rearrange("w h d -> w (h d)"), kvt[b * DEC_S:(b + 1) * DEC_S, 2, c0:c0 + P])
                pool.wait_ge(sem("m_out_ready"), l + 1)
                store(m_p[l, 0].unsqueeze(1), m_out[:, 0:1])
                store(m_s[l].rearrange("b h -> h b"), m_out[:, 1:NC])
                for h in range(MH):
                    pool.wait_ge(*drain_of(("Cs", l, h, 1)))
                    store(C_s[l, :, h].rearrange("b v k -> v b k"), C_sb[:, h % 2, :, :])
                    if h + 2 < MH:
                        pool.wait_ge(sem("outputs_stored"), stored)
                        load_C(h + 2)
                pool.wait_ge(sem("outputs_stored"), stored)
                pool.dma_start(keys_raw, peer_keys[l].rearrange("h c k d -> k (h c) d")).then_inc(sem("keys_loaded"), 16)
                pool.wait_ge(*drain_of(("np", l)))
                store(C_p[l, 0].rearrange("h v k -> v h k"), PTs_flat.rearrange("p (h k) -> p h k", h=MH))
                store(n_p[l, 0].rearrange("h k -> (h k)").unsqueeze(0), kcT_flat[0:1, 0:512])
                pool.wait_ge(*drain_of(("nnr", l)))
                store(n_s[l].rearrange("b h k -> (b h) k"), nrow)
                pool.wait_ge(*drain_of(("cvr", l, 1)))
                store(conv_p[l, 0], pe_tok[0:3, :])
                store(conv_s[l].rearrange("b r c -> (b r) c"), pe_tok[3:27, :])
                pool.wait_ge(sem("outputs_stored"), stored)
                pool.sem_inc(sem("scratch_free"), 1)
                for g in TILES:
                    base = first_slot[l, g] // K
                    pool.wait_ge(sem("idx_ready"), 4 * l + ROUTED[g])
                    if g == "T0":
                        for first in (0, 2):
                            if first:
                                pool.wait_ge(sem("idx_ready"), 4 * l + ROUTED[g] + 1)
                            with pool.Fori(first, first + 2) as i:
                                for half in range(2):
                                    unit(g, i, half, base + 2 * i + half, False)
                    elif g == "S":
                        for half in range(2):
                            unit(g, 0, half, base + half, l == 0, made=("qp", l, 7) if half == 0 else None)
                    else:
                        with pool.Fori(0, UNITS[g] // 2) as i:
                            for half in range(2):
                                unit(g, i, half, base + 2 * i + half, False)

        @block.scalar
        def _(act):
            step = Steps(act, "act_step")
            A = drained["A"]

            def evacuate(key, dst, cols=None, parts=None, src=None):
                b = product(act, key)
                src = b[:, 0:cols] if src is None else src
                if parts is not None:
                    src = src[0:parts]
                step(nc.scalar.activation(dst, src, ACT.Copy), A)

            def root(key, dst, n):
                b = product(act, key)
                step(nc.scalar.activation(dst, b[:, 0:dst.shape[-1]], ACT.Sqrt, bias=eps_t[:, 0:1], scale=1.0 / n), A)

            def squares(cols=slice(0, TOK)):
                step(nc.scalar.activation(hT[:, :, cols], xT[:, :, cols], ACT.Square), "squares_ready")

            def modulate(l, w):
                modT = modT_all[:, l % 2]
                act.wait_ge(sem("xn_ready"), 2 * l + w + 1)
                shift = 24 * w
                for k in range(KD):
                    step(nc.scalar.activation(hT[:, k, ST], qks[:, k, ST], ACT.Identity,
                                              bias=modT[:, shift + k, 0:1], scale=modA[:, w, k, 0:1]), "h_ready")

            def softmax_exp(l, i, S, sink, width):
                act.wait_ge(sem("exp_wanted"), 3 * l + i + 1)
                nh = S.shape[1]
                for h in range(nh):
                    step(nc.scalar.activation(S[:, h, :], S[:, h, :], ACT.Exp, bias=stat[i][:, 1, h:h + 1],
                                              accum_out=stat[i][:, 3, h:h + 1]))
                step(nc.scalar.activation(stat[i][:, 2, 0:nh], stat[i][:, 2, 0:nh], ACT.Exp), "exp_done")

            def gate_exp(l, routed, heads):
                act.wait_ge(sem("gate_exp_wanted"), 4 * l + routed)
                step(nc.scalar.activation(best[:, heads, :], best[:, heads, :], ACT.Exp), "gate_exp_done")

            def expert_unit(n, half, first):
                act.wait_ge(sem("u_row_used"), n * K + K)
                nc.scalar.activation(gelus[:, half, :], dots[:, half, :], ACT.Gelu_apprx_tanh).then_inc(sem("gelu_ready"), 1)
                act.wait_ge(sem("expert_weights_ready"), n + 1)
                for k in range(K):
                    if not (first and half == 0 and k < DIAGS):
                        act.wait_ge(sem("v_row_used"), n * K + (k - DIAGS + 1))
                    nc.scalar.activation(diag[:, k % DIAGS, :], ident, ACT.Copy, scale=wts[:, half, k:k + 1])\
                        .then_inc(sem("diag_ready"), 1)

            act.wait_ge(sem("setup_loaded"), 16 * setup_loads)
            step(nc.scalar.activation(c_tok, c_tok, ACT.Silu), "c_silu")
            for k in range(KD):
                evacuate(("x", k), xT[:, k, :], TOK)
            for h in range(A_HEADS):
                evacuate(("rel", h), rel_rows[:, h, :], SKEW)
            def ada(l, i):
                rows = ada_rows if l or i < 2 else ada_rows_mid
                for m in (2 * i, 2 * i + 1):
                    if i:
                        act.wait_ge(product_ready, nth["adaT", l, i - 1] + 1)
                    evacuate(("ada", l, m), rows[:, m % 2, :], P)

            for l in range(DEPTH):
                if l:
                    act.wait_ge(*drain_of(("pt", l - 1, TILES[-1], 1)))
                squares()
                if l == 0:
                    for i in range(2):
                        ada(0, i)
                root(("ss1", l), rstd[:, :], D)
                modulate(l, 0)
                for m in PROJ_ORDER[:-4]:
                    key = ("proj", l, m)
                    if m == "ig":
                        continue
                    if m == "fg":
                        act.wait_ge(sem("gate_abs_ready"), l + 1)
                        step(nc.scalar.activation(row["M"], row["M"], ACT.Exp, scale=-1.0))
                        step(nc.scalar.activation(row["M"], row["M"], ACT.Ln, bias=1.0), "gate_log_ready")
                        continue
                    if 6 <= m < 14:
                        k = m - 6
                        b = product(act, key)
                        act.wait_ge(sem("cin_padded"), l + 1)
                        step(nc.scalar.activation(cin_p[:, k, 3:], b[:, ST], ACT.Copy))
                        step(nc.scalar.activation(cin_s[:, k, :, 3:], by_sample(b[:, SB]), ACT.Copy), A)
                    else:
                        m = m if m < 6 else m - 8
                        evacuate(key, region1[:, m, :], TOK)
                for t in range(3):
                    n = P if t < 2 else NS
                    evacuate(("kvtok", l, t), kvt[0:n, t, :], 2 * P, n)
                for j in range(2):
                    evacuate(("kct", l, j), kcT[:, 4 * j:4 * j + 4, :].rearrange("p b c -> p (b c)"), 512)
                act.wait_ge(sem("conv_done"), (l + 1) * KD)
                for j in range(2):
                    step(nc.scalar.activation(qks[:, 4 * j:4 * j + 4, :], qks[:, 4 * j:4 * j + 4, :], ACT.Silu), "silu_done")
                act.wait_ge(sem("rows_wanted"), l + 1)
                for r, s in (("e", -1.0), ("wl", 1.0), ("aw", 1.0)):
                    step(nc.scalar.activation(row[r], row[r], ACT.Exp, scale=s), "rows_done")
                softmax_exp(l, 0, S0, None, P)
                softmax_exp(l, 1, S1, None, 2 * P)
                for n in range(A_KV):
                    evacuate(("ssT", l, n), sT[:, n, :], P)
                softmax_exp(l, 2, SS, None, 160)
                for m in PROJ_ORDER[-4:]:
                    evacuate(("proj", l, m), region1[:, m - 8, :], TOK)
                if l == 0:
                    ada(0, 2)
                for t in range(3):
                    n = P if t < 2 else NS
                    evacuate(("ktok", l, t), kt[0:n, t, :], 512, n)
                for t in range(3):
                    n = P if t < 2 else NS
                    evacuate(("vtok", l, t), vt[0:n, t, :], 512, n)
                for h in range(MH):
                    b = product(act, ("bM", l, h))
                    act.wait_ge(sem("cols_ready"), l + 1)
                    step(nc.scalar.activation(WT[:, h, 0:256], b[:, 0:256], ACT.Exp, bias=cols[:, 0, h:h + 1], scale=-1.0))
                    step(nc.scalar.activation(WT[:, h, 256:384], b[:, 256:384], ACT.Exp, bias=cols[:, 1, h:h + 1], scale=-1.0))
                    step(nc.scalar.activation(WT[0:NS, h, 384:416], b[0:NS, 384:416], ACT.Exp,
                                              bias=cols[0:NS, 2, h:h + 1], scale=-1.0), A)
                    evacuate(("bE", l, h), eh[:, h, :], TOK)
                if l == 0:
                    ada(0, 3)
                for t in range(2):
                    for j in range(2 * (t + 1)):
                        if t == 0:
                            b = product(act, ("pT", l, t, j))
                            step(nc.scalar.activation(PT[:, 4 * j:4 * j + 4, 0, :], b.rearrange("p (h q) -> p h q", h=4), ACT.Copy), A)
                        else:
                            b = product(act, ("pT", l, t, j))
                            step(nc.scalar.activation(PT[:, 2 * j:2 * j + 2, :, :].rearrange("p h b q -> p (h b q)"), b, ACT.Copy), A)
                    b = product(act, ("o", l, t))
                    step(nc.scalar.activation(mixT[:, 0:4, t * P:(t + 1) * P], b.rearrange("p (j q) -> p j q", j=4), ACT.Copy), A)
                for n in range(A_KV):
                    b = product(act, ("spT", l, n))
                    step(nc.scalar.activation(PTs[:, n, 0, :], b[:, 0:P], ACT.Copy))
                    step(nc.scalar.activation(PTs[0:NS, n, 1, :], b[0:NS, P:2 * P], ACT.Copy), A)
                b = product(act, ("o", l, 2))
                step(nc.scalar.activation(mixT[:, 0:4, SB], b[:, 0:P].rearrange("p (j q) -> p j q", j=4), ACT.Copy), A)
                for h in range(MH):
                    if l == 0 and h in ADA_AT_HEAD:
                        ada(0, ADA_AT_HEAD[h])
                    for j in range(2):
                        b = product(act, ("CT", l, h, j))
                        step(nc.scalar.activation(CT[:, h % 2, 4 * j:4 * j + 4, :].rearrange("p b k -> p (b k)"), b, ACT.Copy), A)
                    act.wait_ge(*drain_of(("num", l, h)))
                    step(nc.scalar.activation(WT[:, h, 0:TOK], eh[:, h, :], ACT.Square), "hm_squares_ready")
                step(nc.scalar.activation(region1[:, OM:OM + 4, :], region1[:, OM:OM + 4, :], ACT.Sigmoid), "sigmoid_done")
                for h in range(MH):
                    root(("hss", l, h), WT[:, h, 0:TOK], MD)
                evacuate(("Cp", l), PTs_flat, 512)
                evacuate(("np", l), kcT_flat[0:1, 0:512], 512, 1)
                evacuate(("nnr", l), nrow, P, NS)
                for j in range(2):
                    evacuate(("cvr", l, j), pe_tok[0:27, 512 * j:512 * j + 512], 512, 27)
                for j in range(4):
                    evacuate(("ky", l, j), keyT[:, 4 * j:4 * j + 4, :].rearrange("p m k -> p (m k)"), 512)
                act.wait_ge(*drain_of(("out", l, KD - 1)))
                squares(SB)
                root(("ss2", l, "S"), rstd[:, SB], D)
                squares(ST)
                root(("ss2", l, "T"), rstd[:, ST], D)
                for m in QUERY_TILES:
                    evacuate(("qpS", l, m), query_rows[:, m, :], P)
                b = product(act, ("qST", l))
                step(nc.scalar.activation(region1[:, :, SB], b.rearrange("p (m t) -> p m t", m=16), ACT.Copy), A)
                modulate(l, 1)
                for j in range(2):
                    evacuate(("h2", l, 2, j), h2tok[:, 2, 512 * j:512 * j + 512], 512)
                def queries(tile):
                    for j in range(4):
                        evacuate(("qp", l, 4 * tile + j), region1[:, 4 * tile + j, ST], SEQ)
                        if tile == 0 and j == 1:
                            gate_exp(l, 1, slice(0, 2))
                for tile in range(3):
                    queries(tile)
                for g in TILES:
                    base = first_slot[l, g] // K
                    if g == "S":
                        expert_unit(base, 0, l == 0)
                        gate_exp(l, 2, slice(0, 4))
                        for t in (0, 1):
                            for j in range(2):
                                evacuate(("h2", l, t, j), h2tok[:, t, 512 * j:512 * j + 512], 512)
                        queries(3)
                        expert_unit(base + 1, 1, l == 0)
                    elif g == "T0":
                        for n in range(8):
                            expert_unit(base + n, n % 2, False)
                            if n == 0:
                                gate_exp(l, 3, slice(4, 8))
                            if n == 5:
                                gate_exp(l, 4, slice(0, 8))
                            if 1 <= n < 7 and l + 1 < DEPTH:
                                ada(l + 1, n - 1)
                    else:
                        with act.Fori(0, UNITS[g] // 2) as i:
                            for half in range(2):
                                expert_unit(base + 2 * i + half, half, False)
                    act.wait_ge(sem("v_row_used"), first_slot[l, g] + UNITS[g] * K)
                    step(nc.scalar.activation(pe_tok[:, :], acc[:, :, :].rearrange("p c d -> p (c d)"), ACT.Copy), "experts_summed")
            act.wait_ge(*drain_of(("pt", DEPTH - 1, TILES[-1], 1)))
            squares()
            root(("ssf",), rstd[:, :], D)
            act.wait_ge(sem("xn_ready"), 2 * DEPTH + 1)
            for k in range(KD):
                step(nc.scalar.activation(hT[:, k, :], qks[:, k, :], ACT.Copy, scale=prm[:, 0, R_NFIN + k:R_NFIN + k + 1]), "y_ready")
            for t in range(3):
                n = P if t < 2 else NS
                for j in range(2):
                    evacuate(("y", t, j), x_tok[0:n, t, 512 * j:512 * j + 512], 512, n)

        @block.tensor
        def _(pe):
            mm, tr = nc.tensor.matmul, nc.tensor.transpose

            def done(ins):
                ins.then_inc(product_ready, 1)

            def transposes(key, parts):
                b = claim(pe, key)
                for c0, src in parts:
                    n, w = src.shape[0], src.shape[1]
                    ins = tr(b[0:w, c0:c0 + n], src, ident[0:n, 0:n])
                done(ins)

            def sum_squares(key, src, chunks):
                b = claim(pe, key)[:, 0:src.shape[-1]]
                for k in range(chunks):
                    ins = mm(b, ones, src[:, k, :] if chunks > 1 else src, start=k == 0, stop=k == chunks - 1)
                done(ins)

            used = 0

            def weight_tile():
                nonlocal used
                pe.wait_ge(sem(f"weights_loaded_{used % WSLOTS}"), 16 * (used // WSLOTS + 1))
                used += 1
                return wring[:, (used - 1) % WSLOTS, :, :]

            def project(key, w, c, src, n=P):
                b = claim(pe, key)
                for k in range(KD):
                    ins = mm(b[0:n, 0:src.shape[-1]], w[:, k, c:c + n], src[:, k, :], start=k == 0, stop=k == KD - 1)
                done(ins)

            def release(key):
                pe.wait_ge(product_ready, nth[key] + 1)
                pe.sem_inc(sem("weights_used"), 1)

            def spread_columns(b, rows, w):
                for k in range(KD):
                    for j in range(4):
                        ins = mm(b[NS * j:NS * j + NS, 0:P], rows[:, k, :], w[:, k, P * j:P * j + P],
                                 start=k == 0, stop=k == KD - 1, skip_group_check=True)
                done(ins)

            def ada(l, i):
                for m in (2 * i, 2 * i + 1):
                    w = weight_tile()
                    b = claim(pe, ("ada", l, m))
                    spread_columns(b, cT[:, :, :], w)
                    release(("ada", l, m))
                rows = ada_rows if l or i < 2 else ada_rows_mid
                pe.wait_ge(*drain_of(("ada", l, 2 * i + 1)))
                transposes(("adaT", l, i), [(P * r, rows[:, r, :]) for r in range(2)])

            pe.wait_ge(sem("setup_loaded"), 16 * setup_loads)
            for l in range(DEPTH):
                transposes(("params", l), [(0, prm_rows[:, l, :])])
            for k in range(KD):
                transposes(("x", k), [(P * t, x_tok[0:P if t < 2 else NS, t, P * k:P * k + P]) for t in range(3)])
            pe.wait_ge(sem("c_silu"), 1)
            transposes(("c",), [(NC * k, c_tok[:, P * k:P * k + P]) for k in range(KD)])
            pe.wait_ge(sem("rel_spread"), A_HEADS)
            for h in range(A_HEADS):
                b = claim(pe, ("rel", h))
                done(mm(b[:, 0:SKEW], relb[:, h, :], hot, start=True, stop=True))

            pe.wait_ge(*drain_of(("c",)))
            for l in range(DEPTH):
                if l == 0:
                    for i in range(2):
                        ada(0, i)
                pe.wait_ge(sem("conv_state_loaded"), 16 * (l + 1))
                transposes(("cvs", l), [(24 * k, pe_tok[0:24, P * k:P * k + P]) for k in range(KD)])
                pe.wait_ge(sem("squares_ready"), 3 * l + 1)
                sum_squares(("ss1", l), hT, KD)
                pe.wait_ge(sem("h_ready"), KD * (2 * l + 1))
                pe.wait_ge(sem("h_sample_ready"), 2 * l + 1)
                def project_tile(tile):
                    w = weight_tile()
                    for j in range(4 if tile < 5 else 2):
                        project(("proj", l, 4 * tile + j), w, P * j, hT)
                    if tile == 5:
                        project(("proj", l, "ig"), w, 2 * P, hT, MH)
                        project(("proj", l, "fg"), w, 2 * P + MH, hT, MH)
                    release(("proj", l, "fg" if tile == 5 else 4 * tile + 3))

                for tile in PROJ_TILES[:-1]:
                    project_tile(tile)
                pe.wait_ge(*drain_of(("proj", l, KA + 1)))
                tiles = [(slice(P * t, min(P * t + P, TOK)), t) for t in range(3)]
                for tok, t in tiles:
                    transposes(("kvtok", l, t), [(P * j, region1[:, KA + j, tok]) for j in range(2)])
                pe.wait_ge(sem("kc_loaded"), 16 * (l + 1))
                for j in range(2):
                    transposes(("kct", l, j), [(P * b, kc[:, 4 * j + b, :]) for b in range(4)])
                pe.wait_ge(sem("k_doubled"), 64 * (l + 1))
                for t in range(2):
                    for j in range(4):
                        b = claim(pe, ("sc", l, t, j))
                        h0 = j // 2 * GROUP + j % 2
                        for i, h in enumerate((h0, h0 + 2)):
                            half = slice(h % 2 * DH, (h % 2 + 1) * DH)
                            c0 = P if t == 0 else 0
                            ins = mm(b[:, 256 * i + c0:256 * i + 256], region1[half, h // 2, P * t:P * t + P],
                                     kdup[half, h // GROUP, P * (t - 1) + c0:P * (t + 1)], start=True, stop=True)
                        done(ins)
                pe.wait_ge(sem("q_moved"), 128 * (l + 1))
                for n in range(A_KV):
                    half = slice(n * DH, (n + 1) * DH)
                    pe.wait_ge(*drain_of(("kct", l, 1)))
                    bk = claim(pe, ("ssT", l, n))
                    out = bk[:, 0:P].rearrange("p (g b s) -> p g b s", g=GROUP, b=DEC_B)
                    for b in range(DEC_B):
                        ins = mm(out[:, :, b, :], kcT[half, b, :], qd[half, :, DEC_S * b:DEC_S * b + DEC_S], start=True, stop=True)
                    done(ins)
                for n in range(A_KV):
                    half = slice(n * DH, (n + 1) * DH)
                    pe.wait_ge(*drain_of(("ssT", l, n)))
                    b = claim(pe, ("ss", l, n))
                    tr(b[:, 0:P], sT[:, n, :], ident)
                    done(mm(b[:, P:P + NS], qd[half, :, :].rearrange("p g t -> p (g t)"), kdup[half, n, SB], start=True, stop=True))
                project_tile(PROJ_TILES[-1])
                if l == 0:
                    ada(0, 2)
                pe.wait_ge(sem("k_scaled"), l + 1)
                for tok, t in tiles:
                    transposes(("ktok", l, t), [(P * h, qks[:, 4 + h, tok]) for h in range(MH)])
                pe.wait_ge(*drain_of(("proj", l, 17)))
                for tok, t in tiles:
                    transposes(("vtok", l, t), [(P * h, region1[:, VM + h, tok]) for h in range(MH)])
                pe.wait_ge(sem("rows_done"), 3 * (l + 1))
                b = claim(pe, ("cols", l))
                for tok, t in tiles:
                    w = P if t < 2 else NS
                    for j, r in enumerate(("a", "wl")):
                        ins = tr(b[0:w, 8 * t + 4 * j:8 * t + 4 * j + 4], row[r][:, tok], ident[0:MH, 0:MH])
                done(ins)
                pe.wait_ge(sem("n_loaded"), 16 * (l + 1))
                transposes(("nT", l), [(0, nrow)])

                def select(h):
                    return ident[0:MH, h:h + 1].broadcast_to([MH, P])

                b = claim(pe, ("bA", l))
                for h in range(MH):
                    ins = mm(b[:, NS * h:NS * h + NS], select(h), row["aw"], start=True, stop=True)
                done(ins)
                for h in range(MH):
                    b = claim(pe, ("bM", l, h))
                    mm(b[:, 0:256], select(h), row["M"][:, 0:256], start=True, stop=False, skip_group_check=True)
                    mm(b[:, 256:384], select(h), row["M"][:, 128:256], start=False, stop=False, skip_group_check=True)
                    mm(b[:, 384:416], select(h), row["M"][:, 256:288], start=False, stop=False, skip_group_check=True)
                    mm(b[:, 0:128], ident, cst[:, C_CAUSAL:C_CAUSAL + P], start=False, stop=False, skip_group_check=True)
                    mm(b[:, 256:384], ident, cst[:, C_CAUSAL:C_CAUSAL + P], start=False, stop=False, skip_group_check=True)
                    done(mm(b[0:NS, 384:416], ident[0:NS, 0:NS], cst[0:NS, C_CAUSALS:C_CAUSALS + NS], start=False, stop=True, skip_group_check=True))
                    b = claim(pe, ("bE", l, h))
                    done(mm(b[:, 0:TOK], select(h), row["e"], start=True, stop=True))
                    b = claim(pe, ("qk", l, h))
                    mm(b[:, 0:256], qks[:, 4 + h, 0:128], qks[:, h, 0:256], start=True, stop=True)
                    mm(b[:, 256:384], qks[:, 4 + h, 128:256], qks[:, h, 128:256], start=True, stop=True)
                    done(mm(b[0:NS, 384:416], qks[:, 4 + h, SB], qks[:, h, SB], start=True, stop=True))
                if l == 0:
                    ada(0, 3)
                for t in range(2):
                    pe.wait_ge(sem("probs_ready"), 3 * l + t + 1)
                    for j in range(2 * (t + 1)):
                        if t == 0:
                            transposes(("pT", l, t, j), [(P * i, S0[:, 4 * j + i, :]) for i in range(4)])
                        else:
                            transposes(("pT", l, t, j), [(P * (2 * i + kb), S1[:, 2 * j + i, P * kb:P * kb + P])
                                                         for i in range(2) for kb in range(2)])
                    pe.wait_ge(*drain_of(("pT", l, t, 2 * t + 1)))
                    b = claim(pe, ("o", l, t))
                    for h in range(A_HEADS):
                        half, v0 = slice(h % 2 * DH, (h % 2 + 1) * DH), P + h // GROUP * DH
                        for kb in range(t + 1):
                            ins = mm(b[half, P * (h // 2):P * (h // 2) + P], kvt[:, kb, v0:v0 + DH], PT[:, h, kb, :],
                                     start=kb == 0, stop=kb == t)
                    done(ins)
                pe.wait_ge(sem("probs_ready"), 3 * l + 3)
                for n in range(A_KV):
                    transposes(("spT", l, n), [(0, SS[:, n, 0:P]), (P, SS[:, n, P:P + NS])])
                pe.wait_ge(*drain_of(("spT", l, 1)))
                pe.wait_ge(sem("vc_loaded"), 16 * (l + 1))
                bk = claim(pe, ("o", l, 2))
                out = bk[:, 0:P].rearrange("p (j t) -> p j t", j=4)
                for n in range(A_KV):
                    v0 = n * DH
                    for odd in range(2):
                        half = slice(odd * DH, (odd + 1) * DH)
                        to = out[half, 2 * n:2 * n + 2, :]
                        new = PTs[0:NS, n, 1, :].rearrange("p (g t) -> p g t", g=GROUP)[:, odd::2, :]
                        old = PTs[:, n, 0, :].rearrange("p (g t) -> p g t", g=GROUP)[:, odd::2, :]
                        mm(to, kvt[0:NS, 2, P + v0:P + v0 + DH], new, start=True, stop=False, skip_group_check=True)
                        for b in range(DEC_B):
                            t = slice(DEC_S * b, DEC_S * b + DEC_S)
                            ins = mm(to[:, :, t], vc[:, b, v0:v0 + DH], old[:, :, t], start=False, stop=b == DEC_B - 1, skip_group_check=True)
                done(ins)
                pe.wait_ge(*drain_of(("vtok", l, 2)))
                pe.wait_ge(*drain_of(("ktok", l, 2)))
                pe.wait_ge(*drain_of(("qk", l, MH - 1)))
                pe.wait_ge(sem("q_weighted"), l + 1)
                for h in range(MH):
                    if l == 0 and h in ADA_AT_HEAD:
                        ada(0, ADA_AT_HEAD[h])
                    pe.wait_ge(sem(f"C_loaded_{h % 2}"), 16 * (2 * l + h // 2 + 1))
                    for j in range(2):
                        transposes(("CT", l, h, j), [(P * b, C_sb[:, h % 2, 4 * j + b, :]) for b in range(4)])
                    b = claim(pe, ("den", l, h))
                    mm(b[:, 0:256], ones, WT[:, h, 0:256], start=True, stop=False, skip_group_check=True)
                    mm(b[:, 128:256], ones, WT[:, h, 256:384], start=False, stop=False, skip_group_check=True)
                    mm(b[:, SB], ones[0:NS, :], WT[0:NS, h, 384:416], start=False, stop=False, skip_group_check=True)
                    done(mm(b[:, SB], ones, nqa[:, h, :], start=False, stop=True, skip_group_check=True))
                    v = slice(P * h, P * h + P)
                    pe.wait_ge(*drain_of(("CT", l, h, 1)))
                    b = claim(pe, ("num", l, h))
                    mm(b[:, 0:256], vt[:, 0, v], WT[:, h, 0:256], start=True, stop=False, skip_group_check=True)
                    mm(b[:, 128:256], vt[:, 1, v], WT[:, h, 256:384], start=False, stop=False, skip_group_check=True)
                    mm(b[:, SB], vt[0:NS, 2, v], WT[0:NS, h, 384:416], start=False, stop=False, skip_group_check=True)
                    for s in range(DEC_B):
                        t = slice(DEC_S * s, DEC_S * s + DEC_S)
                        ins = mm(b[:, 256 + DEC_S * s:256 + DEC_S * (s + 1)], CT[:, h % 2, s, :], qa[:, h, t],
                                 start=False, stop=s == DEC_B - 1, skip_group_check=True)
                    done(ins)
                    pe.wait_ge(sem("weighted_k_ready"), MH * l + h + 1)
                    for j in range(2):
                        b = claim(pe, ("Cs", l, h, j))
                        done(mm(b, vt[0:NS, 2, v], wk[:, 4 * j:4 * j + 4, :].rearrange("p b k -> p (b k)"), start=True, stop=True))
                for h in range(MH):
                    pe.wait_ge(sem("hm_squares_ready"), MH * l + h + 1)
                    sum_squares(("hss", l, h), WT[:, h, 0:TOK], 1)
                pe.wait_ge(sem("weighted_v_ready"), l + 1)
                b = claim(pe, ("Cp", l))
                for h in range(MH):
                    for t in range(2):
                        ins = mm(b[:, P * h:P * h + P], wv[:, t, h, :], kt[:, t, P * h:P * h + P], start=t == 0, stop=t == 1)
                done(ins)
                b = claim(pe, ("np", l))
                for h in range(MH):
                    for t in range(2):
                        ins = mm(b[0:1, P * h:P * h + P], cols[:, t, 4 + h:5 + h], kt[:, t, P * h:P * h + P], start=t == 0, stop=t == 1)
                done(ins)
                b = claim(pe, ("nn", l))
                for h in range(MH):
                    ins = mm(b[:, DEC_B * h:DEC_B * h + DEC_B], kt[0:NS, 2, P * h:P * h + P], WB[:, h, :], start=True, stop=True)
                done(ins)
                pe.wait_ge(*drain_of(("nn", l)))
                transposes(("nnr", l), [(0, nnT)])
                pe.wait_ge(sem("conv_rows_ready"), l + 1)
                for j in range(2):
                    transposes(("cvr", l, j), [(P * k, cvo[:, 4 * j + k, :]) for k in range(4)])
                pe.wait_ge(sem("keys_loaded"), 16 * (l + 1))
                for j in range(4):
                    transposes(("ky", l, j), [(P * i, keys_raw[:, 4 * j + i, :]) for i in range(4)])
                pe.wait_ge(sem("mlstm_out_ready"), MH * (l + 1))
                for tile in range(2):
                    w = weight_tile()
                    for j in range(4):
                        project(("out", l, 4 * tile + j), w, P * j, mixT)
                    release(("out", l, 4 * tile + 3))
                pe.wait_ge(sem("squares_ready"), 3 * l + 2)
                sum_squares(("ss2", l, "S"), hT[:, :, SB], KD)
                pe.wait_ge(sem("squares_ready"), 3 * l + 3)
                sum_squares(("ss2", l, "T"), hT[:, :, ST], KD)
                pe.wait_ge(sem("h_sample_ready"), 2 * l + 2)
                pe.wait_ge(sem("query_weights_loaded"), 32 * (l + 1))
                query_weights = {m: query_w[:, i] for i, m in enumerate(QUERY_TILES[:2])}
                for tile in QUERY_TILES:
                    if tile not in query_weights:
                        query_weights[tile] = weight_tile()
                    spread_columns(claim(pe, ("qpS", l, tile)), hT[:, :, SB], query_weights[tile])
                pe.wait_ge(*drain_of(("qpS", l, QUERY_TILES[-1])))
                transposes(("qST", l), [(P * m, query_rows[:, m, :]) for m in range(4)])
                pe.wait_ge(*drain_of(("qST", l)))
                b = claim(pe, ("rs", l, "S", 0))
                for q in range(4):
                    for i in range(4):
                        m = 4 * q + i
                        ins = mm(b[NS * q:NS * q + NS, P * i:P * i + P], region1[:, m, SB], keyT[:, m, :], start=True, stop=True)
                done(ins)

                pe.wait_ge(sem("h_repeated"), l + 1)
                for j in range(2):
                    transposes(("h2", l, 2, j), [(P * k, hS4[:, 4 * j + k, :, :].rearrange("p q t -> p (q t)")) for k in range(4)])

                def key_scores(g, quads):
                    for j in quads:
                        b = claim(pe, ("rs", l, g, j))
                        for i in range(4):
                            m = 4 * j + i
                            ins = mm(b[:, P * i:P * i + P], region1[:, m, COL[g]:COL[g] + P], keyT[:, m, :], start=True, stop=True)
                        done(ins)

                def queries(tile):
                    for j in range(4):
                        project(("qp", l, 4 * tile + j), query_weights[tile], P * j, hT[:, :, ST])
                    if tile in QUERY_TILES[2:]:
                        release(("qp", l, 4 * tile + 3))

                def weighted_rows(n, half):
                    for k in range(K):
                        pe.wait_ge(sem("diag_ready"), n * K + (k + 1))
                        pe.wait_ge(v_loaded[k % RV], n * (16 * K // RV) + 16 * (k // RV + 1))
                        for c in range(2):
                            ins = mm(acc[:, c, :], diag[:, k % DIAGS, :], v_ring[:, k % RV, 512 * c:512 * c + 512],
                                     start=False, stop=False, skip_group_check=True)
                        ins.then_inc(sem("v_row_used"), 1)

                pe.wait_ge(sem("h_ready"), KD * (2 * l + 2))
                for tile in range(3):
                    queries(tile)
                pe.wait_ge(*drain_of(("qp", l, 7)))
                key_scores("T0", [0, 1])
                for g in TILES:
                    base = first_slot[l, g] // K
                    if (l, g) != (0, TILES[0]):
                        pe.wait_ge(sem("experts_summed"), 3 * l + TILES.index(g))
                    for c in range(2):
                        for half in range(2):
                            mm(acc[:, c, 256 * half:256 * half + 256], zeros[:, :], cst[:, 0:256],
                               start=True, stop=False, skip_group_check=True)
                    if g == "S":
                        weighted_rows(base, 0)
                        for t in (0, 1):
                            for j in range(2):
                                transposes(("h2", l, t, j), [(P * k, hT[:, 4 * j + k, P * t:P * t + P]) for k in range(4)])
                        pe.wait_ge(*drain_of(("qp", l, 11)))
                        key_scores("T0", [2])
                        queries(3)
                        weighted_rows(base + 1, 1)
                    elif g == "T0":
                        pe.wait_ge(*drain_of(("qp", l, 15)))
                        key_scores("T0", [3])
                        for n in range(8):
                            weighted_rows(base + n, n % 2)
                            if n < 4:
                                key_scores("T1", [n])
                            if 1 <= n < 7 and l + 1 < DEPTH:
                                ada(l + 1, n - 1)
                    else:
                        with pe.Fori(0, UNITS[g] // 2) as i:
                            for half in range(2):
                                weighted_rows(base + 2 * i + half, half)
                    pe.wait_ge(sem("experts_summed"), 3 * l + TILES.index(g) + 1)
                    for j in range(2):
                        b = claim(pe, ("pt", l, g, j))
                        for k in range(4):
                            src = pe_tok[:, 512 * j + P * k:512 * j + P * k + P]
                            if g == "S":
                                ins = mm(b[:, NS * k:NS * k + NS], src, cst[:, C_SUM:C_SUM + NS], start=True, stop=True)
                            else:
                                ins = tr(b[:, P * k:P * k + P], src, ident)
                        done(ins)
            pe.wait_ge(sem("squares_ready"), 3 * DEPTH + 1)
            sum_squares(("ssf",), hT, KD)
            pe.wait_ge(sem("y_ready"), KD)
            for t in range(3):
                for j in range(2):
                    n = P if t < 2 else NS
                    transposes(("y", t, j), [(P * k, hT[:, 4 * j + k, P * t:P * t + n]) for k in range(4)])

        @block.vector
        def _(dve):
            step = Steps(dve, "dve_step")
            V = drained["V"]
            tt, ts, stt = nc.vector.tensor_tensor, nc.vector.tensor_scalar, nc.vector.scalar_tensor_tensor
            copy, reduce = nc.vector.tensor_copy, nc.vector.tensor_reduce

            def normalise(key, cols):
                dve.wait_ge(*drain_of(key))
                step(nc.vector.reciprocal(rstd[:, cols], rstd[:, cols]))
                return tt(qks[:, :, cols], xT[:, :, cols], bc(rstd[:, cols], 1, [P, KD, cols.stop - cols.start]), ALU.mult)

            def modulate_samples(w):
                hs, xs = by_sample(hT[:, :, SB]), by_sample(qks[:, :, SB])
                full = [P, KD, DEC_B, DEC_S]
                step(tt(hs, xs, bc(modA[:, w, :, 1:NC], 3, full), ALU.mult))
                step(tt(hs, hs, bc(modT[:, 24 * w:24 * w + KD, 1:NC], 3, full), ALU.add), "h_sample_ready")

            def scales(w, r):
                step(stt(modA[:, w], modT[:, 24 * w + KD:24 * w + 2 * KD, :], 1.0,
                         bc(prm[:, l, r:r + KD], 2, [P, KD, NC]), ALU.add, ALU.mult))

            def gated_add(modT, b, k0, n, gate0):
                full = [P, n, DEC_B, DEC_S]
                t = tmp[:, 0:n * NS].rearrange("p (k b s) -> p k b s", k=n, b=DEC_B)
                xs = by_sample(xT[:, k0:k0 + n, SB])
                step(tt(t, b.rearrange("p (k b s) -> p k b s", k=n, b=DEC_B), bc(modT[:, gate0 + k0:gate0 + k0 + n, 1:NC], 3, full), ALU.mult))
                step(tt(xs, xs, t, ALU.add), V)

            def softmax_max(i, S, sink):
                nh = S.shape[1]
                st = stat[i][:, :, 0:nh]
                step(reduce(st[:, 0, :], S, AX, ALU.max))
                step(tt(st[:, 0, :], st[:, 0, :], sink, ALU.max))
                step(ts(st[:, 1, :], st[:, 0, :], -1.0, None, ALU.mult))
                step(tt(st[:, 2, :], sink, st[:, 1, :], ALU.add), "exp_wanted")

            def softmax_norm(l, i, S):
                nh = S.shape[1]
                st = stat[i][:, :, 0:nh]
                dve.wait_ge(sem("exp_done"), 3 * l + i + 1)
                step(tt(st[:, 4, :], st[:, 3, :], st[:, 2, :], ALU.add))
                step(nc.vector.reciprocal(st[:, 4, :], st[:, 4, :]))
                step(tt(S, S, bc(st[:, 4, :], 2, list(S.shape)), ALU.mult), "probs_ready")

            def top16(vals, idx, src, width):
                r = rep[:, 0:width]
                step(nc.vector.max(vals[:, 0:8], src))
                step(nc.vector.max_index(idx[:, 0:8], vals[:, 0:8], src))
                step(nc.vector.match_replace(r, vals[:, 0:8], src, -3e38))
                step(nc.vector.max(vals[:, 8:16], r))
                return nc.vector.max_index(idx[:, 8:16], vals[:, 8:16], r)

            def route_heads(l, g, j):
                b = product(dve, ("rs", l, g, j))
                for m in range(4):
                    h, c = 2 * j + m // 2, m % 2
                    step(top16(s_top[:, h, c, :], i_top[:, h, c, :], b[:, P * m:P * m + P], P), V if m == 3 else None)
                if g == "S":
                    dve.wait_ge(*drain_of(("h2", l, 2, 1)))
                for h in (2 * j, 2 * j + 1):
                    full = [P, TOPK, TOPK]
                    step(tt(cand[:, h, :].rearrange("p (i j) -> p i j", i=TOPK), bc(s_top[:, h, 0, :], 2, full),
                            bc(s_top[:, h, 1, :], 1, full), ALU.add))
                    step(top16(best[:, h, :], pos[:, h, :], cand[:, h, :], TOPK * TOPK))

            def center_gates(heads):
                nh = heads.stop - heads.start
                bst, mx = best[:, heads, :], rep[:, 0:nh]
                step(copy(mx, bst[:, :, 0]))
                step(tt(bst, bst, bc(mx, 2, [P, nh, TOPK]), ALU.subtract), "gate_exp_wanted")

            def route_gates(l, g, routed, heads):
                nh = heads.stop - heads.start
                slots = slice(heads.start * TOPK, heads.stop * TOPK)
                gates = g_all[:, TI[g], slots].rearrange("p (h k) -> p h k", h=nh)
                bst, mx = best[:, heads, :], rep[:, 0:nh]
                pi = pij[:, :, heads, :]
                pu = pi.bitcast(U32)
                step(ts(pu[:, 0], pos[:, heads, :], 4, None, ALU.logical_shift_right))
                step(ts(pu[:, 1], pos[:, heads, :], 15, None, ALU.bitwise_and))
                for c in range(2):
                    step(copy(pi[:, c], pu[:, c]))
                step(copy(i_topf[:, heads], i_top[:, heads]))
                full = [P, nh, TOPK, TOPK]
                hit = onehot[:, heads]
                iota = cst[:, C_IOTA:C_IOTA + TOPK].unsqueeze(1).unsqueeze(1).broadcast_to(full)
                for c in range(2):
                    step(tt(hit, iota, bc(pi[:, c], 3, full), ALU.is_equal))
                    step(tt(hit, hit, bc(i_topf[:, heads, c, :], 2, full), ALU.mult))
                    step(reduce(pi[:, c], hit, AX, ALU.add))
                step(stt(pi[:, 0], pi[:, 0], float(N_KEYS), pi[:, 1], ALU.mult, ALU.add))
                dve.wait_ge(sem("gate_exp_done"), 4 * l + routed)
                step(reduce(mx, bst, AX, ALU.add))
                step(nc.vector.reciprocal(mx, mx))
                step(tt(gates, bst, bc(mx, 2, [P, nh, TOPK]), ALU.mult))
                step(ts(idx_all[:, TI[g], slots].rearrange("p (h k) -> p h k", h=nh), pi[:, 0],
                        float(l * N_EXPERTS), None, ALU.add), "idx_ready")

            def expert_unit(g, i, half, n):
                for k in range(K):
                    dve.wait_ge(u_loaded[k % RU], n * (16 * K // RU) + 16 * (k // RU + 1))
                    row_ = u_ring[:, k % RU, :]
                    nc.vector.tensor_tensor_reduce(out=row_, in0=row_, in1=h2tok[:, TI[g], :], scale=1.0, scalar=0.0,
                                                   op0=ALU.mult, op1=ALU.add, accum_out=dots[:, half, k:k + 1])\
                        .then_inc(sem("u_row_used"), 1)
                dve.wait_ge(sem("gelu_ready"), n + 1)
                tt(wts[:, half, :], gelus[:, half, :], g_all[:, TI[g], bass.ds(i * 2 * K + half * K, K)], ALU.mult)\
                    .then_inc(sem("expert_weights_ready"), 1)

            step(nc.vector.memset(eps_t[:, :], EPS))
            step(nc.vector.memset(zeros[:, :], 0.0))
            dve.wait_ge(sem("setup_loaded"), 16 * setup_loads)
            step(nc.vector.memset(relraw[32:33, :], -BIG))
            for h in range(A_HEADS):
                step(ts(relb[:, h, :], ones[0:33, :], relraw[:, h:h + 1], None, ALU.mult), "rel_spread")
            for l in range(DEPTH):
                step(copy(prm[:, l, :], product(dve, ("params", l))[:, 0:R_ROWS]), V)
            step(nc.vector.memset(cT[:, :, :], 0.0))
            step(copy(cT[:, :, 0:NC], product(dve, ("c",))[:, 0:KD * NC].rearrange("p (k c) -> p k c", k=KD)), V)
            def ada(l, i):
                b = product(dve, ("adaT", l, i))
                step(tt(modT_all[:, l % 2, 8 * i:8 * i + 8, :], b[:, 0:2 * P].rearrange("p (j c) -> p j c", j=8)[:, :, 0:NC],
                        bc(prm[:, l, R_BADA + 8 * i:R_BADA + 8 * i + 8], 2, [P, 8, NC]), ALU.add), V)

            def add_experts(l, g):
                modT = modT_all[:, l % 2]
                for j in range(2):
                    b = product(dve, ("pt", l, g, j))
                    if g == "S":
                        gated_add(modT, b[:, 0:4 * NS], 4 * j, 4, 40)
                    else:
                        for k in range(4):
                            m, c = 4 * j + k, slice(COL[g], COL[g] + P)
                            step(stt(xT[:, m, c], b[:, P * k:P * k + P], modT[:, 40 + m, 0:1], xT[:, m, c], ALU.mult, ALU.add),
                                 V if k == 3 else None)

            for l in range(DEPTH):
                modT = modT_all[:, l % 2]
                if l == 0:
                    for i in range(2):
                        ada(0, i)
                scales(0, R_NMIX)
                step(nc.vector.memset(cin_p[:, :, 0:3], 0.0))
                b = product(dve, ("cvs", l))
                step(copy(cin_s[:, :, :, 0:3], b[:, 0:192].rearrange("p (k b r) -> p k b r", k=KD, b=DEC_B)), V)
                step(nc.vector.memset(tmp[:, 0:1], 0.0), "cin_padded")
                step(normalise(("ss1", l), slice(0, TOK)), "xn_ready")
                modulate_samples(0)
                b = product(dve, ("proj", l, "ig"))
                if l == 0:
                    dve.wait_ge(sem("rel_stored"), 16)
                step(ts(row["ig"], b[0:MH, 0:TOK], gate_bias[:, l, 0:1], None, ALU.add), V)
                b = product(dve, ("proj", l, "fg"))
                step(ts(row["e"], b[0:MH, 0:TOK], gate_bias[:, l, 1:2], None, ALU.add), V)
                step(stt(row["M"], row["e"], -1.0, row["e"], ALU.mult, ALU.max), "gate_abs_ready")
                step(ts(row["b"], row["e"], 0.0, None, ALU.min))
                dve.wait_ge(sem("gate_log_ready"), l + 1)
                step(tt(row["wl"], row["b"], row["M"], ALU.subtract))
                s4 = {r: by_sample(row[r][:, SB]) for r in ("ig", "b", "a", "M", "e", "wl")}
                one = ones[0:MH, 0:1].broadcast_to([MH, SEQ])
                step(nc.vector.tensor_tensor_scan(row["b"][:, ST], one, row["wl"][:, ST], 0.0, ALU.mult, ALU.add))
                step(copy(s4["b"][:, :, 0], s4["wl"][:, :, 0]))
                for s in range(1, DEC_S):
                    step(tt(s4["b"][:, :, s], s4["b"][:, :, s - 1], s4["wl"][:, :, s], ALU.add))
                step(tt(row["a"], row["ig"], row["b"], ALU.subtract))
                step(nc.vector.tensor_tensor_scan(row["M"][:, ST], row["a"][:, ST], row["a"][:, ST], 0.0, ALU.max, ALU.max))
                dve.wait_ge(sem("m_loaded"), 16 * (l + 1))
                for s in range(DEC_S):
                    step(tt(s4["M"][:, :, s], s4["a"][:, :, s], m_in if s == 0 else s4["M"][:, :, s - 1], ALU.max))
                step(tt(row["e"], row["b"], row["M"], ALU.add))
                step(copy(m_out[:, 0:1], row["e"][:, SEQ - 1:SEQ]))
                step(copy(m_out[:, 1:NC], s4["e"][:, :, DEC_S - 1]), "m_out_ready")
                step(ts(row["wl"][:, ST], row["a"][:, ST], row["M"][:, SEQ - 1:SEQ], None, ALU.subtract))
                full = [MH, DEC_B, DEC_S]
                step(tt(s4["wl"], s4["a"], bc(s4["M"][:, :, DEC_S - 1], 2, full), ALU.subtract))
                step(tt(by_sample(row["aw"]), bc(m_in, 2, full), s4["M"], ALU.subtract), "rows_wanted")
                for k in range(KD):
                    dve.wait_ge(*drain_of(("proj", l, 6 + k)))
                    for i in range(CONV_W):
                        tap = prm[:, l, R_CONVW + KD * i + k:R_CONVW + KD * i + k + 1]
                        cb = prm[:, l, R_CONVB + k:R_CONVB + k + 1]
                        for dst, src in ((qks[:, k, ST], cin_p[:, k, i:i + SEQ]),
                                         (by_sample(qks[:, k, SB]), cin_s[:, k, :, i:i + DEC_S])):
                            last = i == CONV_W - 1 and dst.shape[-1] == DEC_S
                            step(ts(dst, src, tap, cb, ALU.mult, ALU.add) if i == 0 else
                                 stt(dst, src, tap, dst, ALU.mult, ALU.add), "conv_done" if last else None)
                step(copy(cvo[:, :, 0:3], cin_p[:, :, SEQ:SEQ + 3]))
                step(copy(cvo[:, :, 3:27].rearrange("p k (b r) -> p k b r", b=DEC_B), cin_s[:, :, :, DEC_S:DEC_S + 3]), "conv_rows_ready")
                if l == 0:
                    dve.wait_ge(sem("bias_loaded"), 16 * (1 + A_HEADS * (1 + DEC_B)))
                    step(tt(bias_s[:, :, WINDOW:], bias_s[:, :, WINDOW:],
                            bc(cst[:, C_BLOCKADD:C_BLOCKADD + NS], 1, [P, A_KV, NS]), ALU.add))
                for t, S in ((0, S0), (1, S1)):
                    lo = P if t == 0 else 0
                    for j in range(4):
                        b = product(dve, ("sc", l, t, j)).rearrange("p (h k) -> p h k", h=2)[:, :, lo:]
                        h0 = j // 2 * GROUP + j % 2
                        step(stt(S[:, h0:h0 + 3:2, :], b, DH ** -0.5, bias[:, h0:h0 + 3:2, lo:], ALU.mult, ALU.add), V)
                    softmax_max(t, S, sink_p[:, l, :])
                    if t == 0:
                        dve.wait_ge(sem("silu_done"), 2 * (l + 1))
                        step(ts(qks[:, 4:8, :], qks[:, 4:8, :], MD ** -0.5, None, ALU.mult), "k_scaled")
                softmax_norm(l, 0, S0)
                softmax_norm(l, 1, S1)
                for n in range(A_KV):
                    b = product(dve, ("ss", l, n))
                    step(stt(SS[:, n, :], b[:, 0:160], DH ** -0.5, bias_s[:, n, :], ALU.mult, ALU.add), V)
                softmax_max(2, SS, sink_s[:, l, :])
                if l == 0:
                    ada(0, 2)
                b = product(dve, ("cols", l))
                step(copy(cols[:, 0:2, :].rearrange("p t c -> p (t c)"), b[:, 0:16]))
                step(copy(cols[0:NS, 2, :], b[0:NS, 16:24]), V)
                step(nc.vector.memset(tmp[:, 0:1], 0.0), "cols_ready")
                full = [NS, MH, DEC_B]
                step(tt(WB, bc(cst[0:NS, C_BLOCK:C_BLOCK + DEC_B], 1, full), bc(cols[0:NS, 2, 4:8], 2, full), ALU.mult))
                step(copy(nT, product(dve, ("nT", l))[:, 0:NS]), V)
                step(copy(abc.rearrange("p h t -> p (h t)"), product(dve, ("bA", l))[:, 0:P]), V)
                step(tt(qa, qks[:, 0:4, SB], abc, ALU.mult))
                full = [P, MH, DEC_B, DEC_S]
                n_hb = nT.rearrange("p (b h) -> p h b", b=DEC_B)
                step(tt(by_sample(nqa), by_sample(qa), bc(n_hb, 3, full), ALU.mult), "q_weighted")
                softmax_norm(l, 2, SS)
                for h in range(MH):
                    b = product(dve, ("qk", l, h))
                    dve.wait_ge(*drain_of(("bM", l, h)))
                    step(tt(WT[:, h, 0:384], WT[:, h, 0:384], b[:, 0:384], ALU.mult))
                    step(tt(WT[0:NS, h, 384:416], WT[0:NS, h, 384:416], b[0:NS, 384:416], ALU.mult), V)
                if l == 0:
                    ada(0, 3)
                dve.wait_ge(*drain_of(("vtok", l, 2)))
                dve.wait_ge(product_ready, nth["pT", l, 1, 3] + 1)
                for t in range(2):
                    step(tt(wv[:, t], vt[:, t, :].rearrange("p (h v) -> p h v", h=MH), bc(cols[:, t, 4:8], 2, [P, MH, MD]), ALU.mult),
                         "weighted_v_ready" if t else None)
                al = [by_sample(abc[:, h, :])[:, :, DEC_S - 1] for h in range(MH)]
                for h in range(MH):
                    if l == 0 and h in ADA_AT_HEAD:
                        ada(0, ADA_AT_HEAD[h])
                    dve.wait_ge(*drain_of(("ktok", l, 2)))
                    if h:
                        dve.wait_ge(product_ready, nth["Cs", l, h - 1, 1] + 1)
                    full = [NS, DEC_B, MD]
                    step(tt(wk, bc(kt[0:NS, 2, P * h:P * h + P], 1, full), bc(WB[:, h, :], 2, full), ALU.mult), "weighted_k_ready")
                    b = product(dve, ("den", l, h))
                    dve.wait_ge(*drain_of(("bE", l, h)))
                    step(tt(eh[:, h, :], eh[:, h, :], b[:, 0:TOK], ALU.max))
                    step(stt(eh[:, h, :], b[:, 0:TOK], -1.0, eh[:, h, :], ALU.mult, ALU.max), V)
                    step(nc.vector.reciprocal(eh[:, h, :], eh[:, h, :]))
                    b = product(dve, ("num", l, h))
                    step(tt(eh[:, h, :], eh[:, h, :], b[:, 0:TOK], ALU.mult), V)
                    full = [P, DEC_B, MD]
                    step(tt(C_sb[:, h % 2], C_sb[:, h % 2], bc(al[h], 2, full), ALU.mult))
                    for j in range(2):
                        b = product(dve, ("Cs", l, h, j))
                        c = C_sb[:, h % 2, 4 * j:4 * j + 4, :].rearrange("p b k -> p (b k)")
                        step(tt(c, c, b, ALU.add), V)
                for h in range(MH):
                    dve.wait_ge(*drain_of(("hss", l, h)))
                    r = WT[:, h, 0:TOK]
                    step(nc.vector.reciprocal(r, r))
                    step(tt(eh[:, h, :], eh[:, h, :], r, ALU.mult))
                    if h == 0:
                        dve.wait_ge(sem("sigmoid_done"), l + 1)
                    step(stt(mixT[:, 4 + h, :], eh[:, h, :], prm[:, l, R_MNORM + h:R_MNORM + h + 1], region1[:, OM + h, :],
                             ALU.mult, ALU.mult), "mlstm_out_ready")
                n_new = nnT.rearrange("p (b h) -> p h b", b=DEC_B)
                a_hb = abc.rearrange("p h (b s) -> p h b s", b=DEC_B)[:, :, :, DEC_S - 1]
                step(tt(n_new, n_hb, a_hb, ALU.mult))
                b = product(dve, ("nn", l))
                step(tt(n_new, n_new, b[:, 0:NS].rearrange("p (h b) -> p h b", h=MH), ALU.add), V)
                for m in range(KD):
                    b = product(dve, ("out", l, m))
                    step(stt(xT[:, m, ST], b[:, ST], modT[:, 16 + m, 0:1], xT[:, m, ST], ALU.mult, ALU.add))
                    gated_add(modT, b[:, SB], m, 1, 16)
                scales(1, R_NFFN)
                step(normalise(("ss2", l, "S"), SB))
                modulate_samples(1)
                step(normalise(("ss2", l, "T"), ST), "xn_ready")
                step(copy(hS4, bc(hT[:, :, SB], 2, [P, KD, 4, NS])), "h_repeated")
                route_heads(l, "S", 0)
                center_gates(slice(0, 2))
                route_gates(l, "S", 1, slice(0, 2))
                for g in TILES:
                    base = first_slot[l, g] // K
                    if g == "S":
                        expert_unit(g, 0, 0, base)
                        route_heads(l, "T0", 0)
                        route_heads(l, "T0", 1)
                        center_gates(slice(0, 4))
                        expert_unit(g, 0, 1, base + 1)
                        route_gates(l, "T0", 2, slice(0, 4))
                        route_heads(l, "T0", 2)
                    elif g == "T0":
                        for n in range(8):
                            expert_unit(g, n // 2, n % 2, base + n)
                            if n == 0:
                                add_experts(l, "S")
                                route_heads(l, "T0", 3)
                                center_gates(slice(4, 8))
                                route_gates(l, "T0", 3, slice(4, 8))
                            if 1 <= n < 5:
                                route_heads(l, "T1", n - 1)
                            if n == 5:
                                center_gates(slice(0, 8))
                                route_gates(l, "T1", 4, slice(0, 8))
                            if n >= 2 and l + 1 < DEPTH:
                                ada(l + 1, n - 2)
                    else:
                        with dve.Fori(0, UNITS[g] // 2) as i:
                            for half in range(2):
                                expert_unit(g, i, half, base + 2 * i + half)
                    if g != "S":
                        add_experts(l, g)
            step(normalise(("ssf",), slice(0, TOK)), "xn_ready")


_INS = ["x_prompt", "x_sample", "c_prompt", "c_sample", "cache_k", "cache_v", "state_conv", "state_C", "state_n", "state_m",
        "rel_bias", "w_ada", "b_ada", "norm_mix", "norm_ffn", "w_in", "conv_w", "conv_b", "gate_b", "attn_sinks", "m_norm",
        "w_out", "peer_query", "peer_keys", "peer_u", "peer_v", "norm_final"]
_OUTS = [(1, SEQ, D), (DEC_B, DEC_S, D)] + [
    s for B in (1, DEC_B) for s in ((DEPTH, B, WINDOW, A_KV, DH), (DEPTH, B, WINDOW, A_KV, DH), (DEPTH, B, CONV_W - 1, 2 * MH * MD),
                                    (DEPTH, B, MH, MD, MD), (DEPTH, B, MH, MD), (DEPTH, B, MH))]


def kernel(**inputs):
    import numpy as _np
    import concourse.bacc as _bacc
    from concourse import mybir as _mybir
    from concourse.bass_utils import run_bass_kernel_spmd as _run

    nc = _bacc.Bacc("TRN2", target_bir_lowering=False, num_devices=1)
    arrays = {f"in_{name}": _np.ascontiguousarray(inputs[name]) for name in _INS}
    arrays["in_consts"], arrays["in_buckets"] = constants()
    args = [nc.dram_tensor(name, a.shape, _mybir.dt.from_np(a.dtype), kind="ExternalInput").ap() for name, a in arrays.items()]
    args += [nc.dram_tensor(f"out_{i}", shape, _mybir.dt.float32, kind="ExternalOutput").ap() for i, shape in enumerate(_OUTS)]
    hybrid_trunk(nc, *args)
    r = _run(nc, [arrays], core_ids=[0])
    return tuple(r.results[0][f"out_{i}"] for i in range(len(_OUTS)))
```

```python
from contextlib import ExitStack

import numpy as np

import concourse.bass as bass
from concourse import mybir

F32 = mybir.dt.float32
I32 = mybir.dt.int32
U32 = mybir.dt.uint32
ALU = mybir.AluOpType
ACT = mybir.ActivationFunctionType
AX = mybir.AxisListType.X

P = 128
DEPTH, D, SEQ, DEC_B, DEC_S = 2, 1024, 256, 8, 4
KD = D // P
NS = DEC_B * DEC_S
TOK = SEQ + NS
NC = 1 + DEC_B
A_HEADS, A_KV, DH, WINDOW = 8, 2, 64, 128
GROUP = A_HEADS // A_KV
MH, MD = 4, 128
CONV_W = 4
EPS = 1e-6
BIG = 1e30
N_KEYS, P_HEADS, TOPK = 128, 8, 16
N_EXPERTS = N_KEYS * N_KEYS
IN_COLS = 2824
GATE_COL = IN_COLS - 2 * MH
QA, KA, VA, VM, OM = 0, 4, 5, 6, 10
SKEW = 384
K = 16
RU, RV = 4, 8
DIAGS = 4
BANKS = 6
WSLOTS = 2
R_NMIX, R_NFFN, R_BADA, R_CONVW, R_CONVB, R_MNORM, R_NFIN, R_ROWS = 0, 8, 16, 64, 96, 104, 108, 116
C_ID, C_ONE, C_CAUSAL, C_CAUSALS, C_BLOCK, C_BLOCKADD, C_SUM, C_IOTA, C_COLS = 0, 128, 256, 384, 416, 424, 456, 488, 504
TILES = ["S", "T0", "T1"]
UNITS = {"S": 2, "T0": 8, "T1": 8}
COL = {"T0": 0, "T1": 128, "S": 256}
TI = {"T0": 0, "T1": 1, "S": 2}


def constants():
    c = np.zeros((P, C_COLS), np.float32)
    p = np.arange(P)
    c[:, C_ID:C_ID + P] = np.eye(P)
    c[:, C_ONE:C_ONE + P] = 1.0
    c[:, C_CAUSAL:C_CAUSAL + P] = np.where(p[:, None] > p[None, :], BIG, 0)
    s, t = np.arange(NS)[:, None], np.arange(NS)[None, :]
    c[:NS, C_CAUSALS:C_CAUSALS + NS] = np.where((s // DEC_S == t // DEC_S) & (s <= t), 0, BIG)
    c[:NS, C_BLOCK:C_BLOCK + DEC_B] = s // DEC_S == np.arange(DEC_B)[None, :]
    c[:, C_BLOCKADD:C_BLOCKADD + NS] = np.where((p[:, None] % NS) // DEC_S == t // DEC_S, 0, -BIG)
    c[:, C_SUM:C_SUM + NS] = p[:, None] % NS == t
    c[:, C_IOTA:C_IOTA + TOPK] = np.arange(TOPK)
    hot = np.zeros((33, SKEW), np.float32)
    for x in range(SKEW):
        n = 255 - x
        if 0 <= n < WINDOW:
            large = 16 + int(np.log(max(n, 1) / 16) / np.log(WINDOW / 16) * 16) if n >= 16 else n
            hot[min(large, 31), x] = 1
        else:
            hot[32, x] = 1
    return c, hot


def plan():
    out = []

    def add(eng, *key):
        out.append((key, eng))

    def ada(l, i):
        add("A", "ada", l, 2 * i)
        add("A", "ada", l, 2 * i + 1)
        add("V", "adaT", l, i)

    add("V", "c")
    for m in range(2):
        add("A", "ada", 0, m)
    for l in range(DEPTH):
        add("V", "params", l)
    for k in range(KD):
        add("A", "x", k)
    add("V", "adaT", 0, 0)
    ada(0, 1)
    for l in range(DEPTH):
        add("V", "cvs", l)
        add("A", "ss1", l)
        if l == 0:
            for h in range(A_HEADS):
                add("A", "rel", h)
        for m in PROJ_ORDER[:-4]:
            add("V" if m in ("ig", "fg") else "A", "proj", l, m)
        for t in range(3):
            add("A", "kvtok", l, t)
        for j in range(2):
            add("A", "kct", l, j)
        for t in range(2):
            for j in range(4):
                add("V", "sc", l, t, j)
            if t == 0:
                add("A", "ada", l, 4)
        for n in range(2):
            add("A", "ssT", l, n)
        add("A", "ada", l, 5)
        for n in range(2):
            add("V", "ss", l, n)
        for m in PROJ_ORDER[-4:]:
            add("A", "proj", l, m)
        for t in range(3):
            add("A", "ktok", l, t)
        for t in range(3):
            add("A", "vtok", l, t)
        add("V", "cols", l)
        add("V", "nT", l)
        add("V", "bA", l)
        for h in range(MH):
            add("A", "bM", l, h)
            add("V", "qk", l, h)
            if h % 2:
                add("A", "ada", l, 6 + h // 2)
        for t in range(2):
            for j in range(2 * (t + 1)):
                add("A", "pT", l, t, j)
            add("A", "o", l, t)
            add("A", "ada", l, 8 + t)
        for n in range(2):
            add("A", "spT", l, n)
        add("A", "o", l, 2)
        for h in range(MH):
            for j in range(2):
                add("A", "CT", l, h, j)
            add("V", "den", l, h)
            add("A", "num", l, h)
            for j in range(2):
                add("V", "Cs", l, h, j)
            if h % 2 == 0:
                add("A", "ada", l, 10 + h // 2)
        add("V", "hss", l)
        add("A", "Cp", l)
        for h in range(MH):
            add("V", "hr", l, h)
        add("A", "np", l)
        add("V", "nn", l)
        for i in range(2, 6):
            add("V", "adaT", l, i)
        add("A", "nnr", l)
        for j in range(2):
            add("A", "cvr", l, j)
        for m in range(KD):
            add("V", "out", l, m)
        add("A", "ss2", l, "S")
        for j in range(4):
            add("A", "ky", l, j)
        for m in QUERY_TILES:
            if m == QUERY_TILES[2]:
                add("A", "ss2", l, "T")
            add("A", "qpS", l, m)
        add("A", "qST", l)
        add("V", "rs", l, "S", 0)
        for j in range(2):
            add("A", "h2", l, 2, j)
        for m in range(3):
            for j in range(4):
                add("A", "qp", l, 4 * m + j)
        for m in range(2):
            add("V", "rs", l, "T0", m)
        for t in (0, 1):
            for j in range(2):
                add("A", "h2", l, t, j)
        add("V", "rs", l, "T0", 2)
        for j in range(4):
            add("A", "qp", l, 12 + j)
        for g in TILES:
            if g == "T0":
                add("V", "rs", l, "T0", 3)
                for n in range(8):
                    if n < 4:
                        add("V", "rs", l, "T1", n)
                    if 1 <= n < 3 and l + 1 < DEPTH:
                        ada(l + 1, n - 1)
            for j in range(2):
                add("V", "pt", l, g, j)
    add("A", "ssf")
    for j in range(2):
        for t in range(3):
            add("A", "y", t, j)
    return out


PROJ_TILES = [5, 1, 2, 3, 0, 4]
QUERY_TILES = [0, 1, 2, 3]
ROUTED = {"S": 1, "T0": 2, "T1": 4}
PROJ_ORDER = [20, 21, "ig", "fg"] + [4 * t + j for t in PROJ_TILES[1:] for j in range(4)]


def hybrid_trunk(nc, x_prompt, x_sample, c_prompt, c_sample, cache_k, cache_v, state_conv, state_C, state_n, state_m,
                 rel_bias, w_ada, b_ada, norm_mix, norm_ffn, w_in, conv_w, conv_b, gate_b, attn_sinks, m_norm, w_out,
                 peer_query, peer_keys, peer_u, peer_v, norm_final, consts, buckets,
                 y_p, y_s, k_p, v_p, conv_p, C_p, n_p, m_p, k_s, v_s, conv_s, C_s, n_s, m_s):
    PLAN = plan()
    nth = {key: n for n, (key, _) in enumerate(PLAN)}
    drains = {key: sum(e == eng for _, e in PLAN[:n + 1]) for n, (key, eng) in enumerate(PLAN)}

    ctx = ExitStack()
    with ctx:
        ctx.enter_context(nc.allow_non_contiguous_dma(reason="a few rows of gates, biases and running maxima"))

        def sb(name, shape, dt=F32):
            return ctx.enter_context(nc.sbuf_tensor(name, shape, dt))

        sems = {}

        def sem(name):
            if name not in sems:
                sems[name] = ctx.enter_context(nc.semaphore(name))
            return sems[name]

        rel_dram = nc.dram_tensor("rel_skewed", (A_HEADS, P, SKEW), F32, kind="Internal").ap()

        cst = sb("cst", [P, C_COLS])
        ident, ones = cst[:, C_ID:C_ID + P], cst[:, C_ONE:C_ONE + P]
        wring = sb("wring", [P, WSLOTS, KD, 512])
        xT = sb("xT", [P, KD, TOK])
        hT = sb("hT", [P, KD, TOK])
        region1 = sb("region1", [P, 16, TOK])
        cin = sb("cin", [P, KD * (SEQ + 3) + KD * DEC_B * (DEC_S + 3)])
        cin_p = cin[:, 0:KD * (SEQ + 3)].rearrange("p (k t) -> p k t", k=KD)
        cin_s = cin[:, KD * (SEQ + 3):].rearrange("p (k b t) -> p k b t", k=KD, b=DEC_B)
        keyT = cin[:, 0:16 * P].rearrange("p (m k) -> p m k", m=16)
        qks = sb("qks", [P, KD, TOK])
        qks_flat = qks[:, :, :].rearrange("p k t -> p (k t)")
        mixT = sb("mixT", [P, KD, TOK])
        mixT_flat = mixT[:, :, :].rearrange("p k t -> p (k t)")
        ada_rows = mixT_flat[:, 0:2 * P].rearrange("p (r c) -> p r c", r=2)
        query_rows = mixT_flat[:, 0:4 * P].rearrange("p (m c) -> p m c", m=4)
        bias = sb("bias", [P, A_HEADS, 2 * WINDOW])
        bias_s = sb("bias_s", [P, A_KV, WINDOW + NS])
        prm = sb("prm", [P, DEPTH, R_ROWS])
        gate_bias = sb("gate_bias", [MH, DEPTH, 2])
        sink_p = sb("sink_p", [P, DEPTH, A_HEADS])
        sink_s = sb("sink_s", [P, DEPTH, A_KV])
        eps_t = sb("eps_t", [P, 1])
        act_scratch = sb("act_scratch", [P, 1])[:, :]
        cT = sb("cT", [P, KD, NS])
        modT_all = sb("modT", [P, 2, 48, NC])
        modA = sb("modA", [P, 2, KD, NC])
        rstd = sb("rstd", [P, TOK])
        head_den = sb("head_den", [P, 3, MH])
        head_ssq = sb("head_ssq", [P, 3, MH])
        head_rstd = sb("head_rstd", [P, 3 * MH])
        diag = sb("diag", [P, DIAGS, P])
        dots = sb("dots", [P, 2, K])
        gelus = sb("gelus", [P, 2, K])
        wts = sb("wts", [P, 2, K])
        idx_staged = sb("idx_staged", [P, 2, K], I32)
        idx_all = sb("idx_all", [P, 3, P_HEADS * TOPK], I32)
        g_all = sb("g_all", [P, 3, P_HEADS * TOPK])

        rings = sb("rings", [P, (RU + RV) * D])
        u_ring = rings[:, 0:RU * D].rearrange("p (r d) -> p r d", r=RU)
        v_ring = rings[:, RU * D:].rearrange("p (r d) -> p r d", r=RV)

        query_w = v_ring.rearrange("p (i h) d -> p i (h d)", i=2).rearrange("p i (k n) -> p i k n", k=KD)

        class Cut:
            def __init__(self, region, size):
                self.region, self.size, self.at = region, size, 0

            def __call__(self, n, parts=P):
                self.at += n
                assert self.at <= self.size, self.at
                return self.region[0:parts, self.at - n:self.at]

        cut = Cut(rings, (RU + RV) * D)
        C_flat = cut(2048)
        keys_raw = C_flat.rearrange("p (m k) -> p m k", m=16)
        C_sb = C_flat.rearrange("p (r b k) -> p r b k", r=2, b=DEC_B)
        CT_flat = cut(2048)
        CT = CT_flat.rearrange("p (r b k) -> p r b k", r=2, b=DEC_B)
        kc = cut(1024).rearrange("p (b c) -> p b c", b=DEC_B)
        vc = cut(1024).rearrange("p (b c) -> p b c", b=DEC_B)
        kcT_flat = cut(1024)
        kcT = kcT_flat.rearrange("p (b c) -> p b c", b=DEC_B)
        PT = cut(2048).rearrange("p (h b q) -> p h b q", h=A_HEADS, b=2)
        sT = cut(256).rearrange("p (n r) -> p n r", n=2)
        SS = cut(2 * 160).rearrange("p (n r) -> p n r", n=2)
        PTs_flat = cut(512)
        PTs = PTs_flat.rearrange("p (n j r) -> p n j r", n=2, j=2)
        row = {n: cut(TOK, MH) for n in ("ig", "b", "a", "M", "e", "wl")}
        row["aw"] = cut(NS, MH)
        x_tok = rings[:, 0:3 * D].rearrange("p (t d) -> p t d", t=3)
        c_tok = rings[0:NC, 3 * D:4 * D]
        prm_rows = rings[0:R_ROWS, 4 * D:4 * D + 2 * P].rearrange("p (l c) -> p l c", l=2)
        hot = rings[0:33, 5 * D:5 * D + SKEW]
        relb = rings[0:33, 6 * D:7 * D].rearrange("p (h c) -> p h c", h=A_HEADS)
        relraw = rings[0:33, 7 * D:7 * D + 8]
        rel_rows = rings[:, 8 * D:8 * D + 8 * SKEW].rearrange("p (h c) -> p h c", h=A_HEADS)
        hT_flat = hT[:, :, :].rearrange("p k t -> p (k t)")
        S1 = CT_flat.rearrange("p (h k) -> p h k", h=A_HEADS)
        S0 = mixT[:, 4:8, :].rearrange("p k t -> p (k t)")[:, 0:A_HEADS * P].rearrange("p (h k) -> p h k", h=A_HEADS)
        wv = hT_flat[:, 0:1024].rearrange("p (t h c) -> p t h c", t=2, h=MH)

        MSIZE = 6912
        mreg = sb("mreg", [P, MSIZE])
        cut = Cut(mreg, MSIZE)
        vt = cut(3 * 512).rearrange("p (t c) -> p t c", t=3)
        kt = cut(3 * 512).rearrange("p (t c) -> p t c", t=3)
        WT = cut(4 * 416).rearrange("p (h c) -> p h c", h=MH)
        eh_flat = cut(MH * TOK)
        eh = eh_flat.rearrange("p (h c) -> p h c", h=MH)
        kdup = eh_flat[:, 0:A_KV * TOK].rearrange("p (n t) -> p n t", n=A_KV)
        qd = eh_flat[:, A_KV * TOK:A_KV * TOK + GROUP * NS].rearrange("p (g t) -> p g t", g=GROUP)
        wk = cut(1024, NS).rearrange("p (b k) -> p b k", b=DEC_B)
        cut = Cut(mreg, MSIZE)
        h2tok = cut(3 * D).rearrange("p (t d) -> p t d", t=3)
        cand_flat = cut(2048)
        cand = cand_flat.rearrange("p (h c) -> p h c", h=P_HEADS)
        onehot = cand_flat.rearrange("p (h i j) -> p h i j", h=P_HEADS, i=TOPK)
        hS4 = cand_flat[:, 0:1024].rearrange("p (k q t) -> p k q t", k=KD, q=4)
        rep = cut(256)
        s_top = cut(256).rearrange("p (h c k) -> p h c k", h=P_HEADS, c=2)
        i_top = cut(256).bitcast(U32).rearrange("p (h c k) -> p h c k", h=P_HEADS, c=2)
        i_topf = cut(256).rearrange("p (h c k) -> p h c k", h=P_HEADS, c=2)
        best = cut(128).rearrange("p (h k) -> p h k", h=P_HEADS)
        pos = cut(128).bitcast(U32).rearrange("p (h k) -> p h k", h=P_HEADS)
        pij_flat = cut(256)
        pij = pij_flat.rearrange("p (c h k) -> p c h k", c=2, h=P_HEADS)
        small = sb("small", [P, 1000])
        cut = Cut(small, 1000)
        stat = [cut(40).rearrange("p (w h) -> p w h", w=5) for _ in range(3)]
        cols = cut(36).rearrange("p (t c) -> p t c", t=3)
        WB = cut(32, NS).rearrange("p (h b) -> p h b", h=MH)
        nrow = cut(P, NS)
        nT = cut(32)
        nnT = cut(32)
        abc = cut(P).rearrange("p (h t) -> p h t", h=MH)
        qa = cut(P).rearrange("p (h t) -> p h t", h=MH)
        nqa = cut(P).rearrange("p (h t) -> p h t", h=MH)
        m_in = cut(DEC_B, MH)
        m_out = cut(NC, MH)
        tmp = cut(P)
        zeros = sb("zeros", [P, P])
        pe_tok = sb("pe_tok", [P, D])
        ada_rows_mid = pe_tok[:, :].rearrange("p (r c) -> p r c", r=8)
        cvo = sb("cvo", [P, KD, 27])
        kvt = sb("kvt", [P, 3, 2 * P])

        banks = ctx.enter_context(nc.psum_tensor("banks", [P, BANKS, 512], F32))
        acc = ctx.enter_context(nc.psum_tensor("acc", [P, 2, 512], F32))

        product_ready = sem("product_ready")
        drained = {"A": sem("drained_by_act"), "V": sem("drained_by_dve")}

        def bank(key):
            return banks[:, nth[key] % BANKS, :]

        def drain_of(key):
            return drained[PLAN[nth[key]][1]], drains[key]

        def claim(pe, key):
            if nth[key] >= BANKS:
                pe.wait_ge(*drain_of(PLAN[nth[key] - BANKS][0]))
            return bank(key)

        class Steps:
            def __init__(self, eng, own):
                self.eng, self.own, self.count = eng, own, {}

            def __call__(self, ins, signal=None):
                s = signal or self.own
                ins.then_inc(sem(s) if isinstance(s, str) else s, 1)
                n = self.count[str(s)] = self.count.get(str(s), 0) + 1
                self.eng.wait_ge(sem(s) if isinstance(s, str) else s, n)

        def product(eng, key):
            eng.wait_ge(product_ready, nth[key] + 1)
            return bank(key)

        def bc(ap, axis, shape):
            return ap.unsqueeze(axis).broadcast_to(shape)

        def by_sample(ap):
            return ap.rearrange("p (b s) -> p b s", b=DEC_B) if len(ap.shape) == 2 else \
                ap.rearrange("p k (b s) -> p k b s", b=DEC_B)

        SB, ST = slice(SEQ, TOK), slice(0, SEQ)
        setup_loads = 4 + DEPTH * (9 + GROUP)
        first_slot, slots = {}, 0
        for l in range(DEPTH):
            for g in TILES:
                first_slot[l, g] = slots
                slots += UNITS[g] * K
        u_loaded = [sem(f"u_row_loaded_{r}") for r in range(RU)]
        v_loaded = [sem(f"v_row_loaded_{r}") for r in range(RV)]

        block = ctx.enter_context(nc.Block())

        @block.sync
        def _(sp):
            tile = 0

            def weights(layer, src, c0, n):
                nonlocal tile
                if tile >= WSLOTS:
                    sp.wait_ge(sem("weights_used"), tile - WSLOTS + 1)
                sp.dma_start(wring[:, tile % WSLOTS, :, 0:n],
                             src[layer, :, c0:c0 + n].rearrange("(k p) n -> p k n", p=P))\
                    .then_inc(sem(f"weights_loaded_{tile % WSLOTS}"), 16)
                tile += 1

            for dst, src in ((c_tok[0:1, :], c_prompt), (c_tok[1:NC, :], c_sample), (cst[:, :], consts)):
                sp.dma_start(dst, src).then_inc(sem("first_loaded"), 16)
            for m in range(2):
                weights(0, w_ada, 512 * m, 512)
            load = lambda dst, src: sp.dma_start(dst, src).then_inc(sem("setup_loaded"), 16)
            load(x_tok[:, 0:2, :], x_prompt[0].rearrange("(t p) d -> p t d", p=P))
            load(x_tok[0:NS, 2, :], x_sample.rearrange("b s d -> (b s) d"))
            load(hot, buckets)
            load(relraw[0:32, :], rel_bias)
            for l in range(DEPTH):
                for r, src, n in ((R_NMIX, norm_mix[l], 8), (R_NFFN, norm_ffn[l], 8), (R_BADA, b_ada[l], 48),
                                  (R_CONVB, conv_b[l], 8), (R_MNORM, m_norm[l], 4), (R_NFIN, norm_final, 8)):
                    load(prm_rows[r:r + n, l, :], src.rearrange("(k c) -> k c", c=P))
                load(prm_rows[R_CONVW:R_CONVW + 32, l, :], conv_w[l].rearrange("i (k c) -> (i k) c", c=P))
                load(gate_bias[:, l, :], gate_b[l].rearrange("(g h) -> h g", g=2))
                load(sink_p[:, l, :], attn_sinks[l:l + 1, :].broadcast_to([P, A_HEADS]))
                for g in range(GROUP):
                    load(sink_s[g * NS:(g + 1) * NS, l, :],
                         bass.AP(attn_sinks.tensor, l * A_HEADS + g, [[0, NS], [GROUP, A_KV]]))
            for m in range(2, 4):
                weights(0, w_ada, 512 * m, 512)
            for l in range(DEPTH):
                for m in PROJ_TILES:
                    if m == PROJ_TILES[-1]:
                        for i in range(4, 6):
                            weights(l, w_ada, 512 * i, 512)
                    weights(l, w_in, 512 * m, min(512, IN_COLS - 512 * m))
                    if m == PROJ_TILES[2]:
                        if l:
                            sp.wait_ge(*drain_of(("pt", l - 1, TILES[-1], 1)))
                        else:
                            sp.wait_ge(sem("rel_stored"), 16)
                        sp.dma_start(kc, cache_k[l].rearrange("b w h d -> w b (h d)")).then_inc(sem("kc_loaded"), 16)
                        sp.dma_start(vc, cache_v[l].rearrange("b w h d -> w b (h d)")).then_inc(sem("vc_loaded"), 16)
                for m in range(6, 12):
                    weights(l, w_ada, 512 * m, 512)
                for m in range(2):
                    weights(l, w_out, 512 * m, 512)
                sp.wait_ge(sem("scratch_free"), l + 1)
                for i, m in enumerate(QUERY_TILES[:2]):
                    sp.dma_start(query_w[:, i], peer_query[l, :, 512 * m:512 * m + 512].rearrange("(k p) n -> p k n", p=P))\
                        .then_inc(sem("query_weights_loaded"), 16)
                for m in QUERY_TILES[2:]:
                    weights(l, peer_query, 512 * m, 512)
                if l + 1 < DEPTH:
                    for m in range(4):
                        weights(l + 1, w_ada, 512 * m, 512)
            for j in range(2):
                half = slice(512 * j, 512 * j + 512)
                sp.wait_ge(*drain_of(("y", 1, j)))
                sp.dma_start(y_p[0, :, half].rearrange("(t p) d -> p t d", p=P), x_tok[:, 0:2, half]).then_inc(sem("y_stored"), 16)
                sp.wait_ge(*drain_of(("y", 2, j)))
                sp.dma_start(y_s.rearrange("b s d -> (b s) d")[:, half], x_tok[0:NS, 2, half]).then_inc(sem("y_stored"), 16)
            sp.wait_ge(sem("y_stored"), 64)

        @block.gpsimd
        def _(pool):
            u_rows = peer_u.rearrange("l e d -> (l e) d")
            v_rows = peer_v.rearrange("l e d -> (l e) d")
            u_free = pool.alloc_register("u_free")
            v_free = pool.alloc_register("v_free")
            stage_free = pool.alloc_register("stage_free")
            pool.reg_mov(u_free, 1)
            pool.reg_mov(v_free, 1)
            pool.reg_mov(stage_free, K)
            stored = 0

            def store(dst, src):
                nonlocal stored
                pool.dma_start(dst, src).then_inc(sem("outputs_stored"), 16)
                stored += 16

            def unit(g, i, half, n, first, made=None):
                if not first:
                    pool.wait_ge(sem("v_row_used"), stage_free)
                    pool.reg_add(stage_free, stage_free, K)
                pool.tensor_copy(idx_staged[:, half, :], idx_all[:, TI[g], bass.ds(i * 2 * K + half * K, K)])\
                    .then_inc(sem("idx_staged"), 1)
                pool.wait_ge(sem("idx_staged"), n + 1)
                for k in range(K):
                    if not (first and half == 0 and k < RU):
                        pool.wait_ge(sem("u_row_used"), u_free)
                        pool.reg_add(u_free, u_free, 1)
                    pool.indirect_dma_start(
                        out=u_ring[:, k % RU, :], out_offset=None, in_=u_rows,
                        in_offset=bass.IndirectOffsetOnAxis(ap=idx_staged[:, half, k:k + 1], axis=0))\
                        .then_inc(u_loaded[k % RU], 16)
                if made:
                    pool.wait_ge(product_ready, nth[made] + 1)
                for k in range(K):
                    if not (first and half == 0 and k < RV):
                        pool.wait_ge(sem("v_row_used"), v_free)
                        pool.reg_add(v_free, v_free, 1)
                    pool.indirect_dma_start(
                        out=v_ring[:, k % RV, :], out_offset=None, in_=v_rows,
                        in_offset=bass.IndirectOffsetOnAxis(ap=idx_staged[:, half, k:k + 1], axis=0))\
                        .then_inc(v_loaded[k % RV], 16)

            for l in range(DEPTH):
                if l:
                    pool.wait_ge(*drain_of(("pt", l - 1, TILES[-1], 1)))
                else:
                    pool.wait_ge(sem("setup_loaded"), 16 * setup_loads)
                    pool.wait_ge(*drain_of(("x", KD - 1)))
                pool.dma_start(pe_tok[0:24, :], state_conv[l].rearrange("b r c -> (b r) c")).then_inc(sem("conv_state_loaded"), 16)
                pool.dma_start(nrow, state_n[l].rearrange("b h k -> (b h) k")).then_inc(sem("n_loaded"), 16)
                pool.dma_start(m_in, state_m[l].rearrange("b h -> h b")).then_inc(sem("m_loaded"), 16)
                if l == 0:
                    pool.wait_ge(*drain_of(("rel", A_HEADS - 1)))
                    pool.dma_start(rel_dram.rearrange("h p c -> p h c"), rel_rows).then_inc(sem("rel_stored"), 16)
                    pool.wait_ge(sem("rel_stored"), 16)
                    skew = lambda off, ap: bass.AP(rel_dram.tensor, off, ap)
                    pool.dma_start(bias[:, :, :], skew(127, [[SKEW - 1, P], [P * SKEW, A_HEADS], [1, 2 * WINDOW]]))\
                        .then_inc(sem("bias_loaded"), 16)
                    for h in range(A_HEADS):
                        n, g = h // GROUP, h % GROUP
                        src = slice(g * NS, (g + 1) * NS)
                        pool.dma_start(bias_s[src, n, 0:WINDOW + DEC_S],
                                       skew(h * P * SKEW + 127, [[0, DEC_B], [SKEW - 1, DEC_S], [1, WINDOW + DEC_S]]))\
                            .then_inc(sem("bias_loaded"), 16)
                def load_C(h):
                    pool.dma_start(C_sb[:, h % 2, :, :], state_C[l, :, h].rearrange("b v k -> v b k"))\
                        .then_inc(sem(f"C_loaded_{h % 2}"), 16)
                load_C(0)
                load_C(1)
                pool.wait_ge(*drain_of(("proj", l, KA)))
                for n in range(A_KV):
                    for half in range(2):
                        pool.dma_start(kdup[half * DH:(half + 1) * DH, n, :], region1[n * DH:(n + 1) * DH, KA, :])\
                            .then_inc(sem("k_doubled"), 16)
                pool.wait_ge(*drain_of(("proj", l, QA + 3)))
                for n in range(A_KV):
                    for g in range(GROUP):
                        h = n * GROUP + g
                        pool.dma_start(qd[n * DH:(n + 1) * DH, g, :], region1[h % 2 * DH:(h % 2 + 1) * DH, h // 2, SB])\
                            .then_inc(sem("q_moved"), 16)
                pool.wait_ge(*drain_of(("kvtok", l, 2)))
                for dst_p, dst_s, cache, c0, loaded in ((k_p, k_s, kc, 0, "kc_loaded"), (v_p, v_s, vc, P, "vc_loaded")):
                    store(dst_p[l, 0].rearrange("w h d -> w (h d)"), kvt[:, 1, c0:c0 + P])
                    pool.wait_ge(sem(loaded), 16 * (l + 1))
                    store(dst_s[l, :, 0:WINDOW - DEC_S].rearrange("b w h d -> w b (h d)"), cache[DEC_S:WINDOW, :, :])
                    for b in range(DEC_B):
                        store(dst_s[l, b, WINDOW - DEC_S:].rearrange("w h d -> w (h d)"), kvt[b * DEC_S:(b + 1) * DEC_S, 2, c0:c0 + P])
                pool.wait_ge(sem("m_out_ready"), l + 1)
                store(m_p[l, 0].unsqueeze(1), m_out[:, 0:1])
                store(m_s[l].rearrange("b h -> h b"), m_out[:, 1:NC])
                for h in range(MH):
                    pool.wait_ge(*drain_of(("Cs", l, h, 1)))
                    store(C_s[l, :, h].rearrange("b v k -> v b k"), C_sb[:, h % 2, :, :])
                    if h + 2 < MH:
                        pool.wait_ge(sem("outputs_stored"), stored)
                        load_C(h + 2)
                pool.wait_ge(sem("outputs_stored"), stored)
                pool.dma_start(keys_raw, peer_keys[l].rearrange("h c k d -> k (h c) d")).then_inc(sem("keys_loaded"), 16)
                pool.wait_ge(*drain_of(("np", l)))
                store(C_p[l, 0].rearrange("h v k -> v h k"), PTs_flat.rearrange("p (h k) -> p h k", h=MH))
                store(n_p[l, 0].rearrange("h k -> (h k)").unsqueeze(0), kcT_flat[0:1, 0:512])
                pool.wait_ge(*drain_of(("nnr", l)))
                store(n_s[l].rearrange("b h k -> (b h) k"), nrow)
                pool.wait_ge(*drain_of(("cvr", l, 1)))
                store(conv_p[l, 0], pe_tok[0:3, :])
                store(conv_s[l].rearrange("b r c -> (b r) c"), pe_tok[3:27, :])
                pool.wait_ge(sem("outputs_stored"), stored)
                pool.sem_inc(sem("scratch_free"), 1)
                for g in TILES:
                    base = first_slot[l, g] // K
                    pool.wait_ge(sem("idx_ready"), 4 * l + ROUTED[g])
                    if g == "T0":
                        for first in (0, 2):
                            if first:
                                pool.wait_ge(sem("idx_ready"), 4 * l + ROUTED[g] + 1)
                            with pool.Fori(first, first + 2) as i:
                                for half in range(2):
                                    unit(g, i, half, base + 2 * i + half, False)
                    elif g == "S":
                        for half in range(2):
                            unit(g, 0, half, base + half, l == 0, made=("qp", l, 7) if half == 0 else None)
                    else:
                        with pool.Fori(0, UNITS[g] // 2) as i:
                            for half in range(2):
                                unit(g, i, half, base + 2 * i + half, False)

        @block.scalar
        def _(act):
            step = Steps(act, "act_step")
            A = drained["A"]

            def evacuate(key, dst, cols=None, parts=None, src=None):
                b = product(act, key)
                src = b[:, 0:cols] if src is None else src
                if parts is not None:
                    src = src[0:parts]
                step(nc.scalar.activation(dst, src, ACT.Copy), A)

            def root(key, dst, n, ahead=True):
                if ahead:
                    step(nc.scalar.activation(act_scratch, eps_t[:, 0:1], ACT.Sqrt))
                b = product(act, key)
                step(nc.scalar.activation(dst, b[:, 0:dst.shape[-1]], ACT.Sqrt, bias=eps_t[:, 0:1], scale=1.0 / n), A)

            def squares(cols=slice(0, TOK)):
                step(nc.scalar.activation(hT[:, :, cols], xT[:, :, cols], ACT.Square), "squares_ready")

            def modulate(l, w):
                modT = modT_all[:, l % 2]
                act.wait_ge(sem("xn_ready"), 2 * l + w + 1)
                shift = 24 * w
                for k in range(KD):
                    step(nc.scalar.activation(hT[:, k, ST], qks[:, k, ST], ACT.Identity,
                                              bias=modT[:, shift + k, 0:1], scale=modA[:, w, k, 0:1]), "h_ready")

            def softmax_exp(l, i, S, sink, width):
                act.wait_ge(sem("exp_wanted"), 3 * l + i + 1)
                nh = S.shape[1]
                for h in range(nh):
                    step(nc.scalar.activation(S[:, h, :], S[:, h, :], ACT.Exp, bias=stat[i][:, 1, h:h + 1],
                                              accum_out=stat[i][:, 3, h:h + 1]))
                step(nc.scalar.activation(stat[i][:, 2, 0:nh], stat[i][:, 2, 0:nh], ACT.Exp), "exp_done")

            def gate_exp(l, routed, heads):
                act.wait_ge(sem("gate_exp_wanted"), 4 * l + routed)
                step(nc.scalar.activation(best[:, heads, :], best[:, heads, :], ACT.Exp), "gate_exp_done")

            def expert_unit(n, half, first):
                act.wait_ge(sem("u_row_used"), n * K + K)
                nc.scalar.activation(gelus[:, half, :], dots[:, half, :], ACT.Gelu_apprx_tanh).then_inc(sem("gelu_ready"), 1)
                act.wait_ge(sem("expert_weights_ready"), n + 1)
                for k in range(K):
                    if not (first and half == 0 and k < DIAGS):
                        act.wait_ge(sem("v_row_used"), n * K + (k - DIAGS + 1))
                    nc.scalar.activation(diag[:, k % DIAGS, :], ident, ACT.Copy, scale=wts[:, half, k:k + 1])\
                        .then_inc(sem("diag_ready"), 1)

            act.wait_ge(sem("first_loaded"), 48)
            act.wait_ge(sem("eps_ready"), 1)
            step(nc.scalar.activation(c_tok, c_tok, ACT.Silu), "c_silu")
            def ada(l, i):
                for m in (2 * i, 2 * i + 1):
                    if i:
                        act.wait_ge(product_ready, nth["adaT", l, i - 1] + 1)
                    evacuate(("ada", l, m), ada_rows[:, m % 2, :], P)

            def ada_mid(l, m):
                evacuate(("ada", l, m), ada_rows_mid[:, m - 4, :], P)

            ada(0, 0)
            for k in range(KD):
                evacuate(("x", k), xT[:, k, :], TOK)
            ada(0, 1)
            for l in range(DEPTH):
                if l:
                    act.wait_ge(*drain_of(("pt", l - 1, TILES[-1], 1)))
                squares()
                root(("ss1", l), rstd[:, :], D)
                if l == 0:
                    for h in range(A_HEADS):
                        evacuate(("rel", h), rel_rows[:, h, :], SKEW)
                modulate(l, 0)
                for m in PROJ_ORDER[:-4]:
                    key = ("proj", l, m)
                    if m == "ig":
                        continue
                    if m == "fg":
                        act.wait_ge(sem("gate_abs_ready"), l + 1)
                        step(nc.scalar.activation(row["M"], row["M"], ACT.Exp, scale=-1.0))
                        step(nc.scalar.activation(row["M"], row["M"], ACT.Ln, bias=1.0), "gate_log_ready")
                        continue
                    if 6 <= m < 14:
                        k = m - 6
                        b = product(act, key)
                        act.wait_ge(sem("cin_padded"), l + 1)
                        step(nc.scalar.activation(cin_p[:, k, 3:], b[:, ST], ACT.Copy))
                        step(nc.scalar.activation(cin_s[:, k, :, 3:], by_sample(b[:, SB]), ACT.Copy), A)
                    else:
                        m = m if m < 6 else m - 8
                        evacuate(key, region1[:, m, :], TOK)
                for t in range(3):
                    n = P if t < 2 else NS
                    evacuate(("kvtok", l, t), kvt[0:n, t, :], 2 * P, n)
                for j in range(2):
                    evacuate(("kct", l, j), kcT[:, 4 * j:4 * j + 4, :].rearrange("p b c -> p (b c)"), 512)
                act.wait_ge(sem("conv_done"), (l + 1) * KD)
                for j in range(2):
                    step(nc.scalar.activation(qks[:, 4 * j:4 * j + 4, :], qks[:, 4 * j:4 * j + 4, :], ACT.Silu), "silu_done")
                act.wait_ge(sem("rows_wanted"), l + 1)
                for r, s in (("e", -1.0), ("wl", 1.0), ("aw", 1.0)):
                    step(nc.scalar.activation(row[r], row[r], ACT.Exp, scale=s), "rows_done")
                ada_mid(l, 4)
                softmax_exp(l, 0, S0, None, P)
                softmax_exp(l, 1, S1, None, 2 * P)
                for n in range(A_KV):
                    evacuate(("ssT", l, n), sT[:, n, :], P)
                ada_mid(l, 5)
                softmax_exp(l, 2, SS, None, 160)
                for m in PROJ_ORDER[-4:]:
                    evacuate(("proj", l, m), region1[:, m - 8, :], TOK)
                for t in range(3):
                    n = P if t < 2 else NS
                    evacuate(("ktok", l, t), kt[0:n, t, :], 512, n)
                for t in range(3):
                    n = P if t < 2 else NS
                    evacuate(("vtok", l, t), vt[0:n, t, :], 512, n)
                for h in range(MH):
                    b = bank(("bM", l, h))
                    act.wait_ge(sem("masked"), MH * l + h + 1)
                    act.wait_ge(sem("cols_ready"), l + 1)
                    step(nc.scalar.activation(WT[:, h, 0:256], b[:, 0:256], ACT.Exp, bias=cols[:, 0, h:h + 1], scale=-1.0))
                    step(nc.scalar.activation(WT[:, h, 256:384], b[:, 256:384], ACT.Exp, bias=cols[:, 1, h:h + 1], scale=-1.0))
                    step(nc.scalar.activation(WT[0:NS, h, 384:416], b[0:NS, 384:416], ACT.Exp,
                                              bias=cols[0:NS, 2, h:h + 1], scale=-1.0), A)
                    if h % 2:
                        ada_mid(l, 6 + h // 2)
                for t in range(2):
                    for j in range(2 * (t + 1)):
                        if t == 0:
                            b = product(act, ("pT", l, t, j))
                            step(nc.scalar.activation(PT[:, 4 * j:4 * j + 4, 0, :], b.rearrange("p (h q) -> p h q", h=4), ACT.Copy), A)
                        else:
                            b = product(act, ("pT", l, t, j))
                            step(nc.scalar.activation(PT[:, 2 * j:2 * j + 2, :, :].rearrange("p h b q -> p (h b q)"), b, ACT.Copy), A)
                    b = product(act, ("o", l, t))
                    step(nc.scalar.activation(mixT[:, 0:4, t * P:(t + 1) * P], b.rearrange("p (j q) -> p j q", j=4), ACT.Copy), A)
                    ada_mid(l, 8 + t)
                for n in range(A_KV):
                    b = product(act, ("spT", l, n))
                    step(nc.scalar.activation(PTs[:, n, 0, :], b[:, 0:P], ACT.Copy))
                    step(nc.scalar.activation(PTs[0:NS, n, 1, :], b[0:NS, P:2 * P], ACT.Copy), A)
                b = product(act, ("o", l, 2))
                step(nc.scalar.activation(mixT[:, 0:4, SB], b[:, 0:P].rearrange("p (j q) -> p j q", j=4), ACT.Copy), A)
                for h in range(MH):
                    for j in range(2):
                        b = product(act, ("CT", l, h, j))
                        step(nc.scalar.activation(CT[:, h % 2, 4 * j:4 * j + 4, :].rearrange("p b k -> p (b k)"), b, ACT.Copy), A)
                    evacuate(("num", l, h), eh[:, h, :], TOK)
                    step(nc.scalar.activation(WT[:, h, 0:TOK], eh[:, h, :], ACT.Square), "hm_squares_ready")
                    if h % 2 == 0:
                        ada_mid(l, 10 + h // 2)
                step(nc.scalar.activation(region1[:, OM:OM + 4, :], region1[:, OM:OM + 4, :], ACT.Sigmoid), "sigmoid_done")
                step(nc.scalar.activation(act_scratch, eps_t[:, 0:1], ACT.Sqrt))
                act.wait_ge(sem("head_squares_ready"), l + 1)
                step(nc.scalar.activation(head_rstd[:, :], head_ssq[:, :, :].rearrange("p t h -> p (t h)"), ACT.Sqrt,
                                          bias=eps_t[:, 0:1], scale=1.0 / MD), "head_root_done")
                evacuate(("Cp", l), PTs_flat, 512)
                evacuate(("np", l), kcT_flat[0:1, 0:512], 512, 1)
                evacuate(("nnr", l), nrow, P, NS)
                for j in range(2):
                    evacuate(("cvr", l, j), pe_tok[0:27, 512 * j:512 * j + 512], 512, 27)
                act.wait_ge(*drain_of(("out", l, KD - 1)))
                squares(SB)
                root(("ss2", l, "S"), rstd[:, SB], D)
                squares(ST)
                for j in range(4):
                    evacuate(("ky", l, j), keyT[:, 4 * j:4 * j + 4, :].rearrange("p m k -> p (m k)"), 512)
                for m in QUERY_TILES:
                    if m == QUERY_TILES[2]:
                        root(("ss2", l, "T"), rstd[:, ST], D, False)
                    evacuate(("qpS", l, m), query_rows[:, m, :], P)
                b = product(act, ("qST", l))
                step(nc.scalar.activation(region1[:, :, SB], b.rearrange("p (m t) -> p m t", m=16), ACT.Copy), A)
                modulate(l, 1)
                for j in range(2):
                    evacuate(("h2", l, 2, j), h2tok[:, 2, 512 * j:512 * j + 512], 512)
                def queries(tile):
                    for j in range(4):
                        evacuate(("qp", l, 4 * tile + j), region1[:, 4 * tile + j, ST], SEQ)
                        if tile == 0 and j == 1:
                            gate_exp(l, 1, slice(0, 2))
                for tile in range(3):
                    queries(tile)
                for g in TILES:
                    base = first_slot[l, g] // K
                    if g == "S":
                        expert_unit(base, 0, l == 0)
                        gate_exp(l, 2, slice(0, 4))
                        for t in (0, 1):
                            for j in range(2):
                                evacuate(("h2", l, t, j), h2tok[:, t, 512 * j:512 * j + 512], 512)
                        queries(3)
                        expert_unit(base + 1, 1, l == 0)
                    elif g == "T0":
                        for n in range(8):
                            expert_unit(base + n, n % 2, False)
                            if n == 0:
                                gate_exp(l, 3, slice(4, 8))
                            if n == 5:
                                gate_exp(l, 4, slice(0, 8))
                            if 1 <= n < 3 and l + 1 < DEPTH:
                                ada(l + 1, n - 1)
                    else:
                        with act.Fori(0, UNITS[g] // 2) as i:
                            for half in range(2):
                                expert_unit(base + 2 * i + half, half, False)
                    act.wait_ge(sem("v_row_used"), first_slot[l, g] + UNITS[g] * K)
                    step(nc.scalar.activation(pe_tok[:, :], acc[:, :, :].rearrange("p c d -> p (c d)"), ACT.Copy), "experts_summed")
            act.wait_ge(*drain_of(("pt", DEPTH - 1, TILES[-1], 1)))
            squares()
            root(("ssf",), rstd[:, :], D)
            act.wait_ge(sem("xn_ready"), 2 * DEPTH + 1)
            for k in range(KD):
                step(nc.scalar.activation(hT[:, k, :], qks[:, k, :], ACT.Copy, scale=prm[:, 0, R_NFIN + k:R_NFIN + k + 1]), "y_ready")
            for j in range(2):
                for t in range(3):
                    n = P if t < 2 else NS
                    evacuate(("y", t, j), x_tok[0:n, t, 512 * j:512 * j + 512], 512, n)

        @block.tensor
        def _(pe):
            mm, tr = nc.tensor.matmul, nc.tensor.transpose

            def done(ins):
                ins.then_inc(product_ready, 1)

            def transposes(key, parts):
                b = claim(pe, key)
                for c0, src in parts:
                    n, w = src.shape[0], src.shape[1]
                    ins = tr(b[0:w, c0:c0 + n], src, ident[0:n, 0:n])
                done(ins)

            def sum_squares(key, src, chunks):
                b = claim(pe, key)[:, 0:src.shape[-1]]
                for k in range(chunks):
                    ins = mm(b, ones, src[:, k, :] if chunks > 1 else src, start=k == 0, stop=k == chunks - 1)
                done(ins)

            used = 0

            def weight_tile():
                nonlocal used
                pe.wait_ge(sem(f"weights_loaded_{used % WSLOTS}"), 16 * (used // WSLOTS + 1))
                used += 1
                return wring[:, (used - 1) % WSLOTS, :, :]

            def project(key, w, c, src, n=P, chunks=None, heads=None):
                b = claim(pe, key)
                for k in range(KD):
                    if chunks is not None:
                        pe.wait_ge(sem("h_ready"), chunks + k + 1)
                    if heads is not None and k >= KD - MH:
                        pe.wait_ge(sem("mlstm_out_ready"), heads + k - (KD - MH) + 1)
                    ins = mm(b[0:n, 0:src.shape[-1]], w[:, k, c:c + n], src[:, k, :], start=k == 0, stop=k == KD - 1)
                done(ins)

            def release(key):
                pe.wait_ge(product_ready, nth[key] + 1)
                pe.sem_inc(sem("weights_used"), 1)

            def spread_columns(b, rows, w):
                for k in range(KD):
                    for j in range(4):
                        ins = mm(b[NS * j:NS * j + NS, 0:P], rows[:, k, :], w[:, k, P * j:P * j + P],
                                 start=k == 0, stop=k == KD - 1, skip_group_check=True)
                done(ins)

            def ada_tile(l, m):
                w = weight_tile()
                spread_columns(claim(pe, ("ada", l, m)), cT[:, :, :], w)
                release(("ada", l, m))

            def ada_turned(l, i, rows):
                pe.wait_ge(*drain_of(("ada", l, 2 * i + 1)))
                transposes(("adaT", l, i), [(P * r, rows[:, r, :]) for r in range(2)])

            def ada(l, i):
                ada_tile(l, 2 * i)
                ada_tile(l, 2 * i + 1)
                ada_turned(l, i, ada_rows)

            pe.wait_ge(sem("first_loaded"), 48)
            pe.wait_ge(sem("c_silu"), 1)
            transposes(("c",), [(NC * k, c_tok[:, P * k:P * k + P]) for k in range(KD)])
            pe.wait_ge(*drain_of(("c",)))
            for m in range(2):
                ada_tile(0, m)
            pe.wait_ge(sem("setup_loaded"), 16 * setup_loads)
            for l in range(DEPTH):
                transposes(("params", l), [(0, prm_rows[:, l, :])])
            for k in range(KD):
                transposes(("x", k), [(P * t, x_tok[0:P if t < 2 else NS, t, P * k:P * k + P]) for t in range(3)])
            ada_turned(0, 0, ada_rows)
            ada(0, 1)
            for l in range(DEPTH):
                pe.wait_ge(sem("conv_state_loaded"), 16 * (l + 1))
                transposes(("cvs", l), [(24 * k, pe_tok[0:24, P * k:P * k + P]) for k in range(KD)])
                pe.wait_ge(sem("squares_ready"), 3 * l + 1)
                sum_squares(("ss1", l), hT, KD)
                if l == 0:
                    pe.wait_ge(sem("rel_spread"), A_HEADS)
                    for h in range(A_HEADS):
                        b = claim(pe, ("rel", h))
                        done(mm(b[:, 0:SKEW], relb[:, h, :], hot, start=True, stop=True))
                pe.wait_ge(sem("h_sample_ready"), 2 * l + 1)
                def project_tile(tile):
                    w = weight_tile()
                    for j in range(4 if tile < 5 else 2):
                        project(("proj", l, 4 * tile + j), w, P * j, hT,
                                chunks=KD * 2 * l if tile == PROJ_TILES[0] and j == 0 else None)
                    if tile == 5:
                        project(("proj", l, "ig"), w, 2 * P, hT, MH)
                        project(("proj", l, "fg"), w, 2 * P + MH, hT, MH)
                    release(("proj", l, "fg" if tile == 5 else 4 * tile + 3))

                for tile in PROJ_TILES[:-1]:
                    project_tile(tile)
                pe.wait_ge(*drain_of(("proj", l, KA + 1)))
                tiles = [(slice(P * t, min(P * t + P, TOK)), t) for t in range(3)]
                for tok, t in tiles:
                    transposes(("kvtok", l, t), [(P * j, region1[:, KA + j, tok]) for j in range(2)])
                pe.wait_ge(sem("kc_loaded"), 16 * (l + 1))
                for j in range(2):
                    transposes(("kct", l, j), [(P * b, kc[:, 4 * j + b, :]) for b in range(4)])
                pe.wait_ge(sem("k_doubled"), 64 * (l + 1))
                for t in range(2):
                    for j in range(4):
                        b = claim(pe, ("sc", l, t, j))
                        h0 = j // 2 * GROUP + j % 2
                        for i, h in enumerate((h0, h0 + 2)):
                            half = slice(h % 2 * DH, (h % 2 + 1) * DH)
                            c0 = P if t == 0 else 0
                            ins = mm(b[:, 256 * i + c0:256 * i + 256], region1[half, h // 2, P * t:P * t + P],
                                     kdup[half, h // GROUP, P * (t - 1) + c0:P * (t + 1)], start=True, stop=True)
                        done(ins)
                    if t == 0:
                        ada_tile(l, 4)
                pe.wait_ge(sem("q_moved"), 128 * (l + 1))
                for n in range(A_KV):
                    half = slice(n * DH, (n + 1) * DH)
                    pe.wait_ge(*drain_of(("kct", l, 1)))
                    bk = claim(pe, ("ssT", l, n))
                    out = bk[:, 0:P].rearrange("p (g b s) -> p g b s", g=GROUP, b=DEC_B)
                    for b in range(DEC_B):
                        ins = mm(out[:, :, b, :], kcT[half, b, :], qd[half, :, DEC_S * b:DEC_S * b + DEC_S], start=True, stop=True)
                    done(ins)
                ada_tile(l, 5)
                for n in range(A_KV):
                    half = slice(n * DH, (n + 1) * DH)
                    pe.wait_ge(*drain_of(("ssT", l, n)))
                    b = claim(pe, ("ss", l, n))
                    tr(b[:, 0:P], sT[:, n, :], ident)
                    done(mm(b[:, P:P + NS], qd[half, :, :].rearrange("p g t -> p (g t)"), kdup[half, n, SB], start=True, stop=True))
                project_tile(PROJ_TILES[-1])
                pe.wait_ge(sem("k_scaled"), l + 1)
                for tok, t in tiles:
                    transposes(("ktok", l, t), [(P * h, qks[:, 4 + h, tok]) for h in range(MH)])
                pe.wait_ge(*drain_of(("proj", l, 17)))
                for tok, t in tiles:
                    transposes(("vtok", l, t), [(P * h, region1[:, VM + h, tok]) for h in range(MH)])
                pe.wait_ge(sem("rows_done"), 3 * (l + 1))
                b = claim(pe, ("cols", l))
                for tok, t in tiles:
                    w = P if t < 2 else NS
                    for j, r in enumerate(("a", "wl", "e")):
                        ins = tr(b[0:w, 12 * t + 4 * j:12 * t + 4 * j + 4], row[r][:, tok], ident[0:MH, 0:MH])
                done(ins)
                pe.wait_ge(sem("n_loaded"), 16 * (l + 1))
                transposes(("nT", l), [(0, nrow)])

                def select(h):
                    return ident[0:MH, h:h + 1].broadcast_to([MH, P])

                b = claim(pe, ("bA", l))
                for h in range(MH):
                    ins = mm(b[:, NS * h:NS * h + NS], select(h), row["aw"], start=True, stop=True)
                done(ins)
                for h in range(MH):
                    b = claim(pe, ("bM", l, h))
                    mm(b[:, 0:256], select(h), row["M"][:, 0:256], start=True, stop=False, skip_group_check=True)
                    mm(b[:, 256:384], select(h), row["M"][:, 128:256], start=False, stop=False, skip_group_check=True)
                    done(mm(b[:, 384:416], select(h), row["M"][:, 256:288], start=False, stop=True, skip_group_check=True))
                    b = claim(pe, ("qk", l, h))
                    mm(b[:, 0:256], qks[:, 4 + h, 0:128], qks[:, h, 0:256], start=True, stop=True)
                    mm(b[:, 256:384], qks[:, 4 + h, 128:256], qks[:, h, 128:256], start=True, stop=True)
                    done(mm(b[0:NS, 384:416], qks[:, 4 + h, SB], qks[:, h, SB], start=True, stop=True))
                    if h % 2:
                        ada_tile(l, 6 + h // 2)
                for t in range(2):
                    pe.wait_ge(sem("probs_ready"), 3 * l + t + 1)
                    for j in range(2 * (t + 1)):
                        if t == 0:
                            transposes(("pT", l, t, j), [(P * i, S0[:, 4 * j + i, :]) for i in range(4)])
                        else:
                            transposes(("pT", l, t, j), [(P * (2 * i + kb), S1[:, 2 * j + i, P * kb:P * kb + P])
                                                         for i in range(2) for kb in range(2)])
                    pe.wait_ge(*drain_of(("pT", l, t, 2 * t + 1)))
                    b = claim(pe, ("o", l, t))
                    for h in range(A_HEADS):
                        half, v0 = slice(h % 2 * DH, (h % 2 + 1) * DH), P + h // GROUP * DH
                        for kb in range(t + 1):
                            ins = mm(b[half, P * (h // 2):P * (h // 2) + P], kvt[:, kb, v0:v0 + DH], PT[:, h, kb, :],
                                     start=kb == 0, stop=kb == t)
                    done(ins)
                    ada_tile(l, 8 + t)
                pe.wait_ge(sem("probs_ready"), 3 * l + 3)
                for n in range(A_KV):
                    transposes(("spT", l, n), [(0, SS[:, n, 0:P]), (P, SS[:, n, P:P + NS])])
                pe.wait_ge(*drain_of(("spT", l, 1)))
                pe.wait_ge(sem("vc_loaded"), 16 * (l + 1))
                bk = claim(pe, ("o", l, 2))
                out = bk[:, 0:P].rearrange("p (j t) -> p j t", j=4)
                for n in range(A_KV):
                    v0 = n * DH
                    for odd in range(2):
                        half = slice(odd * DH, (odd + 1) * DH)
                        to = out[half, 2 * n:2 * n + 2, :]
                        new = PTs[0:NS, n, 1, :].rearrange("p (g t) -> p g t", g=GROUP)[:, odd::2, :]
                        old = PTs[:, n, 0, :].rearrange("p (g t) -> p g t", g=GROUP)[:, odd::2, :]
                        mm(to, kvt[0:NS, 2, P + v0:P + v0 + DH], new, start=True, stop=False, skip_group_check=True)
                        for b in range(DEC_B):
                            t = slice(DEC_S * b, DEC_S * b + DEC_S)
                            ins = mm(to[:, :, t], vc[:, b, v0:v0 + DH], old[:, :, t], start=False, stop=b == DEC_B - 1, skip_group_check=True)
                done(ins)
                pe.wait_ge(*drain_of(("vtok", l, 2)))
                pe.wait_ge(*drain_of(("ktok", l, 2)))
                pe.wait_ge(*drain_of(("qk", l, MH - 1)))
                pe.wait_ge(sem("q_weighted"), l + 1)
                for h in range(MH):
                    pe.wait_ge(sem(f"C_loaded_{h % 2}"), 16 * (2 * l + h // 2 + 1))
                    for j in range(2):
                        transposes(("CT", l, h, j), [(P * b, C_sb[:, h % 2, 4 * j + b, :]) for b in range(4)])
                    b = claim(pe, ("den", l, h))
                    mm(b[:, 0:1], WT[:, h, 0:128], ones[:, 0:1], start=True, stop=True)
                    mm(b[:, 1:2], WT[:, h, 128:256], ones[:, 0:1], start=True, stop=False)
                    mm(b[:, 1:2], WT[:, h, 256:384], ones[:, 0:1], start=False, stop=True)
                    mm(b[0:NS, 2:3], WT[0:NS, h, 384:416], ones[0:NS, 0:1], start=True, stop=False)
                    done(mm(b[0:NS, 2:3], nqa[:, h, :], ones[:, 0:1], start=False, stop=True))
                    v = slice(P * h, P * h + P)
                    pe.wait_ge(*drain_of(("CT", l, h, 1)))
                    b = claim(pe, ("num", l, h))
                    mm(b[:, 0:256], vt[:, 0, v], WT[:, h, 0:256], start=True, stop=False, skip_group_check=True)
                    mm(b[:, 128:256], vt[:, 1, v], WT[:, h, 256:384], start=False, stop=False, skip_group_check=True)
                    mm(b[:, SB], vt[0:NS, 2, v], WT[0:NS, h, 384:416], start=False, stop=False, skip_group_check=True)
                    for s in range(DEC_B):
                        t = slice(DEC_S * s, DEC_S * s + DEC_S)
                        ins = mm(b[:, 256 + DEC_S * s:256 + DEC_S * (s + 1)], CT[:, h % 2, s, :], qa[:, h, t],
                                 start=False, stop=s == DEC_B - 1, skip_group_check=True)
                    done(ins)
                    pe.wait_ge(sem("weighted_k_ready"), MH * l + h + 1)
                    for j in range(2):
                        b = claim(pe, ("Cs", l, h, j))
                        done(mm(b, vt[0:NS, 2, v], wk[:, 4 * j:4 * j + 4, :].rearrange("p b k -> p (b k)"), start=True, stop=True))
                    if h % 2 == 0:
                        ada_tile(l, 10 + h // 2)
                pe.wait_ge(sem("hm_squares_ready"), MH * (l + 1))
                b = claim(pe, ("hss", l))
                for tok, t in tiles:
                    for h in range(MH):
                        ins = mm(b[0:P if t < 2 else NS, MH * t + h:MH * t + h + 1], WT[:, h, tok], ones[:, 0:1], start=True, stop=True)
                done(ins)
                pe.wait_ge(sem("weighted_v_ready"), l + 1)
                b = claim(pe, ("Cp", l))
                for h in range(MH):
                    for t in range(2):
                        ins = mm(b[:, P * h:P * h + P], wv[:, t, h, :], kt[:, t, P * h:P * h + P], start=t == 0, stop=t == 1)
                done(ins)
                pe.wait_ge(sem("head_rstd_ready"), l + 1)
                for h in range(MH):
                    b = claim(pe, ("hr", l, h))
                    for tok, t in tiles:
                        n = P if t < 2 else NS
                        ins = mm(b[:, tok], head_rstd[0:n, MH * t + h:MH * t + h + 1].broadcast_to([n, P]), ident[0:n, 0:n],
                                 start=True, stop=True)
                    done(ins)
                b = claim(pe, ("np", l))
                for h in range(MH):
                    for t in range(2):
                        ins = mm(b[0:1, P * h:P * h + P], cols[:, t, 4 + h:5 + h], kt[:, t, P * h:P * h + P], start=t == 0, stop=t == 1)
                done(ins)
                b = claim(pe, ("nn", l))
                for h in range(MH):
                    ins = mm(b[:, DEC_B * h:DEC_B * h + DEC_B], kt[0:NS, 2, P * h:P * h + P], WB[:, h, :], start=True, stop=True)
                done(ins)
                for i in range(2, 6):
                    ada_turned(l, i, ada_rows_mid[:, 2 * i - 4:2 * i - 2, :])
                pe.wait_ge(*drain_of(("nn", l)))
                transposes(("nnr", l), [(0, nnT)])
                pe.wait_ge(sem("conv_rows_ready"), l + 1)
                for j in range(2):
                    transposes(("cvr", l, j), [(P * k, cvo[:, 4 * j + k, :]) for k in range(4)])
                for tile in range(2):
                    w = weight_tile()
                    for j in range(4):
                        project(("out", l, 4 * tile + j), w, P * j, mixT, heads=MH * l if tile == 0 and j == 0 else None)
                    release(("out", l, 4 * tile + 3))
                pe.wait_ge(sem("squares_ready"), 3 * l + 2)
                sum_squares(("ss2", l, "S"), hT[:, :, SB], KD)
                pe.wait_ge(sem("keys_loaded"), 16 * (l + 1))
                for j in range(4):
                    transposes(("ky", l, j), [(P * i, keys_raw[:, 4 * j + i, :]) for i in range(4)])
                pe.wait_ge(sem("h_sample_ready"), 2 * l + 2)
                pe.wait_ge(sem("query_weights_loaded"), 32 * (l + 1))
                query_weights = {m: query_w[:, i] for i, m in enumerate(QUERY_TILES[:2])}
                for tile in QUERY_TILES:
                    if tile == QUERY_TILES[2]:
                        pe.wait_ge(sem("squares_ready"), 3 * l + 3)
                        sum_squares(("ss2", l, "T"), hT[:, :, ST], KD)
                    if tile not in query_weights:
                        query_weights[tile] = weight_tile()
                    spread_columns(claim(pe, ("qpS", l, tile)), hT[:, :, SB], query_weights[tile])
                pe.wait_ge(*drain_of(("qpS", l, QUERY_TILES[-1])))
                transposes(("qST", l), [(P * m, query_rows[:, m, :]) for m in range(4)])
                pe.wait_ge(*drain_of(("qST", l)))
                b = claim(pe, ("rs", l, "S", 0))
                for q in range(4):
                    for i in range(4):
                        m = 4 * q + i
                        ins = mm(b[NS * q:NS * q + NS, P * i:P * i + P], region1[:, m, SB], keyT[:, m, :], start=True, stop=True)
                done(ins)

                pe.wait_ge(sem("h_repeated"), l + 1)
                for j in range(2):
                    transposes(("h2", l, 2, j), [(P * k, hS4[:, 4 * j + k, :, :].rearrange("p q t -> p (q t)")) for k in range(4)])

                def key_scores(g, quads):
                    for j in quads:
                        b = claim(pe, ("rs", l, g, j))
                        for i in range(4):
                            m = 4 * j + i
                            ins = mm(b[:, P * i:P * i + P], region1[:, m, COL[g]:COL[g] + P], keyT[:, m, :], start=True, stop=True)
                        done(ins)

                def queries(tile):
                    for j in range(4):
                        project(("qp", l, 4 * tile + j), query_weights[tile], P * j, hT[:, :, ST])
                    if tile in QUERY_TILES[2:]:
                        release(("qp", l, 4 * tile + 3))

                def weighted_rows(n, half):
                    for k in range(K):
                        pe.wait_ge(sem("diag_ready"), n * K + (k + 1))
                        pe.wait_ge(v_loaded[k % RV], n * (16 * K // RV) + 16 * (k // RV + 1))
                        for c in range(2):
                            ins = mm(acc[:, c, :], diag[:, k % DIAGS, :], v_ring[:, k % RV, 512 * c:512 * c + 512],
                                     start=False, stop=False, skip_group_check=True)
                        ins.then_inc(sem("v_row_used"), 1)

                pe.wait_ge(sem("h_ready"), KD * (2 * l + 2))
                for tile in range(3):
                    queries(tile)
                pe.wait_ge(*drain_of(("qp", l, 7)))
                key_scores("T0", [0, 1])
                for g in TILES:
                    base = first_slot[l, g] // K
                    if (l, g) != (0, TILES[0]):
                        pe.wait_ge(sem("experts_summed"), 3 * l + TILES.index(g))
                    for c in range(2):
                        for half in range(2):
                            mm(acc[:, c, 256 * half:256 * half + 256], zeros[:, :], cst[:, 0:256],
                               start=True, stop=False, skip_group_check=True)
                    if g == "S":
                        weighted_rows(base, 0)
                        for t in (0, 1):
                            for j in range(2):
                                transposes(("h2", l, t, j), [(P * k, hT[:, 4 * j + k, P * t:P * t + P]) for k in range(4)])
                        pe.wait_ge(*drain_of(("qp", l, 11)))
                        key_scores("T0", [2])
                        queries(3)
                        weighted_rows(base + 1, 1)
                    elif g == "T0":
                        pe.wait_ge(*drain_of(("qp", l, 15)))
                        key_scores("T0", [3])
                        for n in range(8):
                            weighted_rows(base + n, n % 2)
                            if n < 4:
                                key_scores("T1", [n])
                            if 1 <= n < 3 and l + 1 < DEPTH:
                                ada(l + 1, n - 1)
                    else:
                        with pe.Fori(0, UNITS[g] // 2) as i:
                            for half in range(2):
                                weighted_rows(base + 2 * i + half, half)
                    pe.wait_ge(sem("experts_summed"), 3 * l + TILES.index(g) + 1)
                    for j in range(2):
                        b = claim(pe, ("pt", l, g, j))
                        for k in range(4):
                            src = pe_tok[:, 512 * j + P * k:512 * j + P * k + P]
                            if g == "S":
                                ins = mm(b[:, NS * k:NS * k + NS], src, cst[:, C_SUM:C_SUM + NS], start=True, stop=True)
                            else:
                                ins = tr(b[:, P * k:P * k + P], src, ident)
                        done(ins)
            pe.wait_ge(sem("squares_ready"), 3 * DEPTH + 1)
            sum_squares(("ssf",), hT, KD)
            for j in range(2):
                pe.wait_ge(sem("y_ready"), 4 * j + 4)
                for t in range(3):
                    n = P if t < 2 else NS
                    transposes(("y", t, j), [(P * k, hT[:, 4 * j + k, P * t:P * t + n]) for k in range(4)])

        @block.vector
        def _(dve):
            step = Steps(dve, "dve_step")
            V = drained["V"]
            tt, ts, stt = nc.vector.tensor_tensor, nc.vector.tensor_scalar, nc.vector.scalar_tensor_tensor
            copy, reduce = nc.vector.tensor_copy, nc.vector.tensor_reduce

            def normalise(key, cols):
                dve.wait_ge(*drain_of(key))
                step(nc.vector.reciprocal(rstd[:, cols], rstd[:, cols]))
                return tt(qks[:, :, cols], xT[:, :, cols], bc(rstd[:, cols], 1, [P, KD, cols.stop - cols.start]), ALU.mult)

            def modulate_samples(w):
                hs, xs = by_sample(hT[:, :, SB]), by_sample(qks[:, :, SB])
                full = [P, KD, DEC_B, DEC_S]
                step(tt(hs, xs, bc(modA[:, w, :, 1:NC], 3, full), ALU.mult))
                step(tt(hs, hs, bc(modT[:, 24 * w:24 * w + KD, 1:NC], 3, full), ALU.add), "h_sample_ready")

            def scales(w, r):
                step(stt(modA[:, w], modT[:, 24 * w + KD:24 * w + 2 * KD, :], 1.0,
                         bc(prm[:, l, r:r + KD], 2, [P, KD, NC]), ALU.add, ALU.mult))

            def gated_add(modT, b, k0, n, gate0):
                full = [P, n, DEC_B, DEC_S]
                t = tmp[:, 0:n * NS].rearrange("p (k b s) -> p k b s", k=n, b=DEC_B)
                xs = by_sample(xT[:, k0:k0 + n, SB])
                step(tt(t, b.rearrange("p (k b s) -> p k b s", k=n, b=DEC_B), bc(modT[:, gate0 + k0:gate0 + k0 + n, 1:NC], 3, full), ALU.mult))
                step(tt(xs, xs, t, ALU.add), V)

            def softmax_max(i, S, sink):
                nh = S.shape[1]
                st = stat[i][:, :, 0:nh]
                step(reduce(st[:, 0, :], S, AX, ALU.max))
                step(tt(st[:, 0, :], st[:, 0, :], sink, ALU.max))
                step(ts(st[:, 1, :], st[:, 0, :], -1.0, None, ALU.mult))
                step(tt(st[:, 2, :], sink, st[:, 1, :], ALU.add), "exp_wanted")

            def softmax_norm(l, i, S):
                nh = S.shape[1]
                st = stat[i][:, :, 0:nh]
                dve.wait_ge(sem("exp_done"), 3 * l + i + 1)
                step(tt(st[:, 4, :], st[:, 3, :], st[:, 2, :], ALU.add))
                step(nc.vector.reciprocal(st[:, 4, :], st[:, 4, :]))
                step(tt(S, S, bc(st[:, 4, :], 2, list(S.shape)), ALU.mult), "probs_ready")

            def top16(vals, idx, src, width):
                r = rep[:, 0:width]
                step(nc.vector.max(vals[:, 0:8], src))
                step(nc.vector.max_index(idx[:, 0:8], vals[:, 0:8], src))
                step(nc.vector.match_replace(r, vals[:, 0:8], src, -3e38))
                step(nc.vector.max(vals[:, 8:16], r))
                return nc.vector.max_index(idx[:, 8:16], vals[:, 8:16], r)

            def route_heads(l, g, j):
                b = product(dve, ("rs", l, g, j))
                for m in range(4):
                    h, c = 2 * j + m // 2, m % 2
                    step(top16(s_top[:, h, c, :], i_top[:, h, c, :], b[:, P * m:P * m + P], P), V if m == 3 else None)
                if g == "S":
                    dve.wait_ge(*drain_of(("h2", l, 2, 1)))
                for h in (2 * j, 2 * j + 1):
                    full = [P, TOPK, TOPK]
                    step(tt(cand[:, h, :].rearrange("p (i j) -> p i j", i=TOPK), bc(s_top[:, h, 0, :], 2, full),
                            bc(s_top[:, h, 1, :], 1, full), ALU.add))
                    step(top16(best[:, h, :], pos[:, h, :], cand[:, h, :], TOPK * TOPK))

            def center_gates(heads):
                nh = heads.stop - heads.start
                bst, mx = best[:, heads, :], rep[:, 0:nh]
                step(copy(mx, bst[:, :, 0]))
                step(tt(bst, bst, bc(mx, 2, [P, nh, TOPK]), ALU.subtract), "gate_exp_wanted")

            def route_gates(l, g, routed, heads):
                nh = heads.stop - heads.start
                slots = slice(heads.start * TOPK, heads.stop * TOPK)
                gates = g_all[:, TI[g], slots].rearrange("p (h k) -> p h k", h=nh)
                bst, mx = best[:, heads, :], rep[:, 0:nh]
                pi = pij[:, :, heads, :]
                pu = pi.bitcast(U32)
                step(ts(pu[:, 0], pos[:, heads, :], 4, None, ALU.logical_shift_right))
                step(ts(pu[:, 1], pos[:, heads, :], 15, None, ALU.bitwise_and))
                for c in range(2):
                    step(copy(pi[:, c], pu[:, c]))
                step(copy(i_topf[:, heads], i_top[:, heads]))
                full = [P, nh, TOPK, TOPK]
                hit = onehot[:, heads]
                iota = cst[:, C_IOTA:C_IOTA + TOPK].unsqueeze(1).unsqueeze(1).broadcast_to(full)
                for c in range(2):
                    step(tt(hit, iota, bc(pi[:, c], 3, full), ALU.is_equal))
                    step(tt(hit, hit, bc(i_topf[:, heads, c, :], 2, full), ALU.mult))
                    step(reduce(pi[:, c], hit, AX, ALU.add))
                step(stt(pi[:, 0], pi[:, 0], float(N_KEYS), pi[:, 1], ALU.mult, ALU.add))
                dve.wait_ge(sem("gate_exp_done"), 4 * l + routed)
                step(reduce(mx, bst, AX, ALU.add))
                step(nc.vector.reciprocal(mx, mx))
                step(tt(gates, bst, bc(mx, 2, [P, nh, TOPK]), ALU.mult))
                step(ts(idx_all[:, TI[g], slots].rearrange("p (h k) -> p h k", h=nh), pi[:, 0],
                        float(l * N_EXPERTS), None, ALU.add), "idx_ready")

            def expert_unit(g, i, half, n):
                for k in range(K):
                    dve.wait_ge(u_loaded[k % RU], n * (16 * K // RU) + 16 * (k // RU + 1))
                    row_ = u_ring[:, k % RU, :]
                    nc.vector.tensor_tensor_reduce(out=row_, in0=row_, in1=h2tok[:, TI[g], :], scale=1.0, scalar=0.0,
                                                   op0=ALU.mult, op1=ALU.add, accum_out=dots[:, half, k:k + 1])\
                        .then_inc(sem("u_row_used"), 1)
                dve.wait_ge(sem("gelu_ready"), n + 1)
                tt(wts[:, half, :], gelus[:, half, :], g_all[:, TI[g], bass.ds(i * 2 * K + half * K, K)], ALU.mult)\
                    .then_inc(sem("expert_weights_ready"), 1)

            step(nc.vector.memset(eps_t[:, :], EPS), "eps_ready")
            step(nc.vector.memset(zeros[:, :], 0.0))
            step(nc.vector.memset(cols, 0.0))
            step(nc.vector.memset(head_den[:, :, :], 1.0))
            step(nc.vector.memset(head_ssq[:, :, :], 1.0))
            step(nc.vector.memset(cT[:, :, :], 0.0))
            step(copy(cT[:, :, 0:NC], product(dve, ("c",))[:, 0:KD * NC].rearrange("p (k c) -> p k c", k=KD)), V)
            dve.wait_ge(sem("setup_loaded"), 16 * setup_loads)
            for l in range(DEPTH):
                step(copy(prm[:, l, :], product(dve, ("params", l))[:, 0:R_ROWS]), V)
            step(nc.vector.memset(relraw[32:33, :], -BIG))
            for h in range(A_HEADS):
                step(ts(relb[:, h, :], ones[0:33, :], relraw[:, h:h + 1], None, ALU.mult), "rel_spread")
            def ada(l, i):
                b = product(dve, ("adaT", l, i))
                step(tt(modT_all[:, l % 2, 8 * i:8 * i + 8, :], b[:, 0:2 * P].rearrange("p (j c) -> p j c", j=8)[:, :, 0:NC],
                        bc(prm[:, l, R_BADA + 8 * i:R_BADA + 8 * i + 8], 2, [P, 8, NC]), ALU.add), V)

            def add_experts(l, g):
                modT = modT_all[:, l % 2]
                for j in range(2):
                    b = product(dve, ("pt", l, g, j))
                    if g == "S":
                        gated_add(modT, b[:, 0:4 * NS], 4 * j, 4, 40)
                    else:
                        for k in range(4):
                            m, c = 4 * j + k, slice(COL[g], COL[g] + P)
                            step(stt(xT[:, m, c], b[:, P * k:P * k + P], modT[:, 40 + m, 0:1], xT[:, m, c], ALU.mult, ALU.add),
                                 V if k == 3 else None)

            for i in range(2):
                ada(0, i)
            for l in range(DEPTH):
                modT = modT_all[:, l % 2]
                scales(0, R_NMIX)
                step(nc.vector.memset(cin_p[:, :, 0:3], 0.0))
                b = product(dve, ("cvs", l))
                step(copy(cin_s[:, :, :, 0:3], b[:, 0:192].rearrange("p (k b r) -> p k b r", k=KD, b=DEC_B)), V)
                step(nc.vector.memset(tmp[:, 0:1], 0.0), "cin_padded")
                step(normalise(("ss1", l), slice(0, TOK)), "xn_ready")
                modulate_samples(0)
                b = product(dve, ("proj", l, "ig"))
                if l == 0:
                    dve.wait_ge(sem("rel_stored"), 16)
                step(ts(row["ig"], b[0:MH, 0:TOK], gate_bias[:, l, 0:1], None, ALU.add), V)
                b = product(dve, ("proj", l, "fg"))
                step(ts(row["e"], b[0:MH, 0:TOK], gate_bias[:, l, 1:2], None, ALU.add), V)
                step(stt(row["M"], row["e"], -1.0, row["e"], ALU.mult, ALU.max), "gate_abs_ready")
                step(ts(row["b"], row["e"], 0.0, None, ALU.min))
                dve.wait_ge(sem("gate_log_ready"), l + 1)
                step(tt(row["wl"], row["b"], row["M"], ALU.subtract))
                s4 = {r: by_sample(row[r][:, SB]) for r in ("ig", "b", "a", "M", "e", "wl")}
                one = ones[0:MH, 0:1].broadcast_to([MH, SEQ])
                step(nc.vector.tensor_tensor_scan(row["b"][:, ST], one, row["wl"][:, ST], 0.0, ALU.mult, ALU.add))
                step(copy(s4["b"][:, :, 0], s4["wl"][:, :, 0]))
                for s in range(1, DEC_S):
                    step(tt(s4["b"][:, :, s], s4["b"][:, :, s - 1], s4["wl"][:, :, s], ALU.add))
                step(tt(row["a"], row["ig"], row["b"], ALU.subtract))
                step(nc.vector.tensor_tensor_scan(row["M"][:, ST], row["a"][:, ST], row["a"][:, ST], 0.0, ALU.max, ALU.max))
                dve.wait_ge(sem("m_loaded"), 16 * (l + 1))
                for s in range(DEC_S):
                    step(tt(s4["M"][:, :, s], s4["a"][:, :, s], m_in if s == 0 else s4["M"][:, :, s - 1], ALU.max))
                step(tt(row["e"], row["b"], row["M"], ALU.add))
                step(copy(m_out[:, 0:1], row["e"][:, SEQ - 1:SEQ]))
                step(copy(m_out[:, 1:NC], s4["e"][:, :, DEC_S - 1]), "m_out_ready")
                step(ts(row["wl"][:, ST], row["a"][:, ST], row["M"][:, SEQ - 1:SEQ], None, ALU.subtract))
                full = [MH, DEC_B, DEC_S]
                step(tt(s4["wl"], s4["a"], bc(s4["M"][:, :, DEC_S - 1], 2, full), ALU.subtract))
                step(tt(by_sample(row["aw"]), bc(m_in, 2, full), s4["M"], ALU.subtract), "rows_wanted")
                for k in range(KD):
                    dve.wait_ge(*drain_of(("proj", l, 6 + k)))
                    for i in range(CONV_W):
                        tap = prm[:, l, R_CONVW + KD * i + k:R_CONVW + KD * i + k + 1]
                        cb = prm[:, l, R_CONVB + k:R_CONVB + k + 1]
                        for dst, src in ((qks[:, k, ST], cin_p[:, k, i:i + SEQ]),
                                         (by_sample(qks[:, k, SB]), cin_s[:, k, :, i:i + DEC_S])):
                            last = i == CONV_W - 1 and dst.shape[-1] == DEC_S
                            step(ts(dst, src, tap, cb, ALU.mult, ALU.add) if i == 0 else
                                 stt(dst, src, tap, dst, ALU.mult, ALU.add), "conv_done" if last else None)
                step(copy(cvo[:, :, 0:3], cin_p[:, :, SEQ:SEQ + 3]))
                step(copy(cvo[:, :, 3:27].rearrange("p k (b r) -> p k b r", b=DEC_B), cin_s[:, :, :, DEC_S:DEC_S + 3]), "conv_rows_ready")
                if l == 0:
                    dve.wait_ge(sem("bias_loaded"), 16 * (1 + A_HEADS))
                    own = bias_s[:, :, WINDOW:WINDOW + DEC_S]
                    step(copy(bias_s[:, :, WINDOW + DEC_S:].rearrange("p n (b s) -> p n b s", s=DEC_S),
                              bc(own, 2, [P, A_KV, DEC_B - 1, DEC_S])))
                    step(tt(bias_s[:, :, WINDOW:], bias_s[:, :, WINDOW:],
                            bc(cst[:, C_BLOCKADD:C_BLOCKADD + NS], 1, [P, A_KV, NS]), ALU.add))
                for t, S in ((0, S0), (1, S1)):
                    lo = P if t == 0 else 0
                    for j in range(4):
                        b = product(dve, ("sc", l, t, j)).rearrange("p (h k) -> p h k", h=2)[:, :, lo:]
                        h0 = j // 2 * GROUP + j % 2
                        step(stt(S[:, h0:h0 + 3:2, :], b, DH ** -0.5, bias[:, h0:h0 + 3:2, lo:], ALU.mult, ALU.add), V)
                    softmax_max(t, S, sink_p[:, l, :])
                    if t == 0:
                        dve.wait_ge(sem("silu_done"), 2 * (l + 1))
                        step(ts(qks[:, 4:8, :], qks[:, 4:8, :], MD ** -0.5, None, ALU.mult), "k_scaled")
                softmax_norm(l, 0, S0)
                softmax_norm(l, 1, S1)
                for n in range(A_KV):
                    b = product(dve, ("ss", l, n))
                    step(stt(SS[:, n, :], b[:, 0:160], DH ** -0.5, bias_s[:, n, :], ALU.mult, ALU.add), V)
                softmax_max(2, SS, sink_s[:, l, :])
                b = product(dve, ("cols", l))
                step(copy(cols[:, 0:2, :].rearrange("p t c -> p (t c)"), b[:, 0:24]))
                step(copy(cols[0:NS, 2, :], b[0:NS, 24:36]), V)
                step(nc.vector.memset(tmp[:, 0:1], 0.0), "cols_ready")
                full = [NS, MH, DEC_B]
                step(tt(WB, bc(cst[0:NS, C_BLOCK:C_BLOCK + DEC_B], 1, full), bc(cols[0:NS, 2, 4:8], 2, full), ALU.mult))
                step(copy(nT, product(dve, ("nT", l))[:, 0:NS]), V)
                step(copy(abc.rearrange("p h t -> p (h t)"), product(dve, ("bA", l))[:, 0:P]), V)
                step(tt(qa, qks[:, 0:4, SB], abc, ALU.mult))
                full = [P, MH, DEC_B, DEC_S]
                n_hb = nT.rearrange("p (b h) -> p h b", b=DEC_B)
                step(tt(by_sample(nqa), by_sample(qa), bc(n_hb, 3, full), ALU.mult), "q_weighted")
                def mask(h):
                    b = product(dve, ("bM", l, h))
                    diagonal = b.rearrange("p (i c) -> p i c", i=2)[:, :, 0:P]
                    step(tt(diagonal, diagonal, bc(cst[:, C_CAUSAL:C_CAUSAL + P], 1, [P, 2, P]), ALU.add))
                    step(tt(b[0:NS, 384:416], b[0:NS, 384:416], cst[0:NS, C_CAUSALS:C_CAUSALS + NS], ALU.add), "masked")

                mask(0)
                mask(1)
                softmax_norm(l, 2, SS)
                for h in range(MH):
                    if h + 2 < MH:
                        mask(h + 2)
                    b = product(dve, ("qk", l, h))
                    dve.wait_ge(*drain_of(("bM", l, h)))
                    step(tt(WT[:, h, 0:384], WT[:, h, 0:384], b[:, 0:384], ALU.mult))
                    step(tt(WT[0:NS, h, 384:416], WT[0:NS, h, 384:416], b[0:NS, 384:416], ALU.mult), V)
                dve.wait_ge(*drain_of(("vtok", l, 2)))
                dve.wait_ge(product_ready, nth["pT", l, 1, 3] + 1)
                for t in range(2):
                    step(tt(wv[:, t], vt[:, t, :].rearrange("p (h v) -> p h v", h=MH), bc(cols[:, t, 4:8], 2, [P, MH, MD]), ALU.mult),
                         "weighted_v_ready" if t else None)
                for h in range(MH):
                    dve.wait_ge(*drain_of(("ktok", l, 2)))
                    if h:
                        dve.wait_ge(product_ready, nth["Cs", l, h - 1, 1] + 1)
                    full = [NS, DEC_B, MD]
                    step(tt(wk, bc(kt[0:NS, 2, P * h:P * h + P], 1, full), bc(WB[:, h, :], 2, full), ALU.mult), "weighted_k_ready")
                    b = product(dve, ("den", l, h))
                    step(copy(head_den[:, 0:2, h], b[:, 0:2]))
                    step(copy(head_den[0:NS, 2, h:h + 1], b[0:NS, 2:3]), V)
                    decay = by_sample(abc[:, h, :])[:, :, DEC_S - 1]
                    step(tt(C_sb[:, h % 2], C_sb[:, h % 2], bc(decay, 2, [P, DEC_B, MD]), ALU.mult))
                    for j in range(2):
                        b = product(dve, ("Cs", l, h, j))
                        c = C_sb[:, h % 2, 4 * j:4 * j + 4, :].rearrange("p b k -> p (b k)")
                        step(tt(c, c, b, ALU.add), V)
                d, m_exp = head_den[:, :, :], cols[:, :, 8:12]
                step(tt(m_exp, d, m_exp, ALU.max))
                step(stt(d, d, -1.0, m_exp, ALU.mult, ALU.max))
                step(nc.vector.reciprocal(d, d))
                b = product(dve, ("hss", l))
                step(tt(head_ssq[:, 0:2, :], b[:, 0:8].rearrange("p (t h) -> p t h", t=2), d[:, 0:2, :], ALU.mult))
                step(tt(head_ssq[0:NS, 2, :], b[0:NS, 8:12], d[0:NS, 2, :], ALU.mult), V)
                step(tt(head_ssq[:, :, :], head_ssq[:, :, :], d, ALU.mult), "head_squares_ready")
                dve.wait_ge(sem("head_root_done"), l + 1)
                step(nc.vector.reciprocal(head_rstd[:, :], head_rstd[:, :]))
                step(tt(head_rstd[:, :], head_rstd[:, :], d.rearrange("p t h -> p (t h)"), ALU.mult), "head_rstd_ready")
                dve.wait_ge(sem("sigmoid_done"), l + 1)
                for h in range(MH):
                    b = product(dve, ("hr", l, h))
                    step(tt(eh[:, h, :], eh[:, h, :], b[:, 0:TOK], ALU.mult), V)
                    step(stt(mixT[:, 4 + h, :], eh[:, h, :], prm[:, l, R_MNORM + h:R_MNORM + h + 1], region1[:, OM + h, :],
                             ALU.mult, ALU.mult), "mlstm_out_ready")
                n_new = nnT.rearrange("p (b h) -> p h b", b=DEC_B)
                a_hb = abc.rearrange("p h (b s) -> p h b s", b=DEC_B)[:, :, :, DEC_S - 1]
                step(tt(n_new, n_hb, a_hb, ALU.mult))
                b = product(dve, ("nn", l))
                step(tt(n_new, n_new, b[:, 0:NS].rearrange("p (h b) -> p h b", h=MH), ALU.add), V)
                for i in range(2, 6):
                    ada(l, i)
                for m in range(KD):
                    b = product(dve, ("out", l, m))
                    step(stt(xT[:, m, ST], b[:, ST], modT[:, 16 + m, 0:1], xT[:, m, ST], ALU.mult, ALU.add))
                    gated_add(modT, b[:, SB], m, 1, 16)
                scales(1, R_NFFN)
                step(normalise(("ss2", l, "S"), SB))
                modulate_samples(1)
                step(normalise(("ss2", l, "T"), ST), "xn_ready")
                step(copy(hS4, bc(hT[:, :, SB], 2, [P, KD, 4, NS])), "h_repeated")
                route_heads(l, "S", 0)
                center_gates(slice(0, 2))
                route_gates(l, "S", 1, slice(0, 2))
                for g in TILES:
                    base = first_slot[l, g] // K
                    if g == "S":
                        expert_unit(g, 0, 0, base)
                        route_heads(l, "T0", 0)
                        route_heads(l, "T0", 1)
                        center_gates(slice(0, 4))
                        expert_unit(g, 0, 1, base + 1)
                        route_gates(l, "T0", 2, slice(0, 4))
                        route_heads(l, "T0", 2)
                    elif g == "T0":
                        for n in range(8):
                            expert_unit(g, n // 2, n % 2, base + n)
                            if n == 0:
                                add_experts(l, "S")
                                route_heads(l, "T0", 3)
                                center_gates(slice(4, 8))
                                route_gates(l, "T0", 3, slice(4, 8))
                            if 1 <= n < 5:
                                route_heads(l, "T1", n - 1)
                            if n == 5:
                                center_gates(slice(0, 8))
                                route_gates(l, "T1", 4, slice(0, 8))
                            if 2 <= n < 4 and l + 1 < DEPTH:
                                ada(l + 1, n - 2)
                    else:
                        with dve.Fori(0, UNITS[g] // 2) as i:
                            for half in range(2):
                                expert_unit(g, i, half, base + 2 * i + half)
                    if g != "S":
                        add_experts(l, g)
            step(normalise(("ssf",), slice(0, TOK)), "xn_ready")


_INS = ["x_prompt", "x_sample", "c_prompt", "c_sample", "cache_k", "cache_v", "state_conv", "state_C", "state_n", "state_m",
        "rel_bias", "w_ada", "b_ada", "norm_mix", "norm_ffn", "w_in", "conv_w", "conv_b", "gate_b", "attn_sinks", "m_norm",
        "w_out", "peer_query", "peer_keys", "peer_u", "peer_v", "norm_final"]
_OUTS = [(1, SEQ, D), (DEC_B, DEC_S, D)] + [
    s for B in (1, DEC_B) for s in ((DEPTH, B, WINDOW, A_KV, DH), (DEPTH, B, WINDOW, A_KV, DH), (DEPTH, B, CONV_W - 1, 2 * MH * MD),
                                    (DEPTH, B, MH, MD, MD), (DEPTH, B, MH, MD), (DEPTH, B, MH))]


def kernel(**inputs):
    import numpy as _np
    import concourse.bacc as _bacc
    from concourse import mybir as _mybir
    from concourse.bass_utils import run_bass_kernel_spmd as _run

    nc = _bacc.Bacc("TRN2", target_bir_lowering=False, num_devices=1)
    arrays = {f"in_{name}": _np.ascontiguousarray(inputs[name]) for name in _INS}
    arrays["in_consts"], arrays["in_buckets"] = constants()
    args = [nc.dram_tensor(name, a.shape, _mybir.dt.from_np(a.dtype), kind="ExternalInput").ap() for name, a in arrays.items()]
    args += [nc.dram_tensor(f"out_{i}", shape, _mybir.dt.float32, kind="ExternalOutput").ap() for i, shape in enumerate(_OUTS)]
    hybrid_trunk(nc, *args)
    r = _run(nc, [arrays], core_ids=[0])
    return tuple(r.results[0][f"out_{i}"] for i in range(len(_OUTS)))
```
